# Optimizing a Trainium2 kernel written in Bass

```python
import math
import jax
import jax.numpy as jnp
from jax import lax
import numpy as np

D_MODEL = 1024
BATCH = 1
SEQ = 256
DEPTH = 1

MEM_LEN = 256
DA_HEADS = 4
DA_HEAD_DIM = 64
DA_V_DIM = 2 * DA_HEAD_DIM
DA_QK_WIDTH = DA_HEADS * 2 * DA_HEAD_DIM
DA_WIDTH = DA_HEADS * DA_V_DIM
RW_HEADS = 4
RW_HEAD_DIM = 64
RW_WIDTH = RW_HEADS * RW_HEAD_DIM
RW_DECAY_LORA = 64
RW_AAA_LORA = 64
RW_GATE_LORA = 128
RW_COLS = 3 * RW_WIDTH + RW_DECAY_LORA + RW_AAA_LORA + RW_GATE_LORA
MEM_HEADS = 4
MEM_HEAD_DIM = 64
MEM_WIDTH = MEM_HEADS * MEM_HEAD_DIM
D_MIX = DA_WIDTH + RW_WIDTH + MEM_WIDTH
D_IN = 2 * DA_QK_WIDTH + DA_WIDTH + RW_COLS + MEM_WIDTH
Q_BLOCK = 128
N_GROUPS = 4
EXPERTS_PER_GROUP = 4
N_EXPERTS = N_GROUPS * EXPERTS_PER_GROUP
TOP_K_IN_GROUP = 2
D_EXPERT = 512
RMS_EPS = 1e-6
RW_GN_EPS = 64e-5
MASK_VALUE = -1e30


def rms_norm(x, gain, eps=RMS_EPS):
    xf = x.astype(jnp.float32)
    y = xf * lax.rsqrt(jnp.mean(xf * xf, axis=-1, keepdims=True) + eps)
    return (y * gain.astype(jnp.float32)).astype(x.dtype)

def alibi_slopes(n_heads):
    return jnp.asarray([2.0 ** (-8.0 * (i + 1) / n_heads) for i in range(n_heads)], dtype=jnp.float32)

def diff_attention(q, k, v, positions, q_gain, k_gain, lam, lam_init, sub_gain):
    B, S, _ = q.shape
    H, d = DA_HEADS, DA_HEAD_DIM
    nb = S // Q_BLOCK
    q = rms_norm(q.reshape(B, S, H, 2, d), q_gain) * (d ** -0.5)
    k = rms_norm(k.reshape(B, S, H, 2, d), k_gain)
    qh = jnp.transpose(q, (0, 2, 3, 1, 4))
    kh = jnp.transpose(k, (0, 2, 3, 1, 4))
    vh = jnp.transpose(v.reshape(B, S, H, DA_V_DIM), (0, 2, 1, 3))
    q_blocks = jnp.moveaxis(qh.reshape(B, H, 2, nb, Q_BLOCK, d), 3, 0)
    pos_blocks = jnp.transpose(positions.reshape(B, nb, Q_BLOCK), (1, 0, 2))
    idx_blocks = jnp.arange(S, dtype=jnp.int32).reshape(nb, Q_BLOCK)
    k_idx = jnp.arange(S, dtype=jnp.int32)
    slopes = alibi_slopes(H)

    def block(args):
        qb, pb, ib = args
        s = jnp.einsum('bhmqd,bhmkd->bhmqk', qb, kh).astype(jnp.float32)
        dist = (pb[:, :, None] - positions[:, None, :]).astype(jnp.float32)
        bias = -slopes[None, :, None, None, None] * dist[:, None, None, :, :]
        causal = ib[:, None] >= k_idx[None, :]
        p = jax.nn.softmax(jnp.where(causal, s + bias, MASK_VALUE), axis=-1)
        attn = p[:, :, 0] - lam * p[:, :, 1]
        return jnp.einsum('bhqk,bhke->bhqe', attn.astype(vh.dtype), vh)

    out = lax.map(block, (q_blocks, pos_blocks, idx_blocks))
    out = jnp.transpose(out, (1, 0, 3, 2, 4)).reshape(B, S, H, DA_V_DIM)
    out = rms_norm(out, sub_gain) * (1.0 - lam_init)
    return out.reshape(B, S, DA_WIDTH)

def rwkv7_step(state, inp):
    r_t, w_t, k_t, v_t, kk_t, a_t = inp
    sa = jnp.einsum('bhvk,bhk->bhv', state, -kk_t)
    state = (state * w_t[:, :, None, :]
             + sa[..., None] * (kk_t * a_t)[:, :, None, :]
             + v_t[..., None] * k_t[:, :, None, :])
    y = jnp.einsum('bhvk,bhk->bhv', state, r_t)
    return state, y

def rwkv7_time_mix(cols, mu, w0, w2, a0, a2, g2, k_k, k_a, r_k, gn_w, gn_b):
    B, S, _ = cols.shape
    H, N = RW_HEADS, RW_HEAD_DIM
    prev = jnp.pad(cols, ((0, 0), (1, 0), (0, 0)))[:, :S]
    cols = cols + (prev - cols) * mu
    o1 = RW_WIDTH
    o2 = 2 * RW_WIDTH
    o3 = 3 * RW_WIDTH
    o4 = o3 + RW_DECAY_LORA
    o5 = o4 + RW_AAA_LORA
    r, k, v, xw, xa, xg = jnp.split(cols, [o1, o2, o3, o4, o5], axis=-1)
    w = -jax.nn.softplus(-(w0 + jnp.tanh(xw) @ w2)) - 0.5
    a = jax.nn.sigmoid(a0 + xa @ a2)
    g = jax.nn.sigmoid(xg) @ g2

    def heads(t):
        return t.reshape(B, S, H, N).astype(jnp.float32)

    r, k, v, w, a = heads(r), heads(k), heads(v), heads(w), heads(a)
    kk = k * k_k.reshape(H, N).astype(jnp.float32)
    kk = kk / jnp.maximum(jnp.sqrt(jnp.sum(kk * kk, axis=-1, keepdims=True)), 1e-12)
    k = k * (1.0 + (a - 1.0) * k_a.reshape(H, N).astype(jnp.float32))
    decay = jnp.exp(-jnp.exp(w))

    def time_major(t):
        return jnp.transpose(t, (1, 0, 2, 3))

    state0 = jnp.zeros((B, H, N, N), jnp.float32)
    _, y = lax.scan(rwkv7_step, state0,
                    (time_major(r), time_major(decay), time_major(k), time_major(v), time_major(kk), time_major(a)))
    y = jnp.transpose(y, (1, 0, 2, 3))
    mean = jnp.mean(y, axis=-1, keepdims=True)
    var = jnp.mean(jnp.square(y - mean), axis=-1, keepdims=True)
    y = (y - mean) * lax.rsqrt(var + RW_GN_EPS)
    y = y * gn_w.reshape(H, N).astype(jnp.float32) + gn_b.reshape(H, N).astype(jnp.float32)
    y = y + jnp.sum(r * k * r_k.astype(jnp.float32), axis=-1, keepdims=True) * v
    return (y.reshape(B, S, RW_WIDTH) * g.astype(jnp.float32)).astype(cols.dtype)

def memory_attention(q, mem_n, w_kv, q_gain, k_gain):
    B, S, _ = q.shape
    M = mem_n.shape[1]
    mk, mv = jnp.split(mem_n @ w_kv, 2, axis=-1)
    q = rms_norm(q.reshape(B, S, MEM_HEADS, MEM_HEAD_DIM), q_gain)
    mk = rms_norm(mk.reshape(B, M, MEM_HEADS, MEM_HEAD_DIM), k_gain)
    mv = mv.reshape(B, M, MEM_HEADS, MEM_HEAD_DIM)
    s = jnp.einsum('bshd,bmhd->bhsm', q, mk).astype(jnp.float32) * (MEM_HEAD_DIM ** -0.5)
    p = jax.nn.softmax(s, axis=-1)
    o = jnp.einsum('bhsm,bmhd->bshd', p.astype(mv.dtype), mv)
    return o.reshape(B, S, MEM_WIDTH)

def hierarchical_moe(xn, w_gr, b_gr, w_er, b_er, w_gate, w_up, w_down):
    B, S, D = xn.shape
    T = B * S
    xt = xn.reshape(T, D)
    rows = jnp.arange(T)
    g_logits = (xt @ w_gr + b_gr).astype(jnp.float32)
    p_g = jax.nn.softmax(g_logits, axis=-1)
    g_idx = jnp.argmax(g_logits, axis=-1)
    p_sel = p_g[rows, g_idx]
    e_logits = (xt @ w_er + b_er).astype(jnp.float32).reshape(T, N_GROUPS, EXPERTS_PER_GROUP)
    e_logits = e_logits[rows, g_idx]
    top_v, top_i = lax.top_k(e_logits, TOP_K_IN_GROUP)
    wts = jax.nn.softmax(top_v, axis=-1) * p_sel[:, None]
    e_global = g_idx[:, None] * EXPERTS_PER_GROUP + top_i
    gate = jnp.sum(jax.nn.one_hot(e_global, N_EXPERTS, dtype=jnp.float32) * wts[..., None], axis=1)
    y = jnp.zeros_like(xt)
    for e in range(N_EXPERTS):
        hdn = jax.nn.silu(xt @ w_gate[e]) * (xt @ w_up[e])
        y = y + gate[:, e:e + 1].astype(xt.dtype) * (hdn @ w_down[e])
    return y.reshape(B, S, D)

def first_inputs(seed: int = 0) -> dict:
    key = jax.random.key(seed)
    ks = iter(jax.random.split(key, 48))
    f32 = jnp.float32

    def nrm(shape, scale):
        return jax.random.normal(next(ks), shape, f32) * scale

    def gain(shape):
        return 1.0 + 0.02 * jax.random.normal(next(ks), shape, f32)

    L = DEPTH
    D = D_MODEL
    inputs = {}
    inputs['x'] = nrm((BATCH, SEQ, D), 1.0)
    inputs['mem'] = nrm((BATCH, MEM_LEN, D), 1.0)
    inputs['positions'] = (jnp.arange(SEQ, dtype=jnp.int32)[None, :]
                           + jax.random.randint(next(ks), (BATCH, 1), 0, 1024, dtype=jnp.int32))
    inputs['attn_norm'] = gain((L, D))
    inputs['w_in'] = nrm((L, D, D_IN), D ** -0.5)
    inputs['da_q_norm'] = gain((L, 2, DA_HEAD_DIM))
    inputs['da_k_norm'] = gain((L, 2, DA_HEAD_DIM))
    inputs['da_lambda_q1'] = nrm((L, DA_HEAD_DIM), 0.1)
    inputs['da_lambda_k1'] = nrm((L, DA_HEAD_DIM), 0.1)
    inputs['da_lambda_q2'] = nrm((L, DA_HEAD_DIM), 0.1)
    inputs['da_lambda_k2'] = nrm((L, DA_HEAD_DIM), 0.1)
    inputs['da_subln'] = gain((L, DA_V_DIM))
    inputs['rw_mu'] = jax.random.uniform(next(ks), (L, RW_COLS), f32)
    inputs['rw_w0'] = jax.random.uniform(next(ks), (L, RW_WIDTH), f32, minval=-6.0, maxval=-0.5)
    inputs['rw_w2'] = nrm((L, RW_DECAY_LORA, RW_WIDTH), 0.1 * RW_DECAY_LORA ** -0.5)
    inputs['rw_a0'] = nrm((L, RW_WIDTH), 0.1)
    inputs['rw_a2'] = nrm((L, RW_AAA_LORA, RW_WIDTH), 0.1 * RW_AAA_LORA ** -0.5)
    inputs['rw_g2'] = nrm((L, RW_GATE_LORA, RW_WIDTH), RW_GATE_LORA ** -0.5)
    inputs['rw_k_k'] = 0.85 + 0.02 * jax.random.normal(next(ks), (L, RW_WIDTH), f32)
    inputs['rw_k_a'] = gain((L, RW_WIDTH))
    inputs['rw_r_k'] = nrm((L, RW_HEADS, RW_HEAD_DIM), 0.1)
    inputs['rw_gn_w'] = gain((L, RW_WIDTH))
    inputs['rw_gn_b'] = nrm((L, RW_WIDTH), 0.01)
    inputs['mem_norm'] = gain((L, D))
    inputs['w_mem_kv'] = nrm((L, D, 2 * MEM_WIDTH), D ** -0.5)
    inputs['mem_q_norm'] = gain((L, MEM_HEAD_DIM))
    inputs['mem_k_norm'] = gain((L, MEM_HEAD_DIM))
    inputs['w_out'] = nrm((L, D_MIX, D), D_MIX ** -0.5)
    inputs['ffn_norm'] = gain((L, D))
    inputs['w_group_router'] = nrm((L, D, N_GROUPS), D ** -0.5)
    inputs['b_group_router'] = nrm((L, N_GROUPS), 0.01)
    inputs['w_expert_router'] = nrm((L, D, N_EXPERTS), D ** -0.5)
    inputs['b_expert_router'] = nrm((L, N_EXPERTS), 0.01)
    inputs['w_e_gate'] = nrm((L, N_EXPERTS, D, D_EXPERT), D ** -0.5)
    inputs['w_e_up'] = nrm((L, N_EXPERTS, D, D_EXPERT), D ** -0.5)
    inputs['w_e_down'] = nrm((L, N_EXPERTS, D_EXPERT, D), D_EXPERT ** -0.5)
    return inputs

def first_block(x, mem, positions, attn_norm, w_in, da_q_norm, da_k_norm, da_lambda_q1, da_lambda_k1,
              da_lambda_q2, da_lambda_k2, da_subln, rw_mu, rw_w0, rw_w2, rw_a0, rw_a2, rw_g2, rw_k_k,
              rw_k_a, rw_r_k, rw_gn_w, rw_gn_b, mem_norm, w_mem_kv, mem_q_norm, mem_k_norm, w_out,
              ffn_norm, w_group_router, b_group_router, w_expert_router, b_expert_router,
              w_e_gate, w_e_up, w_e_down):
    c1 = DA_QK_WIDTH
    c2 = 2 * DA_QK_WIDTH
    c3 = c2 + DA_WIDTH
    c4 = c3 + RW_COLS
    for l in range(DEPTH):
        h = rms_norm(x, attn_norm[l])
        proj = h @ w_in[l]
        q_da, k_da, v_da, rw_cols, q_mem = jnp.split(proj, [c1, c2, c3, c4], axis=-1)
        lam_init = 0.8 - 0.6 * math.exp(-0.3 * l)
        lam = (jnp.exp(jnp.sum(da_lambda_q1[l].astype(jnp.float32) * da_lambda_k1[l].astype(jnp.float32)))
               - jnp.exp(jnp.sum(da_lambda_q2[l].astype(jnp.float32) * da_lambda_k2[l].astype(jnp.float32)))
               + lam_init)
        o_da = diff_attention(q_da, k_da, v_da, positions, da_q_norm[l], da_k_norm[l], lam, lam_init, da_subln[l])
        o_rw = rwkv7_time_mix(rw_cols, rw_mu[l], rw_w0[l], rw_w2[l], rw_a0[l], rw_a2[l], rw_g2[l],
                              rw_k_k[l], rw_k_a[l], rw_r_k[l], rw_gn_w[l], rw_gn_b[l])
        mem_n = rms_norm(mem, mem_norm[l])
        o_mem = memory_attention(q_mem, mem_n, w_mem_kv[l], mem_q_norm[l], mem_k_norm[l])
        mixed = jnp.concatenate([o_da, o_rw.astype(o_da.dtype), o_mem], axis=-1)
        x = x + mixed @ w_out[l]
        xn = rms_norm(x, ffn_norm[l])
        x = x + hierarchical_moe(xn, w_group_router[l], b_group_router[l], w_expert_router[l],
                                 b_expert_router[l], w_e_gate[l], w_e_up[l], w_e_down[l])
    return x


MIX = D_MODEL // 2
GM_CHUNK = 128
GM_GROUPS = 4
GM_GW = MIX // GM_GROUPS
CONV_WIDTH = 4
LRU_BLOCKS = 8
LRU_BW = MIX // LRU_BLOCKS
LRU_C = 8.0
N_HEADS = 8
HEAD_DIM = MIX // N_HEADS
N_KV = 2
HPG = N_HEADS // N_KV
CMP_LEN = 32
CMP_STRIDE = 16
SLC_LEN = 64
SLC_TOPN = 8
WIN = 512
NSA_Q = N_HEADS * HEAD_DIM
NSA_KV = N_KV * HEAD_DIM
POOL_WINDOWS = (2, 4, 8, 16)
POOL_GROUPS = len(POOL_WINDOWS)
POOL_GW = MIX // POOL_GROUPS
N_BRANCH = 4
N_EXPERTS_2 = N_GROUPS * EXPERTS_PER_GROUP
EXPERT_TOPK = 2
D_EXPERT_2 = D_MODEL // 2

EPS = 1e-6
NEG_INF = -1e30
FORCE_SCORE = 1e6

IN_SPLITS = (MIX, MIX, MIX, MIX, NSA_Q, 6 * NSA_KV, 3 * N_HEADS, MIX, N_BRANCH * D_MODEL)
N_IN = sum(IN_SPLITS)


def rms_norm_2(x, g):
    xf = x.astype(jnp.float32)
    y = xf * lax.rsqrt(jnp.mean(xf * xf, axis=-1, keepdims=True) + EPS)
    return (y * g.astype(jnp.float32)).astype(x.dtype)

def gmlp_mixer(u, v, v_norm_g, ws, bs):
    B, S, _ = u.shape
    nc = S // GM_CHUNK
    u = jax.nn.gelu(u)
    v = rms_norm_2(jax.nn.gelu(v), v_norm_g).reshape(B, nc, GM_CHUNK, GM_GROUPS, GM_GW)
    causal = jnp.tril(jnp.ones((GM_CHUNK, GM_CHUNK), dtype=bool))
    w = jnp.where(causal[None], ws, 0.0)
    mixed = jnp.einsum('gts,bnsgc->bntgc', w, v) + bs.T[:, :, None]
    return u * mixed.reshape(B, S, MIX)

def rglru_mixer(gate_in, x_in, conv_w, conv_b, wa, ba, wx, bx, lam):
    B, S, C = x_in.shape
    f32 = jnp.float32
    xp = jnp.pad(x_in, ((0, 0), (CONV_WIDTH - 1, 0), (0, 0)))
    xc = conv_b + sum(xp[:, k:k + S] * conv_w[k] for k in range(CONV_WIDTH))
    xb = xc.reshape(B, S, LRU_BLOCKS, LRU_BW)
    r = jax.nn.sigmoid(jnp.einsum('bshi,hij->bshj', xb, wa).reshape(B, S, C) + ba)
    i = jax.nn.sigmoid(jnp.einsum('bshi,hij->bshj', xb, wx).reshape(B, S, C) + bx)
    log_a = -LRU_C * r.astype(f32) * jax.nn.softplus(-lam.astype(f32))
    a = jnp.exp(log_a)
    b = jnp.sqrt(-jnp.expm1(2.0 * log_a)) * (i * xc).astype(f32)

    def combine(c1, c2):
        a1, b1 = c1
        a2, b2 = c2
        return a1 * a2, a2 * b1 + b2

    _, h = lax.associative_scan(combine, (a, b), axis=1)
    return jax.nn.gelu(gate_in) * h.astype(x_in.dtype)

def _gather_blocks(blocks, idx):
    return blocks[idx].reshape(idx.shape[0], -1, blocks.shape[-1])

_gather_bg = jax.vmap(jax.vmap(_gather_blocks))

def nsa_mixer(q, kv, gate_logits, cmp_pe, cmp_w1, cmp_w2):
    B, S, _ = q.shape
    f32 = jnp.float32
    scale = HEAD_DIM ** -0.5
    t_pos = jnp.arange(S)
    qh = q.reshape(B, S, N_KV, HPG, HEAD_DIM).transpose(0, 2, 3, 1, 4)
    kv = kv.reshape(B, S, 6, N_KV, HEAD_DIM).transpose(2, 0, 3, 1, 4)

    n_sub = CMP_LEN // CMP_STRIDE
    n_chunk = S // CMP_STRIDE
    n_cmp = n_chunk - n_sub + 1
    chunks = kv[0:2].reshape(2, B, N_KV, n_chunk, CMP_STRIDE, HEAD_DIM)
    blocks = jnp.concatenate([chunks[:, :, :, j:j + n_cmp] for j in range(n_sub)], axis=4)
    blocks = blocks + cmp_pe[:, None, None, None]
    flat = blocks.reshape(2, B, N_KV, n_cmp, CMP_LEN * HEAD_DIM)
    hid = jax.nn.gelu(jnp.einsum('cbgnf,cgfe->cbgne', flat, cmp_w1))
    kvc = jnp.einsum('cbgne,cged->cbgnd', hid, cmp_w2)
    k_c, v_c = kvc[0], kvc[1]
    cmp_end = jnp.arange(n_cmp) * CMP_STRIDE + (CMP_LEN - 1)
    cmp_mask = cmp_end[None, :] <= t_pos[:, None]
    s_c = jnp.einsum('bgjsd,bgnd->bgjsn', qh, k_c).astype(f32) * scale
    p_c = jax.nn.softmax(jnp.where(cmp_mask, s_c, NEG_INF), axis=-1)
    p_c = jnp.where(jnp.any(cmp_mask, axis=-1)[:, None], p_c, 0.0)
    o_cmp = jnp.einsum('bgjsn,bgnd->bgjsd', p_c.astype(q.dtype), v_c)

    n_slc = S // SLC_LEN
    topn = min(SLC_TOPN, n_slc)
    c_start = np.arange(n_cmp) * CMP_STRIDE
    s_start = np.arange(n_slc) * SLC_LEN
    overlap = ((c_start[:, None] <= s_start[None, :] + SLC_LEN - 1)
               & (c_start[:, None] + CMP_LEN - 1 >= s_start[None, :])).astype(np.float32)
    imp = jnp.einsum('bgjsn,nm->bgsm', p_c, jnp.asarray(overlap))
    blk = jnp.arange(n_slc)
    cur = t_pos // SLC_LEN
    causal_blk = blk[None, :] * SLC_LEN <= t_pos[:, None]
    forced = (blk[None, :] == 0) | (blk[None, :] == cur[:, None]) | (blk[None, :] == cur[:, None] - 1)
    score = jnp.where(forced, FORCE_SCORE, jnp.where(causal_blk, imp, -1.0))
    top_val, top_idx = lax.top_k(score, topn)
    top_ok = top_val >= 0.0

    nq = S // Q_BLOCK
    ks_blk = kv[2].reshape(B, N_KV, n_slc, SLC_LEN, HEAD_DIM)
    vs_blk = kv[3].reshape(B, N_KV, n_slc, SLC_LEN, HEAD_DIM)

    def slc_block(args):
        q_b, idx_b, ok_b, t_b = args
        k_sel = _gather_bg(ks_blk, idx_b)
        v_sel = _gather_bg(vs_blk, idx_b)
        k_pos = idx_b[..., None] * SLC_LEN + jnp.arange(SLC_LEN)
        ok = (ok_b[..., None] & (k_pos <= t_b[:, None, None])).reshape(B, N_KV, Q_BLOCK, -1)
        s = jnp.einsum('bgjqd,bgqkd->bgjqk', q_b, k_sel).astype(f32) * scale
        p = jax.nn.softmax(jnp.where(ok[:, :, None], s, NEG_INF), axis=-1)
        return jnp.einsum('bgjqk,bgqkd->bgjqd', p.astype(q_b.dtype), v_sel)

    q_blocks = qh.reshape(B, N_KV, HPG, nq, Q_BLOCK, HEAD_DIM).transpose(3, 0, 1, 2, 4, 5)
    idx_blocks = top_idx.reshape(B, N_KV, nq, Q_BLOCK, topn).transpose(2, 0, 1, 3, 4)
    ok_blocks = top_ok.reshape(B, N_KV, nq, Q_BLOCK, topn).transpose(2, 0, 1, 3, 4)
    o_slc = lax.map(slc_block, (q_blocks, idx_blocks, ok_blocks, t_pos.reshape(nq, Q_BLOCK)))
    o_slc = o_slc.transpose(1, 2, 3, 0, 4, 5).reshape(B, N_KV, HPG, S, HEAD_DIM)

    n_pad = WIN // Q_BLOCK
    band_len = Q_BLOCK * (n_pad + 1)
    kw = jnp.pad(kv[4], ((0, 0), (0, 0), (WIN, 0), (0, 0))).reshape(B, N_KV, nq + n_pad, Q_BLOCK, HEAD_DIM)
    vw = jnp.pad(kv[5], ((0, 0), (0, 0), (WIN, 0), (0, 0))).reshape(B, N_KV, nq + n_pad, Q_BLOCK, HEAD_DIM)
    band_k = jnp.concatenate([kw[:, :, j:j + nq] for j in range(n_pad + 1)], axis=3)
    band_v = jnp.concatenate([vw[:, :, j:j + nq] for j in range(n_pad + 1)], axis=3)
    qb = qh.reshape(B, N_KV, HPG, nq, Q_BLOCK, HEAD_DIM)
    s_w = jnp.einsum('bgjiqd,bgikd->bgjiqk', qb, band_k).astype(f32) * scale
    q_idx = jnp.arange(Q_BLOCK)
    k_idx = jnp.arange(band_len)
    delta = WIN + q_idx[:, None] - k_idx[None, :]
    k_abs = (jnp.arange(nq)[:, None] - n_pad) * Q_BLOCK + k_idx[None, :]
    win_mask = ((delta >= 0) & (delta < WIN))[None] & (k_abs >= 0)[:, None, :]
    p_w = jax.nn.softmax(jnp.where(win_mask, s_w, NEG_INF), axis=-1)
    o_win = jnp.einsum('bgjiqk,bgikd->bgjiqd', p_w.astype(q.dtype), band_v).reshape(B, N_KV, HPG, S, HEAD_DIM)

    g = jax.nn.sigmoid(gate_logits.reshape(B, S, N_KV, HPG, 3).transpose(4, 0, 2, 3, 1))[..., None]
    o = g[0] * o_cmp + g[1] * o_slc + g[2] * o_win
    return o.transpose(0, 3, 1, 2, 4).reshape(B, S, NSA_Q)

def pool_mixer(xd, pool_w, pool_scale):
    B, S, C = xd.shape
    f32 = jnp.float32
    xf = xd.astype(f32)
    csum = jnp.pad(lax.cumsum(xf, axis=1), ((0, 0), (1, 0), (0, 0)))
    t = jnp.arange(S)
    outs = []
    for gi, w in enumerate(POOL_WINDOWS):
        c = csum[:, :, gi * POOL_GW:(gi + 1) * POOL_GW]
        lower = jnp.pad(c[:, :S + 1 - w], ((0, 0), (w - 1, 0), (0, 0)))
        cnt = jnp.minimum(t + 1, w).astype(f32)[None, :, None]
        outs.append((c[:, 1:] - lower) / cnt - xf[:, :, gi * POOL_GW:(gi + 1) * POOL_GW])
    pooled = jnp.stack(outs, axis=2).astype(xd.dtype)
    mixed = jnp.einsum('bsgi,gij->bsgj', pooled, pool_w).reshape(B, S, C)
    return mixed * pool_scale

def hybrid_mixer(h, w_in, gm_norm_g, gm_ws, gm_b, conv_w, conv_b, lru_wa, lru_ba, lru_wx,
                 lru_bx, lru_lambda, cmp_pe, cmp_w1, cmp_w2, pool_w, pool_scale, w_branch, w_out):
    B, S, _ = h.shape
    proj = h @ w_in
    cuts = np.cumsum(IN_SPLITS)[:-1].tolist()
    u, v, gate_b, rec_b, q, kv, nsa_g, xd, mg = jnp.split(proj, cuts, axis=-1)
    y_a = gmlp_mixer(u, v, gm_norm_g, gm_ws, gm_b)
    y_b = rglru_mixer(gate_b, rec_b, conv_w, conv_b, lru_wa, lru_ba, lru_wx, lru_bx, lru_lambda)
    y_c = nsa_mixer(q, kv, nsa_g, cmp_pe, cmp_w1, cmp_w2)
    y_d = pool_mixer(xd, pool_w, pool_scale)
    ys = jnp.stack([y_a, y_b, y_c, y_d])
    branch = jnp.einsum('nbsc,ncd->bsnd', ys, w_branch)
    gates = jax.nn.sigmoid(mg.reshape(B, S, N_BRANCH, D_MODEL))
    merged = jnp.sum(gates * branch, axis=2)
    return merged @ w_out

def hier_moe(h, wr_g, br_g, wr_e, br_e, w_gate, w_up, w_down):
    B, S, D = h.shape
    f32 = jnp.float32
    t = h.reshape(-1, D)
    T = t.shape[0]
    grp_p = jax.nn.softmax((t @ wr_g + br_g).astype(f32), axis=-1)
    grp_w, grp_idx = lax.top_k(grp_p, 1)
    exp_logits = (t @ wr_e + br_e).astype(f32).reshape(T, N_GROUPS, EXPERTS_PER_GROUP)
    in_grp = jnp.einsum('tge,tg->te', exp_logits, jax.nn.one_hot(grp_idx[:, 0], N_GROUPS, dtype=f32))
    top_l, top_e = lax.top_k(in_grp, EXPERT_TOPK)
    top_w = jax.nn.softmax(top_l, axis=-1) * grp_w
    expert_id = grp_idx * EXPERTS_PER_GROUP + top_e
    combine = jnp.sum(jax.nn.one_hot(expert_id, N_EXPERTS_2, dtype=f32) * top_w[..., None], axis=1)
    hid = jax.nn.silu(jnp.einsum('td,edf->etf', t, w_gate)) * jnp.einsum('td,edf->etf', t, w_up)
    hid = hid * combine.T[:, :, None].astype(hid.dtype)
    out = jnp.einsum('etf,efd->td', hid, w_down)
    return out.reshape(B, S, D)

def second_inputs(seed: int = 0) -> dict:
    key = jax.random.key(seed)
    ks = iter(jax.random.split(key, 40))
    f32 = jnp.float32
    L = DEPTH

    def nrm(shape, scale):
        return jax.random.normal(next(ks), shape, f32) * scale

    def gain(shape):
        return 1.0 + 0.02 * jax.random.normal(next(ks), shape, f32)

    a_c = jax.random.uniform(next(ks), (L, MIX), f32, minval=0.9, maxval=0.999)
    a0 = a_c ** (1.0 / LRU_C)
    lru_lambda = jnp.log(a0) - jnp.log1p(-a0)
    return {
        'x': nrm((BATCH, SEQ, D_MODEL), 1.0),
        'norm1_g': gain((L, D_MODEL)),
        'w_in': nrm((L, D_MODEL, N_IN), D_MODEL ** -0.5),
        'gm_norm_g': gain((L, MIX)),
        'gm_ws': nrm((L, GM_GROUPS, GM_CHUNK, GM_CHUNK), GM_CHUNK ** -0.5),
        'gm_b': gain((L, GM_GROUPS, GM_CHUNK)),
        'conv_w': nrm((L, CONV_WIDTH, MIX), CONV_WIDTH ** -0.5),
        'conv_b': nrm((L, MIX), 0.02),
        'lru_wa': nrm((L, LRU_BLOCKS, LRU_BW, LRU_BW), LRU_BW ** -0.5),
        'lru_ba': nrm((L, MIX), 0.02),
        'lru_wx': nrm((L, LRU_BLOCKS, LRU_BW, LRU_BW), LRU_BW ** -0.5),
        'lru_bx': nrm((L, MIX), 0.02),
        'lru_lambda': lru_lambda,
        'cmp_pe': nrm((L, 2, CMP_LEN, HEAD_DIM), 0.02),
        'cmp_w1': nrm((L, 2, N_KV, CMP_LEN * HEAD_DIM, HEAD_DIM), (CMP_LEN * HEAD_DIM) ** -0.5),
        'cmp_w2': nrm((L, 2, N_KV, HEAD_DIM, HEAD_DIM), HEAD_DIM ** -0.5),
        'pool_w': nrm((L, POOL_GROUPS, POOL_GW, POOL_GW), POOL_GW ** -0.5),
        'pool_scale': gain((L, MIX)),
        'w_branch': nrm((L, N_BRANCH, MIX, D_MODEL), MIX ** -0.5),
        'w_out': nrm((L, D_MODEL, D_MODEL), D_MODEL ** -0.5),
        'norm2_g': gain((L, D_MODEL)),
        'router_w_group': nrm((L, D_MODEL, N_GROUPS), D_MODEL ** -0.5),
        'router_b_group': nrm((L, N_GROUPS), 0.01),
        'router_w_expert': nrm((L, D_MODEL, N_EXPERTS_2), D_MODEL ** -0.5),
        'router_b_expert': nrm((L, N_EXPERTS_2), 0.01),
        'moe_w_gate': nrm((L, N_EXPERTS_2, D_MODEL, D_EXPERT_2), D_MODEL ** -0.5),
        'moe_w_up': nrm((L, N_EXPERTS_2, D_MODEL, D_EXPERT_2), D_MODEL ** -0.5),
        'moe_w_down': nrm((L, N_EXPERTS_2, D_EXPERT_2, D_MODEL), D_EXPERT_2 ** -0.5),
        'final_norm_g': gain((D_MODEL,)),
    }

def second_block(x, norm1_g, w_in, gm_norm_g, gm_ws, gm_b, conv_w, conv_b, lru_wa, lru_ba, lru_wx,
              lru_bx, lru_lambda, cmp_pe, cmp_w1, cmp_w2, pool_w, pool_scale, w_branch, w_out,
              norm2_g, router_w_group, router_b_group, router_w_expert, router_b_expert,
              moe_w_gate, moe_w_up, moe_w_down, final_norm_g):
    h = x
    for l in range(DEPTH):
        h = h + hybrid_mixer(rms_norm_2(h, norm1_g[l]), w_in[l], gm_norm_g[l], gm_ws[l], gm_b[l],
                             conv_w[l], conv_b[l], lru_wa[l], lru_ba[l], lru_wx[l], lru_bx[l],
                             lru_lambda[l], cmp_pe[l], cmp_w1[l], cmp_w2[l], pool_w[l],
                             pool_scale[l], w_branch[l], w_out[l])
        h = h + hier_moe(rms_norm_2(h, norm2_g[l]), router_w_group[l], router_b_group[l],
                         router_w_expert[l], router_b_expert[l], moe_w_gate[l], moe_w_up[l],
                         moe_w_down[l])
    return rms_norm_2(h, final_norm_g)


def setup_inputs(seed=0):
    out = dict(first_inputs(seed))
    for name, value in second_inputs(seed + 1).items():
        if name != "x":
            out[name + "_2"] = value
    return out


def reference(
    x, mem, positions, attn_norm, w_in, da_q_norm, da_k_norm, da_lambda_q1, da_lambda_k1,
    da_lambda_q2, da_lambda_k2, da_subln, rw_mu, rw_w0, rw_w2, rw_a0, rw_a2, rw_g2, rw_k_k,
    rw_k_a, rw_r_k, rw_gn_w, rw_gn_b, mem_norm, w_mem_kv, mem_q_norm, mem_k_norm, w_out,
    ffn_norm, w_group_router, b_group_router, w_expert_router, b_expert_router, w_e_gate,
    w_e_up, w_e_down, norm1_g_2, w_in_2, gm_norm_g_2, gm_ws_2, gm_b_2, conv_w_2, conv_b_2,
    lru_wa_2, lru_ba_2, lru_wx_2, lru_bx_2, lru_lambda_2, cmp_pe_2, cmp_w1_2, cmp_w2_2,
    pool_w_2, pool_scale_2, w_branch_2, w_out_2, norm2_g_2, router_w_group_2, router_b_group_2,
    router_w_expert_2, router_b_expert_2, moe_w_gate_2, moe_w_up_2, moe_w_down_2,
    final_norm_g_2,
):
    x = first_block(
        x, mem, positions, attn_norm, w_in, da_q_norm, da_k_norm, da_lambda_q1, da_lambda_k1,
        da_lambda_q2, da_lambda_k2, da_subln, rw_mu, rw_w0, rw_w2, rw_a0, rw_a2, rw_g2, rw_k_k,
        rw_k_a, rw_r_k, rw_gn_w, rw_gn_b, mem_norm, w_mem_kv, mem_q_norm, mem_k_norm, w_out,
        ffn_norm, w_group_router, b_group_router, w_expert_router, b_expert_router, w_e_gate,
        w_e_up, w_e_down,
    )
    return second_block(
        x, norm1_g_2, w_in_2, gm_norm_g_2, gm_ws_2, gm_b_2, conv_w_2, conv_b_2, lru_wa_2,
        lru_ba_2, lru_wx_2, lru_bx_2, lru_lambda_2, cmp_pe_2, cmp_w1_2, cmp_w2_2, pool_w_2,
        pool_scale_2, w_branch_2, w_out_2, norm2_g_2, router_w_group_2, router_b_group_2,
        router_w_expert_2, router_b_expert_2, moe_w_gate_2, moe_w_up_2, moe_w_down_2,
        final_norm_g_2,
    )


_drawn_inputs = setup_inputs


def setup_inputs(seed=0):
    import zlib

    import numpy as np

    out = dict(_drawn_inputs(seed))
    spreads = {}
    factors = {'da_lambda_q2': 2.914,
     'da_lambda_k2': 7.18,
     'rw_w2': 8.0,
     'rw_k_k': 24.27,
     'rw_k_a': 4.349,
     'rw_gn_w': 4.135,
     'rw_gn_b': 7.123,
     'mem_norm': 7.55,
     'mem_q_norm': 6.344,
     'mem_k_norm': 8.0,
     'b_group_router': 22.56,
     'b_expert_router': 5.154,
     'norm1_g_2': 3.232,
     'gm_norm_g_2': 8.0,
     'gm_b_2': 8.0,
     'lru_ba_2': 64.0,
     'lru_bx_2': 22.217,
     'cmp_pe_2': 64.0,
     'pool_scale_2': 5.785,
     'norm2_g_2': 4.63,
     'router_b_group_2': 8.0,
     'router_b_expert_2': 19.993,
     'final_norm_g_2': 8.471,
     'da_q_norm': 8.0,
     'da_k_norm': 2.892,
     'da_lambda_q1': 8.0,
     'da_lambda_k1': 8.0,
     'ffn_norm': 4.58,
     'conv_b_2': 7.07}
    for name, (base, spread) in spreads.items():
        noise = np.random.default_rng([zlib.crc32(name.encode()), seed]).standard_normal(out[name].shape)
        drawn = base * np.exp(spread * noise) if base else spread * noise
        out[name] = jnp.asarray(drawn.astype(out[name].dtype))
    for name, factor in factors.items():
        out[name] = (out[name] * factor).astype(out[name].dtype)
    return out
```

```python
from contextlib import ExitStack

import numpy as np

import concourse.bass as bass
from concourse import mybir

F32 = mybir.dt.float32
I32 = mybir.dt.int32
ALU = mybir.AluOpType
ACT = mybir.ActivationFunctionType
AXX = mybir.AxisListType.X

P = 128
S = 256
NT = S // P
D = 1024
KD = D // P
EPS = 1e-6
NEG = -1e30
SLOT = 4096
NSLOT = 6
CAP = 128
MORE_ABOVE = CAP

CONSTS = [("ident", 128), ("ones", 128), ("before", 128), ("upto", 128), ("iota", 128),
          ("levels", 7 * 128), ("pair", 128), ("causal01", 128), ("causal_add", 128),
          ("cmp_add", 30), ("cmp_any", 2), ("group_rank", 4), ("pool_inv", 64)]
PARAMS1 = [("attn_norm", 8), ("da_q", 1), ("da_k", 1), ("lam", 256), ("subln", 1), ("mu", 8), ("w0", 2),
           ("a0", 2), ("w2a2", 256), ("g2", 256), ("k_k", 2), ("k_a", 2), ("r_k", 2), ("gn_w", 2),
           ("gn_b", 2), ("mem_norm", 8), ("mem_q", 1), ("mem_k", 1), ("ffn_norm", 8), ("router", 160),
           ("router_b", 20), ("norm2", 8), ("router_2", 160), ("router_b_2", 20)]
PARAMS2 = [("norm1", 8), ("gm_norm", 4), ("gm_wsT", 512), ("gm_b", 512), ("conv_w", 16), ("conv_b", 4),
           ("lru_wa", 512), ("lru_wx", 512), ("lru_ba", 4), ("lru_bx", 4), ("lru_lam", 4), ("cmp_pe", 64),
           ("cmp_w2", 256), ("pool_w", 512), ("pool_scale", 4)]


def places(entries):
    at, out = 0, {}
    for name, n in entries:
        out[name] = (at, n)
        at += n
    return out, at


class Line:

    def __init__(self, name, sem):
        self.name, self.sem, self.count = name, sem, 0
        self.outside = None
        self.steps, self.waited = [], {}

    def wait(self, *tokens):
        for t in tokens:
            if t is None:
                continue
            if isinstance(t, list):
                self.wait(*t)
                continue
            sem, value = t
            assert value > 0
            if self.waited.get(id(sem), 0) < value:
                self.waited[id(sem)] = value
                self.steps.append(lambda e, sem=sem, value=value: e.wait_ge(sem, value))

    def do(self, emit, *after, signal=True):
        self.wait(*after)
        if not signal:
            self.steps.append(emit)
            return None
        self.count += 1
        sem = self.sem
        self.steps.append(lambda e: emit(e).then_inc(sem, 1))
        return (sem, self.count)

    @property
    def last(self):
        return (self.sem, self.count) if self.count else None

    def read(self, cell):
        got = []
        self.steps.append(lambda e: got.append(e.value_load(cell)))
        return got

    def enter(self, sem):
        self.outside = (self.sem, self.count, dict(self.waited), self.steps)
        self.sem, self.count, self.steps = sem, 0, []

    def leave(self, got, limit):
        inside = self.steps
        self.sem, self.count, self.waited, self.steps = self.outside

        def branch(e):
            with e.If(got[0] > limit):
                for step in inside:
                    step(e)

        self.steps.append(branch)

    def tt(self, out, a, b, op, *after):
        return self.do(lambda e: e.tensor_tensor(out, a, b, op), *after)

    def ts(self, out, a, s1, s2, op0, op1, *after):
        if s2 is None:
            return self.do(lambda e: e.tensor_scalar(out, a, s1, None, op0), *after)
        return self.do(lambda e: e.tensor_scalar(out, a, s1, s2, op0, op1), *after)

    def stt(self, out, a, s, b, op0, op1, *after):
        return self.do(lambda e: e.scalar_tensor_tensor(out=out, in0=a, scalar=s, in1=b, op0=op0, op1=op1), *after)

    def copy(self, out, a, *after):
        return self.do(lambda e: e.tensor_copy(out, a), *after)

    def reduce(self, out, a, op, *after):
        return self.do(lambda e: e.tensor_reduce(out, a, AXX, op), *after)

    def recip(self, out, a, *after):
        return self.do(lambda e: e.reciprocal(out, a), *after)

    def scan(self, out, a, b, *after):
        return self.do(lambda e: e.tensor_tensor_scan(out, a, b, 0.0, ALU.mult, ALU.add), *after)

    def max_of_sum(self, out, a, b, scale, top, *after):
        return self.do(lambda e: e.tensor_tensor_reduce(out=out, in0=a, in1=b, scale=scale, scalar=-3e38,
                                                        op0=ALU.add, op1=ALU.max, accum_out=top), *after)

    def memset(self, out, value, *after):
        return self.do(lambda e: e.memset(out, value), *after)

    def act(self, out, a, func, *after, bias=0.0, scale=1.0, accum=None):
        if accum is not None:
            return self.do(lambda e: e.activation(out, a, func, bias=bias, scale=scale, accum_out=accum), *after)
        return self.do(lambda e: e.activation(out, a, func, bias=bias, scale=scale), *after)

    def mm(self, out, lhsT, rhs, start, stop, *after, signal=False):
        return self.do(lambda e: e.matmul(out, lhsT, rhs, start=start, stop=stop), *after, signal=signal)

    def turn(self, out, a, ident, *after, signal=False):
        n = a.shape[0]
        return self.do(lambda e: e.transpose(out, a, ident[0:n, 0:n]), *after, signal=signal)


class Bank:

    def __init__(self, ap):
        self.ap, self.free, self.taken = ap, [], False


class Banks:

    def __init__(self, aps):
        self.banks, self.at = [Bank(a) for a in aps], 0

    def take(self):
        free = [k for k in range(self.at, self.at + len(self.banks)) if not self.banks[k % len(self.banks)].taken]
        b = self.banks[free[0] % len(self.banks)]
        self.at = free[0] + 1
        b.taken = True
        return b

    @staticmethod
    def give(bank, *tokens):
        bank.free, bank.taken = list(tokens), False


class Load:

    def __init__(self, src, slot, sem, value):
        self.src, self.slot, self.sem, self.ready, self.used = src, slot, sem, (sem, value), None


class Arena:

    def __init__(self, ap, size):
        self.ap, self.size, self.at, self.top = ap, size, 0, 0

    def get(self, *dims):
        n = int(np.prod(dims))
        a = self.ap[:, self.at:self.at + n]
        self.at += n
        self.top = max(self.top, self.at)
        assert self.at <= self.size, (self.at, self.size)
        if len(dims) == 2:
            a = a.rearrange("p (a b) -> p a b", a=dims[0])
        elif len(dims) == 3:
            a = a.rearrange("p (a b c) -> p a b c", a=dims[0], b=dims[1])
        return a


def build(nc, ins, out, debug=None):
    ctx = ExitStack()
    with ctx:
        def sb(name, shape, dt=F32):
            return ctx.enter_context(nc.sbuf_tensor(name, shape, dt))

        def sem(name):
            return ctx.enter_context(nc.semaphore(name))

        pe, ve, ac, gp = (Line(n, sem("done_" + n)) for n in ("pe", "ve", "ac", "gp"))
        lines = (pe, ve, ac, gp)

        def barrier():
            marks = [l.last for l in lines]
            for l in lines:
                l.wait(*marks)

        banks_all = [ctx.enter_context(nc.psum_tensor(f"bank{i}", [P, 512], F32)) for i in range(8)]
        ring = sb("weight_ring", [P, NSLOT * SLOT])
        slot_sems = [sem(f"slot{i}") for i in range(NSLOT)]
        cpos, clen = places(CONSTS)
        ppos, plen = places(PARAMS1)
        qpos, qlen = places(PARAMS2)
        consts, params = sb("consts", [P, clen]), sb("params", [P, plen])
        resid = sb("resid", [P, NT, D])
        arena_size = 23000
        arena_all = sb("arena", [P, arena_size])
        arena = Arena(arena_all, arena_size)
        tail = arena_all[:, arena_size - max(qlen, D):arena_size]

        def C(name, a=0, b=None):
            at, n = cpos[name]
            return consts[:, at + a:at + (n if b is None else b)]

        def PM(name, a=0, b=None):
            at, n = ppos[name]
            return params[:, at + a:at + (n if b is None else b)]

        def PP(name, a=0, b=None):
            at, n = qpos[name]
            return tail[:, at + a:at + (n if b is None else b)]

        ident = C("ident")

        sp = Line("sp", None)
        loads = []
        sems_now = [slot_sems]

        def load(src):
            i, turn = len(loads) % NSLOT, len(loads) // NSLOT + 1
            h = Load(src, ring[:, i * SLOT:i * SLOT + src.shape[1]], sems_now[0][i], 16 * turn)
            h.before = loads[-NSLOT] if len(loads) >= NSLOT else None
            loads.append(h)

            def issue(e):
                if h.before is not None:
                    for sm, value in h.before.used:
                        e.wait_ge(sm, value)
                e.dma_start(h.slot, h.src).then_inc(h.sem, 16)

            sp.steps.append(issue)
            return h

        small_loads = []

        def fetch(dst, src, *after):
            s = sem(f"load{len(small_loads)}")
            small_loads.append((dst, src, s, bool(after)))
            if after:
                ac.wait(*after)
                ac.steps.append(lambda e: e.dma_start(dst, src).then_inc(s, 16))
            return (s, 16)

        dumps = []

        def dump(name, ap):
            if debug is not None and name in debug:
                barrier()
                t = [l.last for l in lines]
                n = int(np.prod(ap.shape[1:]))
                d = nc.dram_tensor("dbg_" + name, [ap.shape[0], n], F32, kind="ExternalOutput").ap()
                s = sem("dbg_" + name)
                dumps.append((name, n))
                v = ap
                if len(ap.shape) == 3:
                    d = d.rearrange("p (a b) -> p a b", a=ap.shape[1])
                elif len(ap.shape) == 4:
                    d = d.rearrange("p (a b c) -> p a b c", a=ap.shape[1], b=ap.shape[2])
                gp.wait(*t)
                gp.steps.append(lambda e: e.dma_start(d, v).then_inc(s, 16))
                for l in lines:
                    l.wait((s, 16))

        t_consts = fetch(consts[:, :], ins["consts"])
        t_resid = fetch(resid[:, :, :], ins["x"].rearrange("(t p) d -> p t d", p=P))
        t_params = fetch(params[:, :], ins["params1"])

        neg_half = sb("neg_half", [P, 32])
        gp.memset(neg_half[:, :], -0.5)
        t_neg = gp.last

        def rstd(dst, sums, count, eps, *after):
            a = ve.ts(sums, sums, 1.0 / count, eps, ALU.mult, ALU.add, *after)
            n = int(np.prod(sums.shape[1:]))
            half = neg_half[:, 0:n]
            if len(sums.shape) == 3:
                half = half.rearrange("p (a b) -> p a b", a=sums.shape[1])
            return gp.tt(dst, sums, half, ALU.pow, a, t_neg)

        pool8 = Banks([b[:, :] for b in banks_all])

        def norm_rows(src, dst, *after):
            ss = arena.get(NT)
            rs = arena.get(NT)
            t = None
            for i in range(NT):
                t = ac.act(dst[:, i, :], src[:, i, :], ACT.Square, *after, accum=ss[:, i:i + 1])
            r = rstd(rs, ss, D, EPS, t)
            for i in range(NT):
                t = ve.ts(dst[:, i, :], src[:, i, :], rs[:, i:i + 1], None, ALU.mult, None, r)
            return t

        def to_channels(src, dst, tiles, gain, *after, scale=None):
            t = None
            for k in range(0, tiles, 2):
                b = pool8.take()
                w = min(2, tiles - k)
                for j in range(w):
                    for i in range(NT):
                        m = pe.turn(b.ap[:, (j * NT + i) * P:(j * NT + i + 1) * P],
                                    src[:, i, (k + j) * P:(k + j + 1) * P], ident, *after, b.free,
                                    signal=(j == w - 1 and i == NT - 1))
                for j in range(w):
                    o, a = dst[:, k + j, :], b.ap[:, j * S:(j + 1) * S]
                    if gain is None:
                        t = ve.ts(o, a, scale, None, ALU.mult, None, m)
                    else:
                        g = gain[:, k + j:k + j + 1] if gain.shape[1] > 1 else gain
                        t = ve.ts(o, a, g, 1.0 if scale is None else scale, ALU.mult, ALU.mult, m)
                pool8.give(b, t)
            return t

        def project_tokens(hT, h, width, finish, *after, at=0, stride=512):
            w = h.slot.rearrange("p (k n) -> p k n", n=stride)
            for i in range(NT):
                b = pool8.take()
                for k in range(w.shape[1]):
                    m = pe.mm(b.ap[:, 0:width], hT[:, k, i * P:(i + 1) * P], w[:, k, at:at + width],
                              k == 0, k == w.shape[1] - 1, *after, h.ready, b.free,
                              signal=(k == w.shape[1] - 1))
                pool8.give(b, *finish(i, b.ap[:, 0:width], m))
            return m

        def project_channels(hT, h, tiles, finish, *after, stride=512):
            w = h.slot.rearrange("p (k n) -> p k n", n=stride)
            for c in range(0, tiles, 2):
                b = pool8.take()
                for j in range(2):
                    for k in range(w.shape[1]):
                        m = pe.mm(b.ap[:, j * S:(j + 1) * S], w[:, k, (c + j) * P:(c + j + 1) * P],
                                  hT[:, k, :], k == 0, k == w.shape[1] - 1, *after, h.ready, b.free,
                                  signal=(j == 1 and k == w.shape[1] - 1))
                ps = b.ap.rearrange("p (j s) -> p j s", j=2)
                pool8.give(b, *finish(c, 2, ps, m))
            return m

        def head_norm(src, width, *after):
            n = width // 64
            sq = sq_flat[:, 0:NT * width].rearrange("p (a b) -> p a b", a=NT)
            ss, rs = arena.get(NT, n), arena.get(NT, n)
            a = ac.act(sq, src, ACT.Square, *after)
            b = ve.reduce(ss.rearrange("p a b -> p (a b)"), sq.rearrange("p a (h e) -> p (a h) e", e=64), ALU.add, a)
            r = rstd(rs, ss, 64, EPS, b)
            v = src.rearrange("p a (h e) -> p (a h) e", e=64)
            rb = rs.rearrange("p a b -> p (a b)").unsqueeze(2).to_broadcast([P, NT * n, 64])
            return ve.tt(v, v, rb, ALU.mult, r)

        mixT = arena.get(KD, S)
        rw_flat = arena.get(8 * (S + 1))
        rw = rw_flat.rearrange("p (a b) -> p a b", a=8)
        phase = arena.at
        qT, kT = arena.get(4, S), arena.get(4, S)
        v_da = arena.get(NT, 512)

        mem = arena.get(NT, D)
        t_mem = fetch(mem, ins["mem"].rearrange("(t p) d -> p t d", p=P))
        memn, memT = arena.get(NT, D), arena.get(KD, S)
        mk, mv = arena.get(NT, 256), arena.get(NT, 256)
        mkT, qmT = arena.get(2, S), arena.get(2, S)
        q_mem = arena.get(NT, 256)
        sq_flat = arena.get(NT * 512)
        sq = sq_flat.rearrange("p (a b) -> p a b", a=NT)
        t = norm_rows(mem, memn, t_mem)
        t_memT = to_channels(memn, memT, KD, PM("mem_norm"), t, t_params, t_consts)
        h = load(ins["w_mem_kv"])

        def fin_kv(i, ps, m):
            a = ve.copy(mk[:, i, :], ps[:, 0:256], m)
            b = ac.act(mv[:, i, :], ps[:, 256:512], ACT.Copy, m, a)
            return a, b

        h.used = [project_tokens(memT, h, 512, fin_kv, t_memT)]
        t_mv = ac.last
        t = head_norm(mk, 256, ve.last)
        t_mkT = to_channels(mk, mkT, 2, PM("mem_k"), t)
        hn, hT = memn, memT
        t = norm_rows(resid, hn, t_resid, h.used[0])
        t_hT = to_channels(hn, hT, KD, PM("attn_norm"), t)
        dump("hT", hT)
        q_da, k_da = arena.get(NT, 512), mem[:, 0, :].rearrange("p (a b) -> p a b", a=NT)

        def into(dst):
            def fin(i, ps, m):
                return (ve.copy(dst[:, i, :], ps, m),)
            return fin

        h = load(ins["w_in_a"][0])
        h.used = [project_tokens(hT, h, 512, into(q_da), t_hT)]
        t_q = head_norm(q_da, 512, ve.last)
        h = load(ins["w_in_a"][1])
        h.used = [project_tokens(hT, h, 512, into(k_da))]
        t_k = head_norm(k_da, 512, ve.last)
        t_qT = to_channels(q_da, qT, 4, PM("da_q"), t_q, scale=64 ** -0.5)
        t_kT = to_channels(k_da, kT, 4, PM("da_k"), t_k)
        t_z = ve.memset(rw[:, :, 0:1], 0.0)
        for j in range(2):
            h = load(ins["w_in_a"][3 + j])

            def fin_rw(c, n, ps, m, j=j):
                return (ac.act(rw[:, 4 * j + c:4 * j + c + n, 1:S + 1], ps, ACT.Copy, m),)

            h.used = [project_channels(hT, h, 4, fin_rw)]
        t_rw = ac.last
        h = load(ins["w_in_a"][2])
        h.used = [project_tokens(hT, h, 512, into(v_da))]
        t_v = ve.last
        h = load(ins["w_in_q"])
        h.used = [project_tokens(hT, h, 256, into(q_mem), stride=256)]
        t = head_norm(q_mem, 256, ve.last)
        t_qmT = to_channels(q_mem, qmT, 2, PM("mem_q"), t)

        rows = [arena.get(2, 256) for _ in range(2)]
        stats = [arena.get(8) for _ in range(2)]
        turned = [arena.get(2, P) for _ in range(4)]
        turned_free = [None] * 4
        n_turned = [0]

        def turn_rows(p, n, t):
            s = n_turned[0] % len(turned)
            n_turned[0] += 1
            b = pool8.take()
            w = (n + P - 1) // P
            for j in range(w):
                m = pe.turn(b.ap[0:min(P, n - j * P), j * P:(j + 1) * P], p[:, j * P:min(n, (j + 1) * P)],
                            ident, t, b.free, signal=(j == w - 1))
            k = min(P, n)
            dst = turned[s]
            a = ac.act(dst[0:k, 0:w, :], b.ap[0:k, 0:w * P].rearrange("p (j q) -> p j q", j=w), ACT.Copy, m,
                       turned_free[s])
            pool8.give(b, a)
            return dst, s, a

        for pair in range(2):
            ob = pool8.take()
            for half in range(2):
                hd = 2 * pair + half
                rr = slice(64 * half, 64 * half + 64)
                for i in range(NT):
                    r, st = rows[i], stats[i]
                    b = pool8.take()
                    m = pe.mm(b.ap[:, 0:S], qmT[rr, pair, i * P:(i + 1) * P], mkT[rr, pair, :], True, True,
                              t_qmT, t_mkT, b.free, signal=True)
                    p = r[:, 0, :]
                    a = ve.ts(p, b.ap[:, 0:S], 64 ** -0.5, None, ALU.mult, None, m)
                    pool8.give(b, a)
                    a = ve.reduce(st[:, 0:1], p, ALU.max, a)
                    a = ve.ts(st[:, 1:2], st[:, 0:1], -1.0, None, ALU.mult, None, a)
                    a = ac.act(p, p, ACT.Exp, a, bias=st[:, 1:2], accum=st[:, 2:3])
                    a = ve.recip(st[:, 3:4], st[:, 2:3], a)
                    a = ve.ts(p, p, st[:, 3:4], None, ALU.mult, None, a)
                    pT, s, a = turn_rows(p, S, a)
                    for j in range(2):
                        m = pe.mm(ob.ap[rr, i * P:(i + 1) * P], mv[:, j, 64 * hd:64 * hd + 64], pT[:, j, :],
                                  j == 0, j == 1, a, t_mv, ob.free, signal=(j == 1))
                    turned_free[s] = m
            a = ve.copy(mixT[:, 6 + pair, :], ob.ap[:, 0:S], m)
            pool8.give(ob, a)
        dump("o_mem", mixT[:, 6:8, :])

        lam_prod, lam_s = arena.get(2, 64), arena.get(8)
        lv = PM("lam").rearrange("p (a b) -> p a b", a=4)
        a = ve.tt(lam_prod, lv[:, 0:2, :], lv[:, 2:4, :], ALU.mult)
        a = ve.reduce(lam_s[:, 0:2], lam_prod, ALU.add, a)
        a = ac.act(lam_s[:, 2:4], lam_s[:, 0:2], ACT.Exp, a)
        a = ve.tt(lam_s[:, 4:5], lam_s[:, 3:4], lam_s[:, 2:3], ALU.subtract, a)
        t_lam = ve.ts(lam_s[:, 5:6], lam_s[:, 4:5], -0.2, None, ALU.add, None, a)
        neg_lam = lam_s[:, 5:6]

        pos_q, pos_k = arena.get(NT).bitcast(I32), arena.get(S).bitcast(I32)
        dist_i = arena.get(NT, S).bitcast(I32)
        t1 = fetch(pos_q, ins["pos_cols"])
        t2 = fetch(pos_k, ins["pos_rows"])
        dist, bias_h = arena.get(NT, S), arena.get(NT, S)
        for i in range(NT):
            g = gp.tt(dist_i[:, i, :], pos_q[:, i:i + 1].to_broadcast([P, S]), pos_k, ALU.subtract, t1, t2)
        t_dist = ve.copy(dist, dist_i, g)

        o_da = q_da
        t_o = None
        for hd in range(4):
            slope = 2.0 ** (-8.0 * (hd + 1) / 4)
            a = ve.ts(bias_h, dist, -slope, None, ALU.mult, None, t_dist, ve.last)
            for i in range(NT):
                dg = bias_h[:, i, i * P:(i + 1) * P]
                a = ve.tt(dg, dg, C("causal01"), ALU.mult, a)
                a = ve.tt(dg, dg, C("causal_add"), ALU.add, a)
            t_bias = a
            for i in range(NT):
                n = (i + 1) * P
                r, st = rows[i], stats[i]
                for mp in range(2):
                    rr = slice(64 * mp, 64 * mp + 64)
                    b = pool8.take()
                    m = pe.mm(b.ap[:, 0:n], qT[rr, hd, i * P:(i + 1) * P], kT[rr, hd, 0:n], True, True,
                              t_qT, t_kT, b.free, signal=True)
                    a = ve.max_of_sum(r[:, mp, 0:n], b.ap[:, 0:n], bias_h[:, i, 0:n], 1.0, st[:, mp:mp + 1],
                                      m, t_bias)
                    pool8.give(b, a)
                    a = ve.ts(st[:, 2 + mp:3 + mp], st[:, mp:mp + 1], -1.0, None, ALU.mult, None, a)
                    a = ac.act(r[:, mp, 0:n], r[:, mp, 0:n], ACT.Exp, a, bias=st[:, 2 + mp:3 + mp],
                               accum=st[:, 4 + mp:5 + mp])
                a = ve.recip(st[:, 6:8], st[:, 4:6], a)
                a1 = ve.ts(r[:, 1, 0:n], r[:, 1, 0:n], st[:, 7:8], neg_lam, ALU.mult, ALU.mult, a, t_lam)
                a = ve.stt(r[:, 0, 0:n], r[:, 0, 0:n], st[:, 6:7], r[:, 1, 0:n], ALU.mult, ALU.add, a1)
                pT, s, a = turn_rows(r[:, 0, :], n, a)
                ob = pool8.take()
                for j in range(i + 1):
                    m = pe.mm(ob.ap[:, 0:P], pT[:, j, :], v_da[:, j, hd * P:(hd + 1) * P], j == 0, j == i,
                              a, t_v, ob.free, signal=(j == i))
                turned_free[s] = m
                t_o = ve.copy(o_da[:, i, hd * P:(hd + 1) * P], ob.ap[:, 0:P], m)
                pool8.give(ob, t_o)
        ss, rs = arena.get(NT, 4), arena.get(NT, 4)
        ov = o_da.rearrange("p a (h e) -> p (a h) e", e=P)
        sqv = sq.rearrange("p a (h e) -> p (a h) e", e=P)
        a = ac.act(sq, o_da, ACT.Square, t_o)
        a = ve.reduce(ss.rearrange("p a b -> p (a b)"), sqv, ALU.add, a)
        a = rstd(rs, ss, P, EPS, a)
        a = ve.tt(ov, ov, rs.rearrange("p a b -> p (a b)").unsqueeze(2).to_broadcast([P, NT * 4, P]), ALU.mult, a)
        to_channels(o_da, mixT[:, 0:4, :], 4, PM("subln"), a, scale=0.8)
        dump("o_da", mixT[:, 0:4, :])

        barrier()
        arena.at = phase
        HP, L = 2, P
        cols_flat, diff_flat = arena.get(8 * S), arena.get(8 * S)
        cols, diff = (x.rearrange("p (a b) -> p a b", a=8) for x in (cols_flat, diff_flat))
        a = ve.tt(diff, rw[:, :, 0:S], rw[:, :, 1:S + 1], ALU.subtract, t_rw, t_z)
        for c in range(8):
            t_cols = ve.stt(cols[:, c, :], diff[:, c, :], PM("mu", c, c + 1), rw[:, c, 1:S + 1],
                            ALU.mult, ALU.add, a)
        r_, k_, v_, xwa, xg = cols[:, 0:2, :], cols[:, 2:4, :], cols[:, 4:6, :], cols[:, 6, :], cols[:, 7, :]
        kk, ld, aa, tmp = diff[:, 0:2, :], diff[:, 2:4, :], diff[:, 4:6, :], diff[:, 6:8, :]
        lora = arena.get(S)
        sg = arena.get(S)
        half_b = arena.get(4)
        gate = arena.get(2, S)
        a1 = ac.act(lora[0:64, :], xwa[0:64, :], ACT.Tanh, t_cols)
        a2 = ac.act(lora[64:128, :], xwa[64:128, :], ACT.Copy, t_cols)
        a3 = ac.act(sg, xg, ACT.Tanh, t_cols, scale=0.5)
        h1 = ve.ts(half_b[:, 0:2], PM("w0"), 0.5, None, ALU.mult, None)
        h2 = ve.ts(half_b[:, 2:4], PM("a0"), 0.5, None, ALU.mult, None)
        a3 = ve.ts(sg, sg, 0.5, 0.5, ALU.mult, ALU.add, a3)
        bw, ba_, bg = pool8.take(), pool8.take(), pool8.take()
        for c in range(2):
            mw = pe.mm(bw.ap[:, c * S:(c + 1) * S], PM("w2a2", c * P, (c + 1) * P)[0:64, :], lora[0:64, :],
                       True, True, a1, bw.free, signal=True)
            ma = pe.mm(ba_.ap[:, c * S:(c + 1) * S], PM("w2a2", c * P, (c + 1) * P)[64:128, :], lora[64:128, :],
                       True, True, a2, ba_.free, signal=True)
            mg = pe.mm(bg.ap[:, c * S:(c + 1) * S], PM("g2", c * P, (c + 1) * P), sg, True, True, a3, bg.free,
                       signal=True)
        for c in range(2):
            aw = ac.act(ld[:, c, :], bw.ap[:, c * S:(c + 1) * S], ACT.Tanh, mw, h1, bias=half_b[:, c:c + 1], scale=0.5)
            a_a = ac.act(aa[:, c, :], ba_.ap[:, c * S:(c + 1) * S], ACT.Tanh, ma, h2, bias=half_b[:, 2 + c:3 + c],
                         scale=0.5)
        t_gate = ac.act(gate, bg.ap.rearrange("p (c s) -> p c s", c=2), ACT.Copy, mg)
        for b in (bw, ba_, bg):
            pool8.give(b, ac.last)
        e5 = 0.6065306597126334
        t_ld = ve.ts(ld, ld, -0.5 * e5, -0.5 * e5, ALU.mult, ALU.add, aw)
        t_aa = ve.ts(aa, aa, 0.5, 0.5, ALU.mult, ALU.add, a_a)
        for c in range(2):
            a = ve.ts(kk[:, c, :], k_[:, c, :], PM("k_k", c, c + 1), None, ALU.mult, None)
        a = ac.act(tmp, kk, ACT.Square, a)
        b = pool8.take()
        m = pe.mm(b.ap, C("pair"), tmp.rearrange("p c s -> p (c s)"), True, True, a, b.free, signal=True)
        n2 = arena.get(2, S)
        n2f = n2.rearrange("p c s -> p (c s)")
        a = ve.ts(n2f, b.ap, 1e-24, None, ALU.max, None, m)
        pool8.give(b, a)
        halves = arena.get(2, S)
        g0 = gp.memset(halves, -0.5, ac.last)
        g = gp.tt(n2, n2, halves, ALU.pow, a, g0)
        t_kk = ve.tt(kk, kk, n2, ALU.mult, g)
        kp = arena.get(2, S)
        for c in range(2):
            a = ve.ts(kp[:, c, :], aa[:, c, :], -1.0, PM("k_a", c, c + 1), ALU.add, ALU.mult, t_aa)
        t_kp = ve.stt(kp, kp, 1.0, k_, ALU.add, ALU.mult, a)
        bonus = arena.get(2, S)
        for c in range(2):
            a = ve.stt(tmp[:, c, :], r_[:, c, :], PM("r_k", c, c + 1), kp[:, c, :], ALU.mult, ALU.mult, t_kp, m)
        b = pool8.take()
        m = pe.mm(b.ap, C("pair"), tmp.rearrange("p c s -> p (c s)"), True, True, a, b.free, signal=True)
        t_bonus = ve.tt(bonus, b.ap.rearrange("p (c s) -> p c s", c=2), v_, ALU.mult, m)
        pool8.give(b, t_bonus)
        cum = arena.get(4, L)
        ldv = ld.rearrange("p c (k l) -> p (c k) l", l=L)
        for c in range(4):
            a = ve.scan(cum[:, c, :], C("ones"), ldv[:, c, :], t_ld)
        mid = arena.get(4)
        a = ve.copy(mid, cum[:, :, L // 2 - 1], a)
        carry = arena.get(2)
        cv = cum.rearrange("p (c k) l -> p c k l", c=2)
        mv2 = mid.rearrange("p (c k) -> p c k", c=2)
        a = ve.tt(carry, cv[:, :, 0, L - 1], mv2[:, :, 0], ALU.subtract, a)
        a = ve.tt(carry, carry, mv2[:, :, 1], ALU.add, a)
        t_carry = ac.act(carry, carry, ACT.Exp, a)
        a = ve.tt(cum, cum, mid.unsqueeze(2).to_broadcast([P, 4, L]), ALU.subtract, a)
        prev = arena.get(4, L)
        a_prev = ve.tt(prev, cum, ldv, ALU.subtract, a)
        e_pos, e_neg = arena.get(4, L), n2.rearrange("p c (k l) -> p (c k) l", l=L)
        x1 = ac.act(e_pos, cum, ACT.Exp, a)
        x2 = ac.act(e_neg, cum, ACT.Exp, a, t_kk, scale=-1.0)
        x3 = ac.act(prev, prev, ACT.Exp, a_prev)

        def fl(x):
            return x.rearrange("p c (k l) -> p (c k) l", l=L)

        rho, alpha, beta, kappa = (arena.get(4, L) for _ in range(4))
        ve.tt(rho, fl(r_), e_pos, ALU.mult, x1)
        ve.tt(alpha, fl(kk), prev, ALU.mult, x3)
        a = ve.tt(aa, kk, aa, ALU.mult)
        ve.tt(beta, fl(aa), e_neg, ALU.mult, a, x2)
        t_ab = ve.tt(kappa, fl(kp), e_neg, ALU.mult)
        dump("rw_abkr", alpha)
        vT, bT, kT0 = arena.get(2, 256), arena.get(256), arena.get(256)
        b = pool8.take()
        for c in range(2):
            for kx in range(2):
                m = pe.turn(b.ap[:, kx * 256 + c * P:kx * 256 + (c + 1) * P], v_[:, c, kx * L:(kx + 1) * L], ident,
                            t_ab, b.free, signal=(c == 1 and kx == 1))
        t_vT = ac.act(vT, b.ap.rearrange("p (k c) -> p k c", k=2), ACT.Copy, m)
        pool8.give(b, t_vT)
        b = pool8.take()
        for c in range(2):
            pe.turn(b.ap[:, c * P:(c + 1) * P], beta[:, 2 * c, :], ident, b.free)
            m = pe.turn(b.ap[:, 256 + c * P:256 + (c + 1) * P], kappa[:, 2 * c, :], ident, signal=True)
        ac.act(bT, b.ap[:, 0:256], ACT.Copy, m)
        t_bkT = ac.act(kT0, b.ap[:, 256:512], ACT.Copy, m)
        pool8.give(b, t_bkT)
        AT, BT, CT, DT = (arena.get(2, 4, P) for _ in range(4))
        TI, TT, X = (x.rearrange("p (a b c) -> p a b c", a=2, b=4)
                     for x in (diff_flat[:, 0:1024], diff_flat[:, 1024:2048], cols_flat[:, 0:1024]))

        def spread(m, n=4):
            return m.unsqueeze(1).to_broadcast([P, n, P])

        for dst, left, right, mask in ((AT, beta, alpha, "before"), (BT, kappa, alpha, "before"),
                                       (CT, beta, rho, "upto"), (DT, kappa, rho, "upto")):
            for half in range(2):
                rr = slice(64 * half, 64 * half + 64)
                b = pool8.take()
                for c in range(4):
                    m = pe.mm(b.ap[:, c * P:(c + 1) * P], left[rr, c, :], right[rr, c, :], True, True, t_ab, b.free,
                              signal=(c == 3))
                a = ve.tt(dst[:, half, :, :], b.ap.rearrange("p (c l) -> p c l", c=4), spread(C(mask)), ALU.mult, m)
                pool8.give(b, a)
        t_grams = ve.last
        for half in range(2):
            gp.wait(t_grams, m)
            g = gp.do(lambda e, half=half: e.tensor_copy(TI[:, half, :, :], spread(ident)))
            g = gp.do(lambda e, half=half: e.tensor_copy(TT[:, half, :, :], spread(ident)))
        t_T = [[g, g], [g, g]]
        level = [rw_flat[:, k * 512:(k + 1) * 512].rearrange("p (c l) -> p c l", c=4) for k in range(2)]
        level_free = [None, None]
        for lv_ in range(7):
            for half in range(2):
                msk = C("levels", lv_ * P, (lv_ + 1) * P)
                g = gp.tt(level[half], AT[:, half, :, :], spread(msk), ALU.mult, t_grams, level_free[half])
                b = pool8.take()
                for c in range(4):
                    m = pe.mm(b.ap[:, c * P:(c + 1) * P], level[half][:, c, :], TI[:, half, c, :], True, True,
                              g, t_T[half], b.free, signal=(c == 3))
                level_free[half] = m
                a = ac.act(X[:, half, :, :], b.ap.rearrange("p (c l) -> p c l", c=4), ACT.Copy, m, t_T[half])
                pool8.give(b, a)
                b1, b2 = pool8.take(), pool8.take()
                if lv_ < 6:
                    for c in range(4):
                        m1 = pe.mm(b1.ap[:, c * P:(c + 1) * P], TT[:, half, c, :], X[:, half, c, :], True, True, a,
                                   b1.free, signal=(c == 3))
                for c in range(4):
                    m2 = pe.mm(b2.ap[:, c * P:(c + 1) * P], X[:, half, c, :], TT[:, half, c, :], True, True, a,
                               b2.free, signal=(c == 3))
                n1 = None
                if lv_ < 6:
                    n1 = ve.tt(TI[:, half, :, :], TI[:, half, :, :], b1.ap.rearrange("p (c l) -> p c l", c=4),
                               ALU.subtract, m1, m2, t_T[half])
                n2_ = ve.tt(TT[:, half, :, :], TT[:, half, :, :], b2.ap.rearrange("p (c l) -> p c l", c=4),
                            ALU.subtract, m2, t_T[half])
                pool8.give(b1, n1) if n1 else pool8.give(b1, *b1.free)
                pool8.give(b2, n2_)
                t_T[half] = [n1, n2_]
        R, SA = arena.get(2, 256), arena.get(2, 256)
        y = arena.get(2, 256)
        state = arena.get(2, P)
        t_state = None
        for kx in range(2):
            b = pool8.take()
            for pair in range(2):
                c = 2 * pair + kx
                if kx:
                    pe.mm(b.ap[:, pair * P:(pair + 1) * P], alpha[:, c, :], state[:, pair, :], True, False,
                          t_state, b.free)
                for half in range(2):
                    hc = slice(pair * P + half * 64, pair * P + half * 64 + 64)
                    m = pe.mm(b.ap[:, hc], BT[:, half, c, :], vT[:, kx, hc], not kx, not kx or half == 1,
                              t_vT, t_grams, b.free, signal=True)
            a = ve.ts(R[:, kx, :], b.ap[:, 0:256], -1.0, None, ALU.mult, None, m)
            pool8.give(b, a)
            b = pool8.take()
            for pair in range(2):
                c = 2 * pair + kx
                for half in range(2):
                    hc = slice(pair * P + half * 64, pair * P + half * 64 + 64)
                    m = pe.mm(b.ap[:, hc], TT[:, half, c, :], R[:, kx, hc], True, True, a, t_T, b.free, signal=True)
            t_sa = ve.copy(SA[:, kx, :], b.ap[:, 0:256], m)
            pool8.give(b, t_sa)
            b = pool8.take()
            for pair in range(2):
                c = 2 * pair + kx
                if kx:
                    pe.mm(b.ap[:, pair * P:(pair + 1) * P], rho[:, c, :], state[:, pair, :], True, False, b.free)
                for half in range(2):
                    hc = slice(pair * P + half * 64, pair * P + half * 64 + 64)
                    pe.mm(b.ap[:, hc], CT[:, half, c, :], SA[:, kx, hc], not kx, False, t_sa, b.free)
                    m = pe.mm(b.ap[:, hc], DT[:, half, c, :], vT[:, kx, hc], False, not kx or half == 1, signal=True)
            t_y = ac.act(y[:, kx, :], b.ap[:, 0:256], ACT.Copy, m)
            pool8.give(b, t_y)
            if not kx:
                b = pool8.take()
                for pair in range(2):
                    pc = slice(pair * P, (pair + 1) * P)
                    pe.mm(b.ap[:, pc], bT[:, pc], SA[:, 0, pc], True, False, t_bkT, b.free)
                    m = pe.mm(b.ap[:, pc], kT0[:, pc], vT[:, 0, pc], False, True, signal=True)
                for pair in range(2):
                    t_state = ve.stt(state[:, pair, :], b.ap[:, pair * P:(pair + 1) * P], carry[:, pair:pair + 1],
                                     C("pair"), ALU.mult, ALU.mult, m, t_carry)
                pool8.give(b, t_state)
        dump("rw_y", y)
        ys = y.rearrange("p k (h e) -> p (k h) e", e=64)
        s1, s2, rs = arena.get(8), arena.get(8), arena.get(8)
        sq8 = R.rearrange("p k (h e) -> p (k h) e", e=64)
        a = ve.reduce(s1, ys, ALU.add, t_y)
        a = ve.ts(s1, s1, 1.0 / 64, None, ALU.mult, None, a)
        a = ve.tt(ys, ys, s1.unsqueeze(2).to_broadcast([P, 8, 64]), ALU.subtract, a)
        b = ac.act(sq8, ys, ACT.Square, a)
        b = ve.reduce(s2, sq8, ALU.add, b)
        a = rstd(rs, s2, 64, 64e-5, b)
        a = ve.tt(ys, ys, rs.unsqueeze(2).to_broadcast([P, 8, 64]), ALU.mult, a)
        b = pool8.take()
        for c in range(2):
            for kx in range(2):
                m = pe.turn(b.ap[:, c * S + kx * P:c * S + (kx + 1) * P], y[:, kx, c * P:(c + 1) * P], ident, a, b.free,
                            signal=True)
        for c in range(2):
            a = ve.ts(mixT[:, 4 + c, :], b.ap[:, c * S:(c + 1) * S], PM("gn_w", c, c + 1), PM("gn_b", c, c + 1),
                      ALU.mult, ALU.add, m)
        pool8.give(b, a)
        a = ve.tt(mixT[:, 4:6, :], mixT[:, 4:6, :], bonus, ALU.add, a)
        t_mix = ve.tt(mixT[:, 4:6, :], mixT[:, 4:6, :], gate, ALU.mult, a, t_gate)
        dump("o_rw", mixT[:, 4:6, :])

        def add_product(xT, src, *after):
            for j in range(2):
                h = load(src[j])

                def fin(i, ps, m, j=j):
                    r = resid[:, i, j * 512:(j + 1) * 512]
                    return (ve.tt(r, r, ps, ALU.add, m),)

                h.used = [project_tokens(xT, h, 512, fin, *after)]

        add_product(mixT, ins["w_out"], t_mix)
        dump("x_mid", resid[:, :, :])

        def moe(tag, gain, router, router_b, w_gu, w_dn, next_params):
            barrier()
            marks = [l.last for l in lines]
            t_next = fetch(tail[:, 0:next_params.shape[1]], next_params, *marks)
            arena.at, arena.size = 0, arena_size - tail.shape[1]
            xn, xT = arena.get(NT, D), arena.get(KD, S)
            t = norm_rows(resid, xn, ve.last)
            t_xn = t
            t_xT = to_channels(xn, xT, KD, gain, t)
            lg = arena.get(NT, 20)
            b = pool8.take()
            rt = router.rearrange("p (k n) -> p k n", k=KD)
            for i in range(NT):
                for k in range(KD):
                    m = pe.mm(b.ap[:, i * 20:(i + 1) * 20], xT[:, k, i * P:(i + 1) * P], rt[:, k, :], k == 0,
                              k == KD - 1, t_xT, b.free, signal=(k == KD - 1))
            a = ve.tt(lg, b.ap[:, 0:40].rearrange("p (i n) -> p i n", i=NT),
                      router_b.unsqueeze(1).to_broadcast([P, NT, 20]), ALU.add, m)
            pool8.give(b, a)
            dump("logits" + tag, lg)
            gl = lg[:, :, 0:4]
            el = lg[:, :, 4:20].rearrange("p i (g e) -> p i g e", g=4)
            rank4 = C("group_rank").unsqueeze(1).to_broadcast([P, NT, 4])

            def first_best(v, oh, mx, t):
                a = ve.reduce(mx, v, ALU.max, t)
                mb = mx.unsqueeze(2).to_broadcast([P, NT, 4])
                a = ve.tt(oh, v, mb, ALU.is_ge, a)
                a = ve.tt(oh, oh, rank4, ALU.mult, a)
                sc = arena.get(NT)
                a = ve.reduce(sc, oh, ALU.max, a)
                sbc = sc.unsqueeze(2).to_broadcast([P, NT, 4])
                return ve.tt(oh, rank4, sbc, ALU.is_equal, a)

            gmax, goh, gd = arena.get(NT), arena.get(NT, 4), arena.get(NT, 4)
            a = first_best(gl, goh, gmax, a)
            a = ve.tt(gd, gl, gmax.unsqueeze(2).to_broadcast([P, NT, 4]), ALU.subtract, a)
            b_ = ac.act(gd, gd, ACT.Exp, a)
            psel = arena.get(NT)
            a = ve.reduce(psel, gd, ALU.add, b_)
            a = ve.recip(psel, psel, a)
            em, ie = arena.get(NT * 4, 4), arena.get(NT, 4)
            emv = em.rearrange("p (i g) e -> p i g e", i=NT)
            for i in range(NT):
                a = ve.tt(em[:, 4 * i:4 * i + 4, :], el[:, i, :, :], goh[:, i, :].unsqueeze(2).to_broadcast([P, 4, 4]),
                          ALU.mult, a)
            for i in range(NT):
                a = ve.reduce(ie[:, i, :], em[:, 4 * i:4 * i + 4, :].rearrange("p g e -> p e g"), ALU.add, a)
            m1, m2, o1, o2 = arena.get(NT), arena.get(NT), arena.get(NT, 4), arena.get(NT, 4)
            a = first_best(ie, o1, m1, a)
            a = ve.stt(ie, o1, -1e30, ie, ALU.mult, ALU.add, a)
            a = first_best(ie, o2, m2, a)
            a = ve.tt(m2, m2, m1, ALU.subtract, a)
            b_ = ac.act(m2, m2, ACT.Exp, a)
            a = ve.ts(m1, m2, 1.0, None, ALU.add, None, b_)
            a = ve.recip(m1, m1, a)
            a = ve.tt(m1, m1, psel, ALU.mult, a)
            a = ve.tt(m2, m2, m1, ALU.mult, a)
            gates = arena.get(NT, 4)
            a = ve.tt(o1, o1, m1.unsqueeze(2).to_broadcast([P, NT, 4]), ALU.mult, a)
            a = ve.tt(o2, o2, m2.unsqueeze(2).to_broadcast([P, NT, 4]), ALU.mult, a)
            t_gates = ve.tt(gates, o1, o2, ALU.add, a)
            dump("gates" + tag, gates)
            b = pool8.take()
            for i in range(NT):
                if i:
                    pe.mm(b.ap[:, 4 * i:4 * i + 4], C("ones"), goh[:, 0, :], True, False, b.free, t_gates)
                m = pe.mm(b.ap[:, 4 * i:4 * i + 4], C("before"), goh[:, i, :], i == 0, True, b.free, t_gates,
                          signal=True)
            for i in range(NT):
                m = pe.mm(b.ap[:, 8:12], C("ones"), goh[:, i, :], i == 0, i == NT - 1, signal=(i == NT - 1))
            place = arena.get(NT, 4)
            counts = arena.get(4)
            top = arena.get(1)
            a = ve.stt(place, b.ap[:, 0:8].rearrange("p (i g) -> p i g", i=NT), 1.0, goh, ALU.add, ALU.mult, m)
            a = ve.ts(place, place, -1.0, None, ALU.add, None, a)
            t_place = a
            a = ve.reduce(top, b.ap[:, 8:12], ALU.max, a)
            pool8.give(b, a)
            top_i = arena.get(1).bitcast(I32)
            t_top = ve.copy(top_i, top, a)

            xg = [arena.get(KD, CAP) for _ in range(2)]
            sel = [arena.get(NT, CAP) for _ in range(2)]
            selT = [arena.get(NT, P) for _ in range(2)]
            sgate = [arena.get(4) for _ in range(2)]
            th = [arena.get(512) for _ in range(2)]
            hid = [arena.get(512) for _ in range(2)]
            hidT = [arena.get(4, CAP) for _ in range(2)]
            yg = arena.get(D)

            def experts(first):
                gu_banks = Banks([x[:, :] for x in banks_all[0:4]])
                y_banks = [Bank(x[:, :]) for x in banks_all[4:6]]
                misc = Banks([x[:, :] for x in banks_all[6:8]])
                start = [l.last for l in lines]
                free = {}
                yg_free = [None]

                def gather(g):
                    s = g % 2
                    for i in range(NT):
                        a = ve.ts(sel[s][:, i, :], C("iota"), float(first), place[:, i, g:g + 1], ALU.add,
                                  ALU.is_equal, t_place, start, free.get(("sel", s)))
                    t_sel = a
                    for kk_ in range(0, KD, 4):
                        b = misc.take()
                        for k in range(kk_, kk_ + 4):
                            for i in range(NT):
                                m = pe.mm(b.ap[:, (k - kk_) * CAP:(k - kk_ + 1) * CAP], xn[:, i, k * P:(k + 1) * P],
                                          sel[s][:, i, :], i == 0, i == NT - 1, t_sel, t_xn, b.free, start,
                                          signal=(k == kk_ + 3 and i == NT - 1))
                        for k in range(kk_, kk_ + 4):
                            a = ve.ts(xg[s][:, k, :], b.ap[:, (k - kk_) * CAP:(k - kk_ + 1) * CAP], gain[:, k:k + 1],
                                      None, ALU.mult, None, m, free.get(("xg", s)))
                        misc.give(b, a)
                    t_xg = a
                    b = misc.take()
                    for i in range(NT):
                        pe.turn(b.ap[:, i * P:(i + 1) * P], sel[s][:, i, :], ident, b.free)
                    for i in range(NT):
                        m = pe.mm(b.ap[:, 256:260], sel[s][:, i, :], gates[:, i, :], i == 0, i == NT - 1, t_gates,
                                  signal=(i == NT - 1))
                    a = ve.copy(selT[s], b.ap[:, 0:256].rearrange("p (i q) -> p i q", i=NT), m, free.get(("selT", s)))
                    a = ve.ts(sgate[s], b.ap[:, 256:260], 0.5, None, ALU.mult, None, m, free.get(("sgate", s)))
                    misc.give(b, a)
                    free[("sel", s)] = m
                    return t_xg, a

                def gate_up(e, t_xg, t_gate):
                    g, s = e // 4, (e // 4) % 2
                    ps = []
                    for which in range(2):
                        h = load(w_gu[e, which])
                        w = h.slot.rearrange("p (k n) -> p k n", k=KD)
                        b = gu_banks.take()
                        for k in range(KD):
                            m = pe.mm(b.ap, xg[s][:, k, :], w[:, k, :], k == 0, k == KD - 1, h.ready, t_xg, b.free,
                                      start, signal=(k == KD - 1))
                        h.used = [m]
                        ps.append((b, m))
                    free[("xg", s)] = m
                    (bg_, mg_), (bu, mu_) = ps
                    u = e % 2
                    a = ac.act(th[u], bg_.ap, ACT.Tanh, mg_, start, free.get(("th", u)), scale=0.5)
                    a = ve.stt(th[u], th[u], 1.0, bg_.ap, ALU.add, ALU.mult, a)
                    gu_banks.give(bg_, a)
                    a = ve.stt(hid[u], th[u], sgate[s][:, e % 4:e % 4 + 1], bu.ap, ALU.mult, ALU.mult, a, mu_, t_gate,
                               free.get(("hid", u)))
                    gu_banks.give(bu, a)
                    free[("th", u)] = a
                    free[("sgate", s)] = a
                    return a

                def turn_hidden(e, t_hid):
                    u = e % 2
                    b = misc.take()
                    for j in range(4):
                        m = pe.turn(b.ap[:, j * CAP:(j + 1) * CAP], hid[u][:, j * P:(j + 1) * P], ident, t_hid, b.free,
                                    signal=(j == 3))
                    free[("hid", u)] = m
                    a = ac.act(hidT[u], b.ap.rearrange("p (j c) -> p j c", j=4), ACT.Copy, m, free.get(("hidT", u)))
                    misc.give(b, a)
                    return a

                def down(e, t_hidT):
                    u = e % 2
                    h = load(w_dn[e])
                    w = h.slot.rearrange("p (k n) -> p k n", k=4)
                    for j in range(2):
                        for k in range(4):
                            m = pe.mm(y_banks[j].ap, hidT[u][:, k, :], w[:, k, j * 512:(j + 1) * 512],
                                      e % 4 == 0 and k == 0, e % 4 == 3 and k == 3, h.ready, t_hidT, y_banks[j].free,
                                      start, signal=(k == 3))
                    h.used = [m]
                    free[("hidT", u)] = m
                    return m

                def scatter(g, m):
                    s = g % 2
                    for j in range(2):
                        a = ac.act(yg[:, j * 512:(j + 1) * 512], y_banks[j].ap, ACT.Copy, m, yg_free[0])
                        y_banks[j].free = [a]
                    for j in range(2):
                        for i in range(NT):
                            b = misc.take()
                            m = pe.mm(b.ap, selT[s][:, i, :], yg[:, j * 512:(j + 1) * 512], True, True, a, b.free,
                                      signal=True)
                            r = resid[:, i, j * 512:(j + 1) * 512]
                            v = ve.tt(r, r, b.ap, ALU.add, m)
                            misc.give(b, v)
                    yg_free[0] = m
                    free[("selT", s)] = m

                ready = {0: gather(0)}
                pending = None
                for e in range(17):
                    if e < 16:
                        g = e // 4
                        t_hid = gate_up(e, *ready[g])
                    if e:
                        t_hT_ = turn_hidden(e - 1, pending)
                        if e < 16 and e % 4 == 2 and e // 4 < 3:
                            ready[e // 4 + 1] = gather(e // 4 + 1)
                        m = down(e - 1, t_hT_)
                        if e % 4 == 0:
                            scatter(e // 4 - 1, m)
                    if e < 16:
                        pending = t_hid
                return m

            counts_read = {}
            for l in lines + (sp,):
                l.wait(t_top)
                counts_read[l.name] = l.read(top_i[0:1, 0:1])
            experts(0)

            barrier()
            sp.wait(*[l.last for l in lines])
            outer_loads = list(loads)
            loads.clear()
            outer_sems = sems_now[0]
            sems_now[0] = [sem(f"more_slot{k}{tag}") for k in range(NSLOT)]
            for l in lines + (sp,):
                l.enter(sem("more_" + l.name + tag))
            for first in range(CAP, S, CAP):
                experts(first)
                barrier()
            sp.wait(*[l.last for l in lines])
            for l in lines + (sp,):
                l.leave(counts_read[l.name], MORE_ABOVE)
            loads[:] = outer_loads
            sems_now[0] = outer_sems
            return t_next

        pool8.banks[0].free
        t_params2 = moe("_1", PM("ffn_norm"), PM("router"), PM("router_b"), ins["w_gu_1"], ins["w_dn_1"],
                        ins["params2"])
        barrier()
        dump("x_1", resid[:, :, :])

        arena.at = 0
        hT = arena.get(KD, S)
        u_a, gate_b, q_c = arena.get(4, S), arena.get(4, S), arena.get(4, S)
        rec = arena.get(4, S + 3)
        vk_at = arena.at
        v_a = arena.get(NT, 512)
        kv_c = arena.get(4, S)
        vg = arena.get(NT, 280)
        PAD = 16
        xd = arena.get(4, S + PAD)
        y_c = arena.get(4, S)
        phase = arena.at
        hn = arena.get(NT, D)
        t = norm_rows(resid, hn)
        t_hT = to_channels(hn, hT, KD, PP("norm1"), t, t_params2)
        arena.at = phase
        t_pad = [ve.memset(rec[:, :, 0:3], 0.0), ve.memset(xd[:, :, 0:PAD], 0.0)]

        def into_channels(dst, off=0):
            def fin(c, n, ps, m):
                return (ac.act(dst[:, c:c + n, off:off + S], ps, ACT.Copy, m),)
            return fin

        h = load(ins["w_kv_2"])
        h.used = [project_channels(hT, h, 4, into_channels(kv_c), t_hT)]
        t_kvc = ac.last
        h = load(ins["w_vg_2"])

        def fin_vg(i, ps, m):
            return (ac.act(vg[:, i, :], ps, ACT.Copy, m),)

        h.used = [project_tokens(hT, h, 280, fin_vg, stride=280)]
        t_vg = ac.last
        h = load(ins["w_in_2"][4])
        h.used = [project_channels(hT, h, 4, into_channels(q_c))]
        t_qc = ac.last
        h = load(ins["w_in_2"][3])
        h.used = [project_channels(hT, h, 4, into_channels(rec, 3))]
        t_rec = ac.last

        blocks = [arena.get(32, 15) for _ in range(2)]
        for c in range(2):
            kvv = kv_c[:, c, :].rearrange("p (n b) -> p b n", b=16)
            for half in range(2):
                pe_ = PP("cmp_pe", c * 32 + half * 16, c * 32 + half * 16 + 16)
                t_blk = ve.tt(blocks[c][:, half * 16:half * 16 + 16, :], kvv[:, :, half:half + 15],
                              pe_.unsqueeze(2).to_broadcast([P, 16, 15]), ALU.add, t_kvc)
        hidc, gtmp = arena.get(2, 15), arena.get(2, 15)
        b = pool8.take()
        for c in range(2):
            h = load(ins["w_cmp1"][c])
            w = h.slot.rearrange("p (l e) -> p l e", l=32)
            for l in range(32):
                m = pe.mm(b.ap[:, c * 15:c * 15 + 15], w[:, l, :], blocks[c][:, l, :], l == 0, l == 31, h.ready,
                          t_blk, b.free, signal=(l == 31))
            h.used = [m]
        a = ve.copy(hidc, b.ap[:, 0:30].rearrange("p (c n) -> p c n", c=2), m)
        pool8.give(b, a)

        def gelu(dst, x, tmp, *after):
            a = ac.act(tmp, x, ACT.Square, *after)
            a = ve.ts(tmp, tmp, 0.044715, 1.0, ALU.mult, ALU.add, a)
            a = ve.tt(tmp, tmp, x, ALU.mult, a)
            a = ac.act(tmp, tmp, ACT.Tanh, a, scale=0.7978845608028654)
            a = ve.stt(tmp, tmp, 1.0, x, ALU.add, ALU.mult, a)
            return ve.ts(dst, tmp, 0.5, None, ALU.mult, None, a)

        a = gelu(hidc, hidc, gtmp, a)
        kc, vc = arena.get(15), arena.get(P)[0:15, :]
        b = pool8.take()
        pe.mm(b.ap[:, 0:15], PP("cmp_w2", 0, P), hidc[:, 0, :], True, True, a, b.free)
        m = pe.mm(b.ap[0:15, 128:256], hidc[:, 1, :], PP("cmp_w2", P, 2 * P), True, True, signal=True)
        ve.copy(kc, b.ap[:, 0:15], m)
        t_cmp = ve.copy(vc, b.ap[0:15, 128:256], m)
        pool8.give(b, t_cmp)
        gates3 = arena.get(NT, 24)
        a = ac.act(gates3, vg[:, :, 256:280], ACT.Tanh, t_vg, scale=0.5)
        t_g3 = ve.ts(gates3, gates3, 0.5, 0.5, ALU.mult, ALU.add, a)
        g3 = gates3.rearrange("p i (h b) -> p i h b", b=3)

        def proj_gate_b():
            h = load(ins["w_in_2"][2])
            h.used = [project_channels(hT, h, 4, into_channels(gate_b))]
            return ac.last

        def proj_xd():
            h = load(ins["w_in_2"][5])
            h.used = [project_channels(hT, h, 4, into_channels(xd, PAD))]
            return ac.last

        def proj_v():
            h = load(ins["w_in_2"][1])
            h.used = [project_tokens(hT, h, 512, into(v_a))]
            return ve.last

        def proj_u():
            h = load(ins["w_in_2"][0])
            h.used = [project_channels(hT, h, 4, into_channels(u_a))]
            return ac.last

        t_gb, t_xd = proj_gate_b(), proj_xd()

        pc, pst, pcT = arena.get(8, 15), arena.get(4, 8), [arena.get(8, P) for _ in range(NT)]
        t_pcT = []
        for i in range(NT):
            bb = [pool8.take(), pool8.take()]
            for g in range(2):
                rr = slice(64 * g, 64 * g + 64)
                for j in range(4):
                    m = pe.mm(bb[g].ap[:, j * 15:j * 15 + 15], q_c[rr, j, i * P:(i + 1) * P], kc[rr, :], True, True,
                              t_qc, t_cmp, bb[g].free, signal=(j == 3))
                ca = C("cmp_add", 15 * i, 15 * i + 15).unsqueeze(1).to_broadcast([P, 4, 15])
                a = ve.stt(pc[:, 4 * g:4 * g + 4, :], bb[g].ap[:, 0:60].rearrange("p (j n) -> p j n", j=4), 0.125,
                           ca, ALU.mult, ALU.add, m, pe.last)
                pool8.give(bb[g], a)
            a = ve.reduce(pst[:, 0, :], pc, ALU.max, a)
            a = ve.tt(pc, pc, pst[:, 0, :].unsqueeze(2).to_broadcast([P, 8, 15]), ALU.subtract, a)
            a = ac.act(pc, pc, ACT.Exp, a)
            a = ve.reduce(pst[:, 1, :], pc, ALU.add, a)
            a = ve.recip(pst[:, 2, :], pst[:, 1, :], a)
            a = ve.stt(pst[:, 3, :], pst[:, 2, :], C("cmp_any", i, i + 1), g3[:, i, :, 0], ALU.mult, ALU.mult, a, t_g3)
            a = ve.tt(pc, pc, pst[:, 3, :].unsqueeze(2).to_broadcast([P, 8, 15]), ALU.mult, a)
            bb = [pool8.take(), pool8.take()]
            for g in range(2):
                for j in range(4):
                    m = pe.turn(bb[g].ap[0:15, j * P:(j + 1) * P], pc[:, 4 * g + j, :], ident, a, bb[g].free,
                                signal=(j == 3))
                x = ac.act(pcT[i][0:15, 4 * g:4 * g + 4, :],
                           bb[g].ap[0:15, :].rearrange("p (j q) -> p j q", j=4), ACT.Copy, m)
                pool8.give(bb[g], x)
            t_pcT.append(x)

        cmask = arena.get(2, P)
        a = ve.memset(cmask[:, 0, :], 0.0)
        t_cmask = ve.copy(cmask[:, 1, :], C("causal_add"))
        cm = cmask.rearrange("p a b -> p (a b)")
        rows = [arena.get(2, 256) for _ in range(4)]
        stats = [arena.get(8) for _ in range(4)]
        turned = [arena.get(2, P) for _ in range(8)]
        turned_free = [None] * 8
        n_turned[0] = 0
        row_free = [None] * 4
        n_row = 0

        def nsa_scores(g, j, i, r, st, free_r):
            n = (i + 1) * P
            rr = slice(64 * g, 64 * g + 64)
            hh = 4 * g + j
            for br in range(2):
                b = pool8.take()
                m = pe.mm(b.ap[:, 0:n], q_c[rr, j, i * P:(i + 1) * P], kv_c[rr, 2 + br, 0:n], True, True, t_qc, t_kvc,
                          b.free, signal=True)
                a = ve.max_of_sum(r[:, br, 0:n], b.ap[:, 0:n], cm[:, S - n:S], 0.125, st[:, br:br + 1], m, t_cmask,
                                  free_r)
                pool8.give(b, a)
            a = ve.ts(st[:, 2:4], st[:, 0:2], -1.0, None, ALU.mult, None, a)
            for br in range(2):
                x = ac.act(r[:, br, 0:n], r[:, br, 0:n], ACT.Exp, a, bias=st[:, 2 + br:3 + br],
                           accum=st[:, 4 + br:5 + br])
            a = ve.recip(st[:, 4:6], st[:, 4:6], x)
            a = ve.tt(st[:, 6:8], st[:, 4:6], g3[:, i, hh, 1:3], ALU.mult, a, t_g3)
            for br in range(2):
                x = ve.ts(r[:, br, 0:n], r[:, br, 0:n], st[:, 6 + br:7 + br], None, ALU.mult, None, a)
            return x

        t_v = t_u = None
        units = [(j, g, i) for j in range(4) for g in range(2) for i in range(NT)]
        scored = {}
        LEAD = 2

        def nsa_ahead(n):
            if n < len(units):
                j, g, i = units[n]
                s = n % 4
                scored[n] = nsa_scores(g, j, i, rows[s], stats[s], row_free[s])

        for n in range(LEAD):
            nsa_ahead(n)
        for n, (j, g, i) in enumerate(units):
            nsa_ahead(n + LEAD)
            s = n % 4
            if g == 0 and i == 0:
                ob = pool8.take()
            rr = slice(64 * g, 64 * g + 64)
            hh = 4 * g + j
            w = (i + 1) * P
            got = [turn_rows(rows[s][:, br, :], w, scored[n]) for br in range(2)]
            row_free[s] = pe.last
            pe.mm(ob.ap[rr, i * P:(i + 1) * P], vc[:, 64 * g:64 * g + 64], pcT[i][0:15, hh, :], True, False,
                  t_pcT[i], t_cmp, ob.free)
            for br in range(2):
                pT, slot_, t_pT = got[br]
                for k in range(i + 1):
                    m = pe.mm(ob.ap[rr, i * P:(i + 1) * P], vg[:, k, br * P + 64 * g:br * P + 64 * g + 64],
                              pT[:, k, :], False, br == 1 and k == i, t_pT, t_vg, signal=(k == i))
                turned_free[slot_] = m
            if g == 1 and i == NT - 1:
                t_yc = ve.copy(y_c[:, j, :], ob.ap[:, 0:S], m)
                pool8.give(ob, t_yc)
            if n == 5:
                t_v = proj_v()
            if n == 10:
                t_u = proj_u()
        dump("y_c", y_c)

        barrier()
        arena.at = phase
        cl, cz, cy, cs, cq, cp = (arena.get(4) for _ in range(6))
        a = ve.ts(cz, PP("lru_lam"), -1.0, None, ALU.mult, None)
        a = ve.tt(cy, PP("lru_lam"), cz, ALU.max, a)
        a = ac.act(cy, cy, ACT.Exp, a, scale=-1.0)
        a = ve.ts(cs, cy, 2.0, None, ALU.add, None, a)
        a = ve.recip(cs, cs, a)
        a = ve.tt(cs, cs, cy, ALU.mult, a)
        a = ve.tt(cq, cs, cs, ALU.mult, a)
        a = ve.ts(cp, cq, 1.0 / 17, None, ALU.mult, None, a)
        for k in (15, 13, 11, 9, 7, 5, 3):
            a = ve.stt(cp, cp, 1.0 / k, cq, ALU.add, ALU.mult, a)
        a = ve.stt(cp, cp, 1.0, cs, ALU.add, ALU.mult, a)
        a = ve.ts(cp, cp, 2.0, None, ALU.mult, None, a)
        a = ve.stt(cl, cz, 0.0, cp, ALU.max, ALU.add, a)
        t_cl = ve.ts(cl, cl, -4.0, None, ALU.mult, None, a)
        half_b = arena.get(8)
        h1 = ve.ts(half_b[:, 0:4], PP("lru_ba"), 0.5, None, ALU.mult, None)
        h2 = ve.ts(half_b[:, 4:8], PP("lru_bx"), 0.5, None, ALU.mult, None)
        xc, la, th_, ti, tmp4 = (arena.get(4, S) for _ in range(5))
        t_xc = []
        for c in range(4):
            a = ve.ts(xc[:, c, :], rec[:, c, 0:S], PP("conv_w", c, c + 1), PP("conv_b", c, c + 1), ALU.mult, ALU.add,
                      t_rec, t_pad)
            for k in range(1, 4):
                a = ve.stt(xc[:, c, :], rec[:, c, k:k + S], PP("conv_w", 4 * k + c, 4 * k + c + 1), xc[:, c, :],
                           ALU.mult, ALU.add, a)
            t_xc.append(a)
        for name, dst, hb in (("lru_wa", la, 0), ("lru_wx", ti, 4)):
            for c2 in range(0, 4, 2):
                b = pool8.take()
                for c in (c2, c2 + 1):
                    m = pe.mm(b.ap[:, (c - c2) * S:(c - c2 + 1) * S], PP(name, c * P, (c + 1) * P), xc[:, c, :], True,
                              True, t_xc[c], b.free, signal=True)
                for c in (c2, c2 + 1):
                    a = ac.act(dst[:, c, :], b.ap[:, (c - c2) * S:(c - c2 + 1) * S], ACT.Tanh, m, h1, h2,
                               bias=half_b[:, hb + c:hb + c + 1], scale=0.5)
                pool8.give(b, a)
        t_ti = a
        for c in range(4):
            a = ve.ts(la[:, c, :], la[:, c, :], 1.0, cl[:, c:c + 1], ALU.add, ALU.mult, t_ti, t_cl)
        t_la = a
        a = ac.act(th_, la, ACT.Tanh, t_la)
        t_a = ac.act(la, la, ACT.Exp, t_la, a)
        a = ve.ts(tmp4, th_, -1.0, 1.0, ALU.mult, ALU.add, a)
        a = ve.recip(tmp4, tmp4, a)
        a = ve.tt(tmp4, tmp4, th_, ALU.mult, a)
        a = ve.ts(tmp4, tmp4, -2.0, 1e-30, ALU.mult, ALU.max, a)
        t_sq = ac.act(tmp4, tmp4, ACT.Sqrt, a)
        a = ve.stt(ti, ti, 1.0, xc, ALU.add, ALU.mult)
        a = ve.stt(ti, ti, 0.5, tmp4, ALU.mult, ALU.mult, a, t_sq)
        for c in range(4):
            a = ve.scan(th_[:, c, :], la[:, c, :], ti[:, c, :], a, t_a)
        t_h = a
        a = gelu(gate_b, gate_b, tmp4, t_gb, t_h)
        t_yb = ve.tt(gate_b, gate_b, th_, ALU.mult, a)
        dump("y_b", gate_b)

        win = [arena.get(4, S + PAD) for _ in range(2)]
        Z = S + PAD
        a = ve.tt(win[0][:, :, 1:Z], xd[:, :, 1:Z], xd[:, :, 0:Z - 1], ALU.add, t_xd, t_pad)
        a = ve.tt(win[1][:, 1:4, 3:Z], win[0][:, 1:4, 3:Z], win[0][:, 1:4, 1:Z - 2], ALU.add, a)
        a = ve.tt(win[0][:, 2:4, 7:Z], win[1][:, 2:4, 7:Z], win[1][:, 2:4, 3:Z - 4], ALU.add, a)
        a = ve.tt(win[1][:, 3, 15:Z], win[0][:, 3, 15:Z], win[0][:, 3, 7:Z - 8], ALU.add, a)
        for c, wlen in enumerate((2, 4, 8, 16)):
            src = win[c % 2][:, c, :]
            f1 = ve.tt(src[:, PAD:PAD + 16], src[:, PAD:PAD + 16], C("pool_inv", 16 * c, 16 * c + 16), ALU.mult, a)
            f1 = ve.tt(src[:, PAD:PAD + 16], src[:, PAD:PAD + 16], xd[:, c, PAD:PAD + 16], ALU.subtract, f1)
            f2 = ve.stt(src[:, PAD + 16:Z], src[:, PAD + 16:Z], 1.0 / wlen, xd[:, c, PAD + 16:Z], ALU.mult,
                        ALU.subtract, a)
        t_pool = f2
        y_d = xc
        for c2 in range(0, 4, 2):
            b = pool8.take()
            for c in (c2, c2 + 1):
                m = pe.mm(b.ap[:, (c - c2) * S:(c - c2 + 1) * S], PP("pool_w", c * P, (c + 1) * P),
                          win[c % 2][:, c, PAD:Z], True, True, f1, t_pool, b.free, signal=True)
            for c in (c2, c2 + 1):
                a = ve.ts(y_d[:, c, :], b.ap[:, (c - c2) * S:(c - c2 + 1) * S], PP("pool_scale", c, c + 1), None,
                          ALU.mult, None, m)
            pool8.give(b, a)
        t_yd = a
        dump("y_d", y_d)

        wsT = PP("gm_wsT").rearrange("p (g t) -> p g t", g=4)
        t_ws = ve.tt(wsT, wsT, C("upto").unsqueeze(1).to_broadcast([P, 4, P]), ALU.mult)
        gt = tmp4
        v_flat = v_a.rearrange("p i n -> p (i n)")
        g_flat = gt.rearrange("p i n -> p (i n)")
        a = gelu(v_flat, v_flat, g_flat, t_v, t_yb)
        ss, rs = arena.get(NT), arena.get(NT)
        for i in range(NT):
            x = ac.act(g_flat[:, i * 512:(i + 1) * 512], v_a[:, i, :], ACT.Square, a, accum=ss[:, i:i + 1])
        r = rstd(rs, ss, 512, EPS, x)
        for i in range(NT):
            t_vn = ve.ts(v_a[:, i, :], v_a[:, i, :], rs[:, i:i + 1], None, ALU.mult, None, r)
        t_ug = gelu(u_a, u_a, gt, t_u, t_vn)
        mixed = la
        for i in range(NT):
            b = pool8.take()
            for g in range(4):
                m = pe.mm(b.ap[:, g * P:(g + 1) * P], v_a[:, i, g * P:(g + 1) * P], wsT[:, g, :], True, True, t_vn,
                          t_ws, b.free, signal=(g == 3))
            for g in range(4):
                a = ve.stt(mixed[:, g, i * P:(i + 1) * P], b.ap[:, g * P:(g + 1) * P], PP("gm_norm", g, g + 1),
                           PP("gm_b", g * P, (g + 1) * P), ALU.mult, ALU.add, m)
            pool8.give(b, a)
        t_ya = ve.tt(u_a, u_a, mixed, ALU.mult, a, t_ug)
        dump("y_a", u_a)

        barrier()
        tg = [win[0].rearrange("p a b -> p (a b)")[:, 512 * k:512 * k + 512] for k in range(2)]
        merged = arena_all[:, vk_at:vk_at + NT * D].rearrange("p (i d) -> p i d", i=NT)
        tg_free = [None, None]
        n_tg = 0
        for n, yT in enumerate((u_a, gate_b, y_c, y_d)):
            hb_ = load(ins["w_branch"][n])
            wb = hb_.slot.rearrange("p (k n) -> p k n", k=4)
            for half in range(2):
                hm = load(ins["w_mg"][n, half])
                wm = hm.slot.rearrange("p (k n) -> p k n", k=KD)
                for i in range(NT):
                    bm, bb_ = pool8.take(), pool8.take()
                    for k in range(KD):
                        m1 = pe.mm(bm.ap, hT[:, k, i * P:(i + 1) * P], wm[:, k, :], k == 0, k == KD - 1, hm.ready,
                                   bm.free, signal=(k == KD - 1))
                    for k in range(4):
                        m2 = pe.mm(bb_.ap, yT[:, k, i * P:(i + 1) * P], wb[:, k, half * 512:(half + 1) * 512], k == 0,
                                   k == 3, hb_.ready, bb_.free, signal=(k == 3))
                    u = n_tg % 2
                    n_tg += 1
                    a = ac.act(tg[u], bm.ap, ACT.Tanh, m1, tg_free[u], scale=0.5)
                    pool8.give(bm, a)
                    mv_ = merged[:, i, half * 512:(half + 1) * 512]
                    if n == 0:
                        a = ve.stt(mv_, tg[u], 1.0, bb_.ap, ALU.add, ALU.mult, a, m2)
                        pool8.give(bb_, a)
                    else:
                        a = ve.stt(tg[u], tg[u], 1.0, bb_.ap, ALU.add, ALU.mult, a, m2)
                        pool8.give(bb_, a)
                        a = ve.tt(mv_, mv_, tg[u], ALU.add, a)
                    tg_free[u] = a
                hm.used = [m1]
            hb_.used = [m2]
        mergedT = hT
        t = to_channels(merged, mergedT, KD, None, ve.last, pe.last, scale=0.5)
        add_product(mergedT, ins["w_out_2"], t)
        dump("x_mid2", resid[:, :, :])
        t_final = moe("_2", PM("norm2"), PM("router_2"), PM("router_b_2"), ins["w_gu_2"], ins["w_dn_2"],
                      ins["final_gain"])
        barrier()
        dump("x_2", resid[:, :, :])

        arena.at = 0
        fin_ = arena.get(NT, D)
        t = norm_rows(resid, fin_)
        t_end = ve.tt(fin_, fin_, tail[:, 0:D].unsqueeze(1).to_broadcast([P, NT, D]), ALU.mult, t, t_final)

        s_out = sem("stored")

        block = ctx.enter_context(nc.Block())

        @block.sync
        def _(eng):
            for step in sp.steps:
                step(eng)
            eng.wait_ge(*t_end)
            eng.dma_start(out.rearrange("a (t p) d -> p (a t) d", p=P), fin_).then_inc(s_out, 16)
            eng.wait_ge(s_out, 16)

        @block.gpsimd
        def _(eng):
            for step in gp.steps:
                step(eng)

        @block.scalar
        def _(eng):
            for dst, src, sm, late in small_loads:
                if not late:
                    eng.dma_start(dst, src).then_inc(sm, 16)
            for step in ac.steps:
                step(eng)

        @block.tensor
        def _(eng):
            for step in pe.steps:
                step(eng)

        @block.vector
        def _(eng):
            for step in ve.steps:
                step(eng)
    print("arena top", arena.top, "semaphores ok; counts", [(l.name, l.count) for l in lines], "loads", len(loads))




def columns(v):
    return np.asarray(v).reshape(-1, P).T


def rows_(v):
    v = np.asarray(v).reshape(1, -1)
    return np.broadcast_to(v, (P, v.shape[1]))


def chunk(w):
    k = w.shape[0] // P
    return w.reshape(k, P, w.shape[1]).transpose(1, 0, 2).reshape(P, -1)


def lay_constants():
    p = np.arange(P)
    j, t = p[:, None], p[None, :]
    f = {}
    f["ident"] = (j == t)
    f["ones"] = np.ones((P, P))
    f["before"] = (j < t)
    f["upto"] = (j <= t)
    f["iota"] = np.broadcast_to(p[None, :], (P, P))
    f["levels"] = np.concatenate([((t // (2 * s) == j // (2 * s)) & (t // s % 2 == 1) & (j // s % 2 == 0))
                                  for s in (1, 2, 4, 8, 16, 32, 64)], axis=1)
    f["pair"] = (j // 64 == t // 64)
    f["causal01"] = (t <= j)
    f["causal_add"] = np.where(t <= j, 0.0, NEG)
    tok = np.arange(S).reshape(NT, P)
    end = np.arange(15) * 16 + 31
    f["cmp_add"] = np.where(end[None, None, :] <= tok[:, :, None], 0.0, NEG).transpose(1, 0, 2).reshape(P, 30)
    f["cmp_any"] = (tok >= 31).T
    f["group_rank"] = np.broadcast_to(np.array([4.0, 3.0, 2.0, 1.0]), (P, 4))
    f["pool_inv"] = np.broadcast_to(
        np.concatenate([1.0 / np.minimum(np.arange(16) + 1, w) for w in (2, 4, 8, 16)]), (P, 64))
    return np.concatenate([f[n].astype(np.float32).reshape(P, -1) for n, _ in CONSTS], axis=1)


def lay(entries, f):
    for n, w in entries:
        assert f[n].shape == (P, w), (n, f[n].shape, w)
    return np.ascontiguousarray(np.concatenate([f[n] for n, _ in entries], axis=1))


def block_diagonal(w):
    z = np.zeros_like(w[..., 0, :, :])
    return np.concatenate([np.concatenate([w[..., 0, :, :], z], -1), np.concatenate([z, w[..., 1, :, :]], -1)], -2)


def arrange(i):
    f = {k: np.asarray(v) for k, v in i.items()}
    o = {"consts": lay_constants(), "x": f["x"][0], "mem": f["mem"][0]}
    pos = f["positions"][0].astype(np.int32)
    o["pos_cols"] = np.ascontiguousarray(pos.reshape(NT, P).T)
    o["pos_rows"] = np.ascontiguousarray(np.broadcast_to(pos[None, :], (P, S)))
    twice = lambda v: np.concatenate([v, v]).reshape(P, 1)

    def router(g, e, bg, be):
        w = np.concatenate([g[0], e[0]], axis=1)
        return chunk(w), rows_(np.concatenate([bg[0], be[0]]))

    r1, rb1 = router(f["w_group_router"], f["w_expert_router"], f["b_group_router"], f["b_expert_router"])
    r2, rb2 = router(f["router_w_group_2"], f["router_w_expert_2"], f["router_b_group_2"], f["router_b_expert_2"])
    p1 = {
        "attn_norm": columns(f["attn_norm"]), "da_q": columns(f["da_q_norm"]), "da_k": columns(f["da_k_norm"]),
        "lam": rows_(np.concatenate([f["da_lambda_q1"][0], f["da_lambda_q2"][0], f["da_lambda_k1"][0],
                                     f["da_lambda_k2"][0]])),
        "subln": columns(f["da_subln"]), "mu": columns(f["rw_mu"]), "w0": columns(f["rw_w0"]),
        "a0": columns(f["rw_a0"]), "w2a2": np.concatenate([f["rw_w2"][0], f["rw_a2"][0]], axis=0),
        "g2": f["rw_g2"][0], "k_k": columns(f["rw_k_k"]), "k_a": columns(f["rw_k_a"]),
        "r_k": columns(f["rw_r_k"]), "gn_w": columns(f["rw_gn_w"]), "gn_b": columns(f["rw_gn_b"]),
        "mem_norm": columns(f["mem_norm"]), "mem_q": twice(f["mem_q_norm"][0]), "mem_k": twice(f["mem_k_norm"][0]),
        "ffn_norm": columns(f["ffn_norm"]), "router": r1, "router_b": rb1, "norm2": columns(f["norm2_g_2"]),
        "router_2": r2, "router_b_2": rb2,
    }
    o["params1"] = lay(PARAMS1, p1)
    w_in = f["w_in"][0]
    o["w_in_a"] = np.stack([chunk(w_in[:, a:a + 512]) for a in range(0, 2560, 512)])
    o["w_in_q"] = chunk(w_in[:, 2560:2816])
    o["w_mem_kv"] = chunk(f["w_mem_kv"][0])
    o["w_out"] = np.stack([chunk(f["w_out"][0][:, a:a + 512]) for a in (0, 512)])
    w2 = f["w_in_2"][0]
    cuts = {"u": 0, "v": 512, "gate": 1024, "rec": 1536, "q": 2048, "kv": 2560, "g": 3328, "xd": 3352, "mg": 3864}
    kinds = [w2[:, 2560 + 128 * c:2688 + 128 * c] for c in range(6)]
    wq = w2[:, 2048:2560].reshape(D, 2, 4, 64).transpose(0, 2, 1, 3).reshape(D, 512)
    o["w_kv_2"] = chunk(np.concatenate([kinds[0], kinds[1], kinds[2], kinds[4]], axis=1))
    o["w_vg_2"] = chunk(np.concatenate([kinds[3], kinds[5], w2[:, 3328:3352]], axis=1))
    o["w_in_2"] = np.stack([chunk(w) for w in (w2[:, 0:512], w2[:, 512:1024], w2[:, 1024:1536], w2[:, 1536:2048], wq,
                                               w2[:, cuts["xd"]:cuts["mg"]])])
    o["w_mg"] = np.stack([np.stack([chunk(w2[:, a:a + 512]) for a in (cuts["mg"] + n * D, cuts["mg"] + n * D + 512)])
                          for n in range(4)])
    wb = f["w_branch_2"][0]
    wb = np.stack([wb[0], wb[1], wb[2].reshape(2, 4, 64, D).transpose(1, 0, 2, 3).reshape(512, D), wb[3]])
    o["w_branch"] = np.stack([chunk(w) for w in wb])
    o["w_out_2"] = np.stack([chunk(f["w_out_2"][0][:, a:a + 512]) for a in (0, 512)])
    w1 = f["cmp_w1_2"][0].reshape(2, 2, 32, 64, 64).transpose(0, 2, 1, 3, 4)
    o["w_cmp1"] = block_diagonal(w1).transpose(0, 2, 1, 3).reshape(2, P, SLOT)

    def tiles(w):
        return w.transpose(1, 0, 2).reshape(P, -1)

    pe_ = f["cmp_pe_2"][0].transpose(2, 0, 1).reshape(64, 64)
    p2 = {
        "norm1": columns(f["norm1_g_2"]), "gm_norm": columns(f["gm_norm_g_2"]),
        "gm_wsT": f["gm_ws_2"][0].transpose(2, 0, 1).reshape(P, 512), "gm_b": rows_(f["gm_b_2"][0]),
        "conv_w": np.concatenate([columns(f["conv_w_2"][0][k]) for k in range(4)], axis=1),
        "conv_b": columns(f["conv_b_2"]),
        "lru_wa": tiles(block_diagonal(f["lru_wa_2"][0].reshape(4, 2, 64, 64))),
        "lru_wx": tiles(block_diagonal(f["lru_wx_2"][0].reshape(4, 2, 64, 64))),
        "lru_ba": columns(f["lru_ba_2"]), "lru_bx": columns(f["lru_bx_2"]), "lru_lam": columns(f["lru_lambda_2"]),
        "cmp_pe": np.concatenate([pe_, pe_], axis=0), "cmp_w2": tiles(block_diagonal(f["cmp_w2_2"][0])),
        "pool_w": tiles(f["pool_w_2"][0]), "pool_scale": columns(f["pool_scale_2"]),
    }
    o["params2"] = lay(PARAMS2, p2)
    o["final_gain"] = rows_(f["final_norm_g_2"])
    for tag, (g, u, d) in {"1": ("w_e_gate", "w_e_up", "w_e_down"),
                           "2": ("moe_w_gate_2", "moe_w_up_2", "moe_w_down_2")}.items():
        gu = np.stack([f[g][0], f[u][0]], axis=1)
        o["w_gu_" + tag] = np.ascontiguousarray(
            gu.reshape(16, 2, KD, P, 512).transpose(0, 1, 3, 2, 4)).reshape(16, 2, P, SLOT)
        o["w_dn_" + tag] = np.ascontiguousarray(
            f[d][0].reshape(16, 4, P, D).transpose(0, 2, 1, 3)).reshape(16, P, SLOT)
    return {k: np.ascontiguousarray(v) for k, v in o.items()}


def program(nc, arrays, debug=None):
    ins = {n: nc.dram_tensor("in_" + n, a.shape, mybir.dt.from_np(a.dtype), kind="ExternalInput").ap()
           for n, a in arrays.items()}
    out = nc.dram_tensor("out_0", (1, S, D), F32, kind="ExternalOutput").ap()
    build(nc, ins, out, debug)


def kernel(**inputs):
    import concourse.bacc as _bacc
    from concourse.bass_utils import run_bass_kernel_spmd as _run

    arrays = arrange(inputs)
    nc = _bacc.Bacc("TRN2", target_bir_lowering=False, num_devices=1)
    program(nc, arrays)
    r = _run(nc, [{"in_" + n: a for n, a in arrays.items()}], core_ids=[0])
    return r.results[0]["out_0"]
```

```python
from contextlib import ExitStack

import numpy as np

import concourse.bass as bass
from concourse import mybir

F32 = mybir.dt.float32
I32 = mybir.dt.int32
F32R = mybir.dt.float32r
ALU = mybir.AluOpType
ACT = mybir.ActivationFunctionType
AXX = mybir.AxisListType.X

P = 128
S = 256
NT = S // P
D = 1024
KD = D // P
EPS = 1e-6
NEG = -1e30
SLOT = 4096
NSLOT = 3
NSPLIT = 3
HALF = SLOT // 2
CAP = 128
MORE_ABOVE = CAP

CONSTS = [("ident", 128), ("ones", 128), ("before", 128), ("upto", 128), ("iota", 128),
          ("levels", 7 * 128), ("pair", 128), ("causal01", 128), ("causal_add", 128),
          ("cmp_add", 30), ("cmp_any", 2), ("group_rank", 4), ("pool_inv", 64)]
PARAMS1 = [("attn_norm", 8), ("da_q", 1), ("da_k", 1), ("lam", 256), ("subln", 1), ("mu", 8), ("w0", 2),
           ("a0", 2), ("w2a2", 256), ("g2", 256), ("k_k", 2), ("k_a", 2), ("r_k", 2), ("gn_w", 2),
           ("gn_b", 2), ("mem_norm", 8), ("mem_q", 1), ("mem_k", 1), ("ffn_norm", 8), ("router", 160),
           ("router_b", 20), ("norm2", 8), ("router_2", 160), ("router_b_2", 20)]
PARAMS2 = [("norm1", 8), ("gm_norm", 4), ("gm_wsT", 512), ("gm_b", 512), ("conv_w", 16), ("conv_b", 4),
           ("lru_wa", 512), ("lru_wx", 512), ("lru_ba", 4), ("lru_bx", 4), ("lru_lam", 4), ("cmp_pe", 64),
           ("cmp_w2", 256), ("pool_w", 512), ("pool_scale", 4)]


def places(entries):
    at, out = 0, {}
    for name, n in entries:
        out[name] = (at, n)
        at += n
    return out, at


class Line:

    def __init__(self, name, sem):
        self.name, self.sem, self.count = name, sem, 0
        self.outside = None
        self.steps, self.waited = [], {}

    def wait(self, *tokens):
        for t in tokens:
            if t is None:
                continue
            if isinstance(t, list):
                self.wait(*t)
                continue
            sem, value = t
            assert value > 0
            if self.waited.get(id(sem), 0) < value:
                self.waited[id(sem)] = value
                self.steps.append(lambda e, sem=sem, value=value: e.wait_ge(sem, value))

    def do(self, emit, *after, signal=True):
        self.wait(*after)
        if not signal:
            self.steps.append(emit)
            return None
        self.count += 1
        sem = self.sem
        self.steps.append(lambda e: emit(e).then_inc(sem, 1))
        return (sem, self.count)

    @property
    def last(self):
        return (self.sem, self.count) if self.count else None

    def read(self, cell):
        got = []
        self.steps.append(lambda e: got.append(e.value_load(cell)))
        return got

    def enter(self, sem):
        self.outside = (self.sem, self.count, dict(self.waited), self.steps)
        self.sem, self.count, self.steps = sem, 0, []

    def leave(self, got, limit):
        inside = self.steps
        self.sem, self.count, self.waited, self.steps = self.outside

        def branch(e):
            with e.If(got[0] > limit):
                for step in inside:
                    step(e)

        self.steps.append(branch)

    def tt(self, out, a, b, op, *after):
        return self.do(lambda e: e.tensor_tensor(out, a, b, op), *after)

    def ts(self, out, a, s1, s2, op0, op1, *after):
        if s2 is None:
            return self.do(lambda e: e.tensor_scalar(out, a, s1, None, op0), *after)
        return self.do(lambda e: e.tensor_scalar(out, a, s1, s2, op0, op1), *after)

    def stt(self, out, a, s, b, op0, op1, *after):
        return self.do(lambda e: e.scalar_tensor_tensor(out=out, in0=a, scalar=s, in1=b, op0=op0, op1=op1), *after)

    def copy(self, out, a, *after):
        return self.do(lambda e: e.tensor_copy(out, a), *after)

    def reduce(self, out, a, op, *after):
        return self.do(lambda e: e.tensor_reduce(out, a, AXX, op), *after)

    def recip(self, out, a, *after):
        return self.do(lambda e: e.reciprocal(out, a), *after)

    def scan(self, out, a, b, *after):
        return self.do(lambda e: e.tensor_tensor_scan(out, a, b, 0.0, ALU.mult, ALU.add), *after)

    def max_of_sum(self, out, a, b, scale, top, *after):
        return self.do(lambda e: e.tensor_tensor_reduce(out=out, in0=a, in1=b, scale=scale, scalar=-3e38,
                                                        op0=ALU.add, op1=ALU.max, accum_out=top), *after)

    def memset(self, out, value, *after):
        return self.do(lambda e: e.memset(out, value), *after)

    def act(self, out, a, func, *after, bias=0.0, scale=1.0, accum=None):
        if accum is not None:
            return self.do(lambda e: e.activation(out, a, func, bias=bias, scale=scale, accum_out=accum), *after)
        return self.do(lambda e: e.activation(out, a, func, bias=bias, scale=scale), *after)

    def mm(self, out, lhsT, rhs, start, stop, *after, signal=False):
        return self.do(lambda e: e.matmul(out, lhsT, rhs, start=start, stop=stop), *after, signal=signal)

    def turn(self, out, a, ident, *after, signal=False):
        n = a.shape[0]
        return self.do(lambda e: e.transpose(out, a, ident[0:n, 0:n]), *after, signal=signal)


class Bank:

    def __init__(self, ap):
        self.ap, self.free, self.taken = ap, [], False


class Banks:

    def __init__(self, aps):
        self.banks, self.at = [Bank(a) for a in aps], 0

    def take(self):
        while True:
            free = [k for k in range(self.at, self.at + len(self.banks)) if not self.banks[k % len(self.banks)].taken]
            if free:
                break
            yield
        b = self.banks[free[0] % len(self.banks)]
        self.at = free[0] + 1
        b.taken = True
        return b

    @staticmethod
    def give(bank, *tokens):
        bank.free, bank.taken = list(tokens), False


class Load:

    def __init__(self, src, slot, sem, value):
        self.src, self.slot, self.sem, self.ready, self.used = src, slot, sem, (sem, value), None


class Arena:

    def __init__(self, ap, size):
        self.ap, self.size, self.at, self.top = ap, size, 0, 0

    def get(self, *dims):
        n = int(np.prod(dims))
        a = self.ap[:, self.at:self.at + n]
        self.at += n
        self.top = max(self.top, self.at)
        assert self.at <= self.size, (self.at, self.size)
        if len(dims) == 2:
            a = a.rearrange("p (a b) -> p a b", a=dims[0])
        elif len(dims) == 3:
            a = a.rearrange("p (a b c) -> p a b c", a=dims[0], b=dims[1])
        return a


def weave(*gens):
    alive = list(gens)
    while alive:
        for g in list(alive):
            try:
                next(g)
            except StopIteration:
                alive.remove(g)
        yield


def run(gen):
    rounds = 0
    while True:
        rounds += 1
        assert rounds < 100000, "chains wait for each other"
        try:
            next(gen)
        except StopIteration as e:
            return e.value


def build(nc, ins, out, debug=None):
    ctx = ExitStack()
    with ctx:
        def sb(name, shape, dt=F32):
            return ctx.enter_context(nc.sbuf_tensor(name, shape, dt))

        def sem(name):
            return ctx.enter_context(nc.semaphore(name))

        pe, ve, ac, gp = (Line(n, sem("done_" + n)) for n in ("pe", "ve", "ac", "gp"))
        lines = (pe, ve, ac, gp)

        def barrier():
            marks = [l.last for l in lines]
            for l in lines:
                l.wait(*marks)

        banks_all = [ctx.enter_context(nc.psum_tensor(f"bank{i}", [P, 512], F32)) for i in range(8)]
        ring = sb("weight_ring", [P, NSLOT * SLOT])
        slot_sems = [sem(f"slot{i}") for i in range(NSLOT)]
        cpos, clen = places(CONSTS)
        ppos, plen = places(PARAMS1)
        qpos, qlen = places(PARAMS2)
        consts, params = sb("consts", [P, clen]), sb("params", [P, plen])
        resid = sb("resid", [P, NT, D])
        late = sb("late_params", [P, max(qlen, D)])
        tail = late[:, :]

        def C(name, a=0, b=None):
            at, n = cpos[name]
            return consts[:, at + a:at + (n if b is None else b)]

        def PM(name, a=0, b=None):
            at, n = ppos[name]
            return params[:, at + a:at + (n if b is None else b)]

        def PP(name, a=0, b=None):
            at, n = qpos[name]
            return tail[:, at + a:at + (n if b is None else b)]

        ident = C("ident")

        sp = Line("sp", None)
        loads = []
        sems_now = [slot_sems]

        def load(src):
            i, turn = len(loads) % NSLOT, len(loads) // NSLOT + 1
            h = Load(src, ring[:, i * SLOT:i * SLOT + src.shape[1]], sems_now[0][i], 16 * turn)
            h.before = loads[-NSLOT] if len(loads) >= NSLOT else None
            loads.append(h)

            def issue(e):
                if h.before is not None:
                    for sm, value in h.before.used:
                        e.wait_ge(sm, value)
                e.dma_start(h.slot, h.src).then_inc(h.sem, 16)

            sp.steps.append(issue)
            return h

        small_loads = []

        def fetch(dst, src, *after):
            s = sem(f"load{len(small_loads)}")
            small_loads.append((dst, src, s, bool(after)))
            if after:
                ac.wait(*after)
                ac.steps.append(lambda e: e.dma_start(dst, src).then_inc(s, 16))
            return (s, 16)

        dumps = []

        def dump(name, ap):
            if debug is not None and name in debug:
                barrier()
                t = [l.last for l in lines]
                n = int(np.prod(ap.shape[1:]))
                d = nc.dram_tensor("dbg_" + name, [ap.shape[0], n], F32, kind="ExternalOutput").ap()
                s = sem("dbg_" + name)
                dumps.append((name, n))
                v = ap
                if len(ap.shape) == 3:
                    d = d.rearrange("p (a b) -> p a b", a=ap.shape[1])
                elif len(ap.shape) == 4:
                    d = d.rearrange("p (a b c) -> p a b c", a=ap.shape[1], b=ap.shape[2])
                gp.wait(*t)
                gp.steps.append(lambda e: e.dma_start(d, v).then_inc(s, 16))
                for l in lines:
                    l.wait((s, 16))

        neg_half = sb("neg_half", [P, 32])
        gp.memset(neg_half[:, :], -0.5)
        t_neg = gp.last

        def rstd(dst, sums, count, eps, *after):
            a = ve.ts(sums, sums, 1.0 / count, eps, ALU.mult, ALU.add, *after)
            n = int(np.prod(sums.shape[1:]))
            half = neg_half[:, 0:n]
            if len(sums.shape) == 3:
                half = half.rearrange("p (a b) -> p a b", a=sums.shape[1])
            return gp.tt(dst, sums, half, ALU.pow, a, t_neg)

        pool8 = Banks([b[:, :] for b in banks_all])

        def norm_rows(src, dst, stat, *after):
            ss, rs = stat[:, 0:NT], stat[:, NT:2 * NT]
            t = None
            for i in range(NT):
                t = ac.act(dst[:, i, :], src[:, i, :], ACT.Square, *after, accum=ss[:, i:i + 1])
            r = rstd(rs, ss, D, EPS, t)
            for i in range(NT):
                t = ve.ts(dst[:, i, :], src[:, i, :], rs[:, i:i + 1], None, ALU.mult, None, r)
            return t

        def to_channels(src, dst, tiles, gain, *after, scale=1.0):
            t = None
            for k in range(0, tiles, 2):
                b = yield from pool8.take()
                w = min(2, tiles - k)
                for j in range(w):
                    for i in range(NT):
                        m = pe.turn(b.ap[:, (j * NT + i) * P:(j * NT + i + 1) * P],
                                    src[:, i, (k + j) * P:(k + j + 1) * P], ident, *after, b.free,
                                    signal=(j == w - 1 and i == NT - 1))
                yield
                for j in range(w):
                    o, a = dst[:, k + j, :], b.ap[:, j * S:(j + 1) * S]
                    if gain is None:
                        t = ve.ts(o, a, scale, None, ALU.mult, None, m)
                    else:
                        g = gain[:, k + j:k + j + 1] if gain.shape[1] > 1 else gain
                        t = ve.ts(o, a, g, scale, ALU.mult, ALU.mult, m)
                pool8.give(b, t)
            return t

        def project_tokens(hT, h, width, finish, *after, stride=512):
            w = h.slot.rearrange("p (k n) -> p k n", n=stride)
            for i in range(NT):
                b = yield from pool8.take()
                for k in range(w.shape[1]):
                    m = pe.mm(b.ap[:, 0:width], hT[:, k, i * P:(i + 1) * P], w[:, k, 0:width],
                              k == 0, k == w.shape[1] - 1, *after, h.ready, b.free,
                              signal=(k == w.shape[1] - 1))
                    if k % 2:
                        yield
                if i == NT - 1:
                    h.used = [m]
                pool8.give(b, *finish(i, b.ap[:, 0:width], m))

        def project_channels(hT, h, tiles, finish, *after, stride=512):
            w = h.slot.rearrange("p (k n) -> p k n", n=stride)
            for c in range(0, tiles, 2):
                b = yield from pool8.take()
                for j in range(2):
                    for k in range(w.shape[1]):
                        m = pe.mm(b.ap[:, j * S:(j + 1) * S], w[:, k, (c + j) * P:(c + j + 1) * P],
                                  hT[:, k, :], k == 0, k == w.shape[1] - 1, *after, h.ready, b.free,
                                  signal=(j == 1 and k == w.shape[1] - 1))
                        if k % 4 == 3:
                            yield
                if c + 2 == tiles:
                    h.used = [m]
                pool8.give(b, *finish(c, 2, b.ap.rearrange("p (j s) -> p j s", j=2), m))

        def head_norm(src, width, sq_flat, stat, *after):
            n = NT * width // 64
            sq = sq_flat[:, 0:NT * width].rearrange("p (h e) -> p h e", e=64)
            ss, rs = stat[:, 0:n], stat[:, n:2 * n]
            v = src.rearrange("p a (h e) -> p (a h) e", e=64)
            a = ac.act(sq, v, ACT.Square, *after, ve.last)
            yield
            a = ve.reduce(ss, sq, ALU.add, a)
            r = rstd(rs, ss, 64, EPS, a)
            yield
            return ve.tt(v, v, rs.unsqueeze(2).to_broadcast([P, n, 64]), ALU.mult, r)

        def into(dst):
            def fin(i, ps, m):
                return (ac.act(dst[:, i, :], ps, ACT.Copy, m),)
            return fin

        class Turner:

            def __init__(self, tiles):
                self.tiles, self.free, self.n = tiles, [None] * len(tiles), 0

            def turn(self, p, n, t):
                s = self.n % len(self.tiles)
                self.n += 1
                b = yield from pool8.take()
                w = (n + P - 1) // P
                for j in range(w):
                    m = pe.turn(b.ap[0:min(P, n - j * P), j * P:(j + 1) * P], p[:, j * P:min(n, (j + 1) * P)],
                                ident, t, b.free, signal=(j == w - 1))
                yield
                k = min(P, n)
                dst = self.tiles[s]
                a = ac.act(dst[0:k, 0:w, :], b.ap[0:k, 0:w * P].rearrange("p (j q) -> p j q", j=w), ACT.Copy, m,
                           self.free[s])
                pool8.give(b, a)
                return dst, s, a

        phase_stack = ExitStack()

        def open_arena(name, size):
            return Arena(phase_stack.enter_context(nc.sbuf_tensor(name, [P, size], F32)), size)

        arena = open_arena("mixers_1", 31000)
        tok = {}

        def have(name):
            while name not in tok:
                yield
            return tok[name]

        mixT = arena.get(KD, S)
        rw_flat = arena.get(8 * (S + 1))
        rw = rw_flat.rearrange("p (a b) -> p a b", a=8)
        qT, kT = arena.get(4, S), arena.get(4, S)
        v_da = arena.get(NT, 512)
        mkT, qmT, mv = arena.get(2, S), arena.get(2, S), arena.get(NT, 256)
        mem = arena.get(NT, D)
        memn, memT = arena.get(NT, D), arena.get(KD, S)
        hn, hT = memn, memT
        hn8 = memn.rearrange("p a b -> p (a b)").rearrange("p (a b) -> p a b", a=8)
        sq_flat = arena.get(NT * 512)
        q_da = arena.get(NT, 512)
        mk = q_da.rearrange("p a b -> p (a b)")[:, 0:512].rearrange("p (a b) -> p a b", a=NT)
        q_mem = arena.get(NT, 256)
        k_da = mem[:, 0, :].rearrange("p (a b) -> p a b", a=NT)
        nstat = arena.get(4 * NT + 64)

        t_mem = fetch(mem, ins["mem"].rearrange("(t p) d -> p t d", p=P))
        t_consts = fetch(consts[:, :], ins["consts"])
        t_params = fetch(params[:, :], ins["params1"])
        t_resid = fetch(resid[:, :, :], ins["x"].rearrange("(t p) d -> p t d", p=P))
        pos_q, pos_k = arena.get(NT).bitcast(I32), arena.get(S).bitcast(I32)
        t_pos = [fetch(pos_q, ins["pos_cols"]), fetch(pos_k, ins["pos_rows"])]

        def project_1():
            t = norm_rows(mem, memn, nstat[:, 0:4], t_mem)
            t = yield from to_channels(memn, memT, KD, PM("mem_norm"), t, t_params, t_consts)
            h = load(ins["w_mem_kv"])

            def fin_kv(i, ps, m):
                a = ac.act(mk[:, i, :], ps[:, 0:256], ACT.Copy, m)
                return (ac.act(mv[:, i, :], ps[:, 256:512], ACT.Copy, m),)

            yield from project_tokens(memT, h, 512, fin_kv, t)
            tok["mv"] = ac.last
            t_kv = h.used
            t = yield from head_norm(mk, 256, sq_flat, nstat[:, 4:], ac.last)
            tok["mkT"] = yield from to_channels(mk, mkT, 2, PM("mem_k"), t)
            t = norm_rows(resid, hn, nstat[:, 0:4], t_resid, t_kv[0])
            t_hT = yield from to_channels(hn, hT, KD, PM("attn_norm"), t)
            tok["z"] = ve.memset(rw[:, :, 0:1], 0.0)
            for j in range(2):
                h = load(ins["w_in_a"][3 + j])

                def fin_rw(c, n, ps, m, j=j):
                    return (ac.act(rw[:, 4 * j + c:4 * j + c + n, 1:S + 1], ps, ACT.Copy, m),)

                yield from project_channels(hT, h, 4, fin_rw, t_hT)
            tok["rw"] = ac.last
            h = load(ins["w_in_q"])
            yield from project_tokens(hT, h, 256, into(q_mem), stride=256)
            t = yield from head_norm(q_mem, 256, sq_flat, nstat[:, 4:], ac.last)
            tok["qmT"] = yield from to_channels(q_mem, qmT, 2, PM("mem_q"), t)
            h = load(ins["w_in_a"][0])
            yield from project_tokens(hT, h, 512, into(q_da))
            t = yield from head_norm(q_da, 512, sq_flat, nstat[:, 4:], ac.last)
            tok["qT"] = yield from to_channels(q_da, qT, 4, PM("da_q"), t, scale=64 ** -0.5)
            h = load(ins["w_in_a"][1])
            yield from project_tokens(hT, h, 512, into(k_da))
            t = yield from head_norm(k_da, 512, sq_flat, nstat[:, 4:], ac.last)
            tok["kT"] = yield from to_channels(k_da, kT, 4, PM("da_k"), t)
            h = load(ins["w_in_a"][2])
            yield from project_tokens(hT, h, 512, into(v_da))
            tok["v"] = ac.last
            tok["projected"] = pe.last

        def memory_attention(pair, r2, st, turner):
            t_qmT = yield from have("qmT")
            t_mkT, t_mv = tok["mkT"], tok["mv"]
            ob = yield from pool8.take()
            for half in range(2):
                hd = 2 * pair + half
                rr = slice(64 * half, 64 * half + 64)
                for i in range(NT):
                    p = r2[:, i, :]
                    b = yield from pool8.take()
                    m = pe.mm(b.ap[:, 0:S], qmT[rr, pair, i * P:(i + 1) * P], mkT[rr, pair, :], True, True,
                              t_qmT, t_mkT, b.free, signal=True)
                    yield
                    a = ve.ts(p, b.ap[:, 0:S], 64 ** -0.5, None, ALU.mult, None, m)
                    pool8.give(b, a)
                    a = ve.reduce(st[:, 0:1], p, ALU.max, a)
                    a = ve.ts(st[:, 1:2], st[:, 0:1], -1.0, None, ALU.mult, None, a)
                    yield
                    a = ac.act(p, p, ACT.Exp, a, bias=st[:, 1:2], accum=st[:, 2:3])
                    yield
                    a = ve.recip(st[:, 3:4], st[:, 2:3], a)
                    a = ve.ts(p, p, st[:, 3:4], None, ALU.mult, None, a)
                    yield
                    pT, s, a = yield from turner.turn(p, S, a)
                    yield
                    for j in range(2):
                        m = pe.mm(ob.ap[rr, i * P:(i + 1) * P], mv[:, j, 64 * hd:64 * hd + 64], pT[:, j, :],
                                  j == 0, j == 1, a, t_mv, ob.free, signal=(j == 1))
                    turner.free[s] = m
            a = ve.copy(mixT[:, 6 + pair, :], ob.ap[:, 0:S], m)
            pool8.give(ob, a)
            tok["o_mem"] = a

        lam_prod, lam_s = arena.get(2, 64), arena.get(8)
        dist = arena.get(NT, S)
        dist_i = dist.bitcast(I32)
        neg_lam = lam_s[:, 5:6]

        def attention_setup():
            lv = PM("lam").rearrange("p (a b) -> p a b", a=4)
            a = ve.tt(lam_prod, lv[:, 0:2, :], lv[:, 2:4, :], ALU.mult, t_params)
            a = ve.reduce(lam_s[:, 0:2], lam_prod, ALU.add, a)
            yield
            a = ac.act(lam_s[:, 2:4], lam_s[:, 0:2], ACT.Exp, a)
            yield
            a = ve.tt(lam_s[:, 4:5], lam_s[:, 3:4], lam_s[:, 2:3], ALU.subtract, a)
            tok["lam"] = ve.ts(neg_lam, lam_s[:, 4:5], -0.2, None, ALU.add, None, a)
            for i in range(NT):
                g = gp.tt(dist_i[:, i, :], pos_q[:, i:i + 1].to_broadcast([P, S]), pos_k, ALU.subtract, t_pos)
            yield
            tok["dist"] = ve.copy(dist, dist_i, g)

        o_da = q_da

        def diff_attention(heads, bias_h, r, st, turner):
            t_qT = yield from have("qT")
            t_kT = yield from have("kT")
            t_v = yield from have("v")
            last_use = None
            for hd in heads:
                slope = 2.0 ** (-8.0 * (hd + 1) / 4)
                a = ve.ts(bias_h, dist, -slope, None, ALU.mult, None, tok["dist"], last_use)
                for i in range(NT):
                    dg = bias_h[:, i, i * P:(i + 1) * P]
                    a = ve.tt(dg, dg, C("causal01"), ALU.mult, a)
                    a = ve.tt(dg, dg, C("causal_add"), ALU.add, a)
                t_bias = a
                yield
                for i in range(NT):
                    n = (i + 1) * P
                    for mp in range(2):
                        rr = slice(64 * mp, 64 * mp + 64)
                        b = yield from pool8.take()
                        m = pe.mm(b.ap[:, 0:n], qT[rr, hd, i * P:(i + 1) * P], kT[rr, hd, 0:n], True, True,
                                  t_qT, t_kT, b.free, signal=True)
                        yield
                        a = ve.max_of_sum(r[:, mp, 0:n], b.ap[:, 0:n], bias_h[:, i, 0:n], 1.0, st[:, mp:mp + 1],
                                          m, t_bias)
                        last_use = a
                        pool8.give(b, a)
                        a = ve.ts(st[:, 2 + mp:3 + mp], st[:, mp:mp + 1], -1.0, None, ALU.mult, None, a)
                        yield
                        a = ac.act(r[:, mp, 0:n], r[:, mp, 0:n], ACT.Exp, a, bias=st[:, 2 + mp:3 + mp],
                                   accum=st[:, 4 + mp:5 + mp])
                    yield
                    a = ve.recip(st[:, 6:8], st[:, 4:6], a)
                    a1 = ve.ts(r[:, 1, 0:n], r[:, 1, 0:n], st[:, 7:8], neg_lam, ALU.mult, ALU.mult, a, tok["lam"])
                    a = ve.stt(r[:, 0, 0:n], r[:, 0, 0:n], st[:, 6:7], r[:, 1, 0:n], ALU.mult, ALU.add, a1)
                    yield
                    pT, s, a = yield from turner.turn(r[:, 0, :], n, a)
                    yield
                    ob = yield from pool8.take()
                    for j in range(i + 1):
                        m = pe.mm(ob.ap[:, 0:P], pT[:, j, :], v_da[:, j, hd * P:(hd + 1) * P], j == 0, j == i,
                                  a, t_v, ob.free, signal=(j == i))
                    turner.free[s] = m
                    yield
                    t_o = ve.copy(o_da[:, i, hd * P:(hd + 1) * P], ob.ap[:, 0:P], m)
                    pool8.give(ob, t_o)
            tok[f"da{heads[-1]}"] = t_o

        def diff_attention_end():
            yield from have("da1")
            t_o = yield from have("da3")
            ss, rs = nstat[:, 0:8], nstat[:, 8:16]
            ov = o_da.rearrange("p a (h e) -> p (a h) e", e=P)
            sqv = sq_flat.rearrange("p (h e) -> p h e", e=P)
            a = ac.act(sqv, ov, ACT.Square, ve.last)
            yield
            a = ve.reduce(ss, sqv, ALU.add, a)
            a = rstd(rs, ss, P, EPS, a)
            yield
            a = ve.tt(ov, ov, rs.unsqueeze(2).to_broadcast([P, NT * 4, P]), ALU.mult, a)
            tok["o_da"] = yield from to_channels(o_da, mixT[:, 0:4, :], 4, PM("subln"), a, scale=0.8)

        def rwkv():
            t_rw = yield from have("rw")
            t_z = tok["z"]
            HP, L = 2, P
            cols_flat, diff_flat = arena.get(8 * S), arena.get(8 * S)
            cols, diff = (x.rearrange("p (a b) -> p a b", a=8) for x in (cols_flat, diff_flat))
            a = ve.tt(diff, rw[:, :, 0:S], rw[:, :, 1:S + 1], ALU.subtract, t_rw, t_z)
            for c in range(8):
                t_cols = ve.stt(cols[:, c, :], diff[:, c, :], PM("mu", c, c + 1), rw[:, c, 1:S + 1],
                                ALU.mult, ALU.add, a)
                if c % 3 == 2:
                    yield
            r_, k_, v_, xwa, xg = cols[:, 0:2, :], cols[:, 2:4, :], cols[:, 4:6, :], cols[:, 6, :], cols[:, 7, :]
            kk, ld, aa, tmp = diff[:, 0:2, :], diff[:, 2:4, :], diff[:, 4:6, :], diff[:, 6:8, :]
            lora = arena.get(S)
            sg = arena.get(S)
            half_b = arena.get(4)
            gate = arena.get(2, S)
            a1 = ac.act(lora[0:64, :], xwa[0:64, :], ACT.Tanh, t_cols)
            a2 = ac.act(lora[64:128, :], xwa[64:128, :], ACT.Copy, t_cols)
            a3 = ac.act(sg, xg, ACT.Tanh, t_cols, scale=0.5)
            h1 = ve.ts(half_b[:, 0:2], PM("w0"), 0.5, None, ALU.mult, None)
            h2 = ve.ts(half_b[:, 2:4], PM("a0"), 0.5, None, ALU.mult, None)
            a3 = ve.ts(sg, sg, 0.5, 0.5, ALU.mult, ALU.add, a3)
            bw = yield from pool8.take()
            ba_ = yield from pool8.take()
            bg = yield from pool8.take()
            for c in range(2):
                mw = pe.mm(bw.ap[:, c * S:(c + 1) * S], PM("w2a2", c * P, (c + 1) * P)[0:64, :], lora[0:64, :],
                           True, True, a1, bw.free, signal=True)
                ma = pe.mm(ba_.ap[:, c * S:(c + 1) * S], PM("w2a2", c * P, (c + 1) * P)[64:128, :], lora[64:128, :],
                           True, True, a2, ba_.free, signal=True)
                mg = pe.mm(bg.ap[:, c * S:(c + 1) * S], PM("g2", c * P, (c + 1) * P), sg, True, True, a3, bg.free,
                           signal=True)
            yield
            for c in range(2):
                aw = ac.act(ld[:, c, :], bw.ap[:, c * S:(c + 1) * S], ACT.Tanh, mw, h1, bias=half_b[:, c:c + 1], scale=0.5)
                a_a = ac.act(aa[:, c, :], ba_.ap[:, c * S:(c + 1) * S], ACT.Tanh, ma, h2, bias=half_b[:, 2 + c:3 + c],
                             scale=0.5)
            t_gate = ac.act(gate, bg.ap.rearrange("p (c s) -> p c s", c=2), ACT.Copy, mg)
            for b in (bw, ba_, bg):
                pool8.give(b, ac.last)
            yield
            e5 = 0.6065306597126334
            t_ld = ve.ts(ld, ld, -0.5 * e5, -0.5 * e5, ALU.mult, ALU.add, aw)
            t_aa = ve.ts(aa, aa, 0.5, 0.5, ALU.mult, ALU.add, a_a)
            for c in range(2):
                a = ve.ts(kk[:, c, :], k_[:, c, :], PM("k_k", c, c + 1), None, ALU.mult, None)
            a = ac.act(tmp, kk, ACT.Square, a)
            yield
            b = yield from pool8.take()
            m = pe.mm(b.ap, C("pair"), tmp.rearrange("p c s -> p (c s)"), True, True, a, b.free, signal=True)
            n2 = arena.get(2, S)
            n2f = n2.rearrange("p c s -> p (c s)")
            a = ve.ts(n2f, b.ap, 1e-24, None, ALU.max, None, m)
            pool8.give(b, a)
            yield
            a = ac.act(n2, n2, ACT.Sqrt, a)
            yield
            a = ve.recip(n2f, n2f, a)
            t_kk = ve.tt(kk, kk, n2, ALU.mult, a)
            kp = arena.get(2, S)
            for c in range(2):
                a = ve.ts(kp[:, c, :], aa[:, c, :], -1.0, PM("k_a", c, c + 1), ALU.add, ALU.mult, t_aa)
            t_kp = ve.stt(kp, kp, 1.0, k_, ALU.add, ALU.mult, a)
            yield
            bonus = arena.get(2, S)
            for c in range(2):
                a = ve.stt(tmp[:, c, :], r_[:, c, :], PM("r_k", c, c + 1), kp[:, c, :], ALU.mult, ALU.mult, t_kp, m)
            b = yield from pool8.take()
            m = pe.mm(b.ap, C("pair"), tmp.rearrange("p c s -> p (c s)"), True, True, a, b.free, signal=True)
            t_bonus = ve.tt(bonus, b.ap.rearrange("p (c s) -> p c s", c=2), v_, ALU.mult, m)
            pool8.give(b, t_bonus)
            yield
            cum = arena.get(4, L)
            ldv = ld.rearrange("p c (k l) -> p (c k) l", l=L)
            for c in range(4):
                a = ve.scan(cum[:, c, :], C("ones"), ldv[:, c, :], t_ld)
            yield
            mid = arena.get(4)
            a = ve.copy(mid, cum[:, :, L // 2 - 1], a)
            carry = arena.get(2)
            cv = cum.rearrange("p (c k) l -> p c k l", c=2)
            mv2 = mid.rearrange("p (c k) -> p c k", c=2)
            a = ve.tt(carry, cv[:, :, 0, L - 1], mv2[:, :, 0], ALU.subtract, a)
            a = ve.tt(carry, carry, mv2[:, :, 1], ALU.add, a)
            t_carry = ac.act(carry, carry, ACT.Exp, a)
            a = ve.tt(cum, cum, mid.unsqueeze(2).to_broadcast([P, 4, L]), ALU.subtract, a)
            prev = arena.get(4, L)
            a_prev = ve.tt(prev, cum, ldv, ALU.subtract, a)
            e_pos, e_neg = arena.get(4, L), n2.rearrange("p c (k l) -> p (c k) l", l=L)
            x1 = ac.act(e_pos, cum, ACT.Exp, a)
            x2 = ac.act(e_neg, cum, ACT.Exp, a, t_kk, scale=-1.0)
            x3 = ac.act(prev, prev, ACT.Exp, a_prev)

            yield

            def fl(x):
                return x.rearrange("p c (k l) -> p (c k) l", l=L)

            rho, alpha, beta, kappa = e_pos, prev, fl(aa), fl(kp)
            ve.tt(rho, fl(r_), e_pos, ALU.mult, x1)
            ve.tt(alpha, fl(kk), prev, ALU.mult, x3)
            a = ve.tt(aa, kk, aa, ALU.mult)
            ve.tt(beta, fl(aa), e_neg, ALU.mult, a, x2)
            t_ab = ve.tt(kappa, fl(kp), e_neg, ALU.mult)
            yield

            late_mem = mem[:, 1, :]
            vT, bT, kT0 = (late_mem[:, 0:512].rearrange("p (k c) -> p k c", k=2), late_mem[:, 512:768],
                           late_mem[:, 768:1024])
            b = yield from pool8.take()
            for c in range(2):
                for kx in range(2):
                    m = pe.turn(b.ap[:, kx * 256 + c * P:kx * 256 + (c + 1) * P], v_[:, c, kx * L:(kx + 1) * L], ident,
                                t_ab, b.free, signal=(c == 1 and kx == 1))
            t_vT = ac.act(vT, b.ap.rearrange("p (k c) -> p k c", k=2), ACT.Copy, m)
            pool8.give(b, t_vT)
            b = yield from pool8.take()
            for c in range(2):
                pe.turn(b.ap[:, c * P:(c + 1) * P], beta[:, 2 * c, :], ident, b.free)
                m = pe.turn(b.ap[:, 256 + c * P:256 + (c + 1) * P], kappa[:, 2 * c, :], ident, signal=True)
            ac.act(bT, b.ap[:, 0:256], ACT.Copy, m)
            t_bkT = ac.act(kT0, b.ap[:, 256:512], ACT.Copy, m)
            pool8.give(b, t_bkT)
            t_free = yield from have("projected")
            AT, BT, CT, DT = (x[:, k * 4:k * 4 + 4, :].rearrange("p a (b c) -> p (a b) c", c=P)
                              .rearrange("p (a b) c -> p a b c", a=2) for x, k in
                              ((hT, 0), (hT, 1), (hn8, 0), (hn8, 1)))
            TI, TT, X = (x.rearrange("p (a b c) -> p a b c", a=2, b=4)
                         for x in (diff_flat[:, 0:1024], diff_flat[:, 1024:2048], cols_flat[:, 0:1024]))

            def spread(m, n=4):
                return m.unsqueeze(1).to_broadcast([P, n, P])

            for dst, left, right, mask in ((AT, beta, alpha, "before"), (BT, kappa, alpha, "before"),
                                           (CT, beta, rho, "upto"), (DT, kappa, rho, "upto")):
                for half in range(2):
                    rr = slice(64 * half, 64 * half + 64)
                    b = yield from pool8.take()
                    for c in range(4):
                        m = pe.mm(b.ap[:, c * P:(c + 1) * P], left[rr, c, :], right[rr, c, :], True, True, t_ab, b.free,
                                  signal=(c == 3))
                    yield
                    a = ve.tt(dst[:, half, :, :], b.ap.rearrange("p (c l) -> p c l", c=4), spread(C(mask)), ALU.mult, m,
                              t_free)
                    pool8.give(b, a)
            t_grams = ve.last
            t_T = []
            for half in range(2):
                t_T.append([ac.act(TI[:, half, :, :], spread(ident), ACT.Copy, t_grams, m),
                            ve.copy(TT[:, half, :, :], spread(ident), t_grams, m)])
            level = [rw_flat[:, k * 512:(k + 1) * 512].rearrange("p (c l) -> p c l", c=4) for k in range(4)]

            def invert(half):
                level_free = [None, None]
                for lv_ in range(7):
                    msk = C("levels", lv_ * P, (lv_ + 1) * P)
                    block = level[half + 2 * (lv_ % 2)]
                    g = gp.tt(block, AT[:, half, :, :], spread(msk), ALU.mult, t_grams, level_free[lv_ % 2])
                    b = yield from pool8.take()
                    for c in range(4):
                        m = pe.mm(b.ap[:, c * P:(c + 1) * P], block[:, c, :], TI[:, half, c, :], True, True,
                                  g, t_T[half], b.free, signal=(c == 3))
                    level_free[lv_ % 2] = m
                    yield
                    a = ac.act(X[:, half, :, :], b.ap.rearrange("p (c l) -> p c l", c=4), ACT.Copy, m, t_T[half])
                    pool8.give(b, a)
                    yield
                    b2 = yield from pool8.take()
                    for c in range(4):
                        m2 = pe.mm(b2.ap[:, c * P:(c + 1) * P], X[:, half, c, :], TT[:, half, c, :], True, True, a,
                                   b2.free, signal=(c == 3))
                    n1 = m1 = None
                    if lv_ < 6:
                        b1 = yield from pool8.take()
                        for c in range(4):
                            m1 = pe.mm(b1.ap[:, c * P:(c + 1) * P], TT[:, half, c, :], X[:, half, c, :], True, True,
                                       a, b1.free, signal=(c == 3))
                        yield
                        n1 = ve.tt(TI[:, half, :, :], TI[:, half, :, :], b1.ap.rearrange("p (c l) -> p c l", c=4),
                                   ALU.subtract, m1, m2, t_T[half])
                        pool8.give(b1, n1)
                    n2_ = ve.tt(TT[:, half, :, :], TT[:, half, :, :], b2.ap.rearrange("p (c l) -> p c l", c=4),
                                ALU.subtract, m2, m1, t_T[half])
                    pool8.give(b2, n2_)
                    t_T[half] = [n1, n2_]
                    yield

            yield from weave(invert(0), invert(1))
            R, SA = (rw_flat[:, x:x + 512].rearrange("p (k c) -> p k c", k=2) for x in (1024, 1536))
            y = cols_flat[:, 1024:1536].rearrange("p (k c) -> p k c", k=2)
            state = cols_flat[:, 1536:1792].rearrange("p (c v) -> p c v", c=2)
            t_state = None
            for kx in range(2):
                b = yield from pool8.take()
                for pair in range(2):
                    c = 2 * pair + kx
                    if kx:
                        pe.mm(b.ap[:, pair * P:(pair + 1) * P], alpha[:, c, :], state[:, pair, :], True, False,
                              t_state, b.free)
                    for half in range(2):
                        hc = slice(pair * P + half * 64, pair * P + half * 64 + 64)
                        m = pe.mm(b.ap[:, hc], BT[:, half, c, :], vT[:, kx, hc], not kx, not kx or half == 1,
                                  t_vT, t_grams, b.free, signal=True)
                yield
                a = ve.ts(R[:, kx, :], b.ap[:, 0:256], -1.0, None, ALU.mult, None, m)
                pool8.give(b, a)
                b = yield from pool8.take()
                for pair in range(2):
                    c = 2 * pair + kx
                    for half in range(2):
                        hc = slice(pair * P + half * 64, pair * P + half * 64 + 64)
                        m = pe.mm(b.ap[:, hc], TT[:, half, c, :], R[:, kx, hc], True, True, a, t_T, b.free, signal=True)
                yield
                t_sa = ve.copy(SA[:, kx, :], b.ap[:, 0:256], m)
                pool8.give(b, t_sa)
                b = yield from pool8.take()
                for pair in range(2):
                    c = 2 * pair + kx
                    if kx:
                        pe.mm(b.ap[:, pair * P:(pair + 1) * P], rho[:, c, :], state[:, pair, :], True, False, b.free)
                    for half in range(2):
                        hc = slice(pair * P + half * 64, pair * P + half * 64 + 64)
                        pe.mm(b.ap[:, hc], CT[:, half, c, :], SA[:, kx, hc], not kx, False, t_sa, b.free)
                        m = pe.mm(b.ap[:, hc], DT[:, half, c, :], vT[:, kx, hc], False, not kx or half == 1, signal=True)
                yield
                t_y = ac.act(y[:, kx, :], b.ap[:, 0:256], ACT.Copy, m)
                pool8.give(b, t_y)
                if not kx:
                    b = yield from pool8.take()
                    for pair in range(2):
                        pc = slice(pair * P, (pair + 1) * P)
                        pe.mm(b.ap[:, pc], bT[:, pc], SA[:, 0, pc], True, False, t_bkT, b.free)
                        m = pe.mm(b.ap[:, pc], kT0[:, pc], vT[:, 0, pc], False, True, signal=True)
                    yield
                    for pair in range(2):
                        t_state = ve.stt(state[:, pair, :], b.ap[:, pair * P:(pair + 1) * P], carry[:, pair:pair + 1],
                                         C("pair"), ALU.mult, ALU.mult, m, t_carry)
                    pool8.give(b, t_state)
            yield
            ys = y.rearrange("p k (h e) -> p (k h) e", e=64)
            s1, s2, rs = arena.get(8), arena.get(8), arena.get(8)
            sq8 = R.rearrange("p k (h e) -> p (k h) e", e=64)
            a = ve.reduce(s1, ys, ALU.add, t_y)
            a = ve.ts(s1, s1, 1.0 / 64, None, ALU.mult, None, a)
            a = ve.tt(ys, ys, s1.unsqueeze(2).to_broadcast([P, 8, 64]), ALU.subtract, a)
            b = ac.act(sq8, ys, ACT.Square, a)
            b = ve.reduce(s2, sq8, ALU.add, b)
            yield
            a = rstd(rs, s2, 64, 64e-5, b)
            a = ve.tt(ys, ys, rs.unsqueeze(2).to_broadcast([P, 8, 64]), ALU.mult, a)
            yield
            b = yield from pool8.take()
            for c in range(2):
                for kx in range(2):
                    m = pe.turn(b.ap[:, c * S + kx * P:c * S + (kx + 1) * P], y[:, kx, c * P:(c + 1) * P], ident, a, b.free,
                                signal=True)
            for c in range(2):
                a = ve.ts(mixT[:, 4 + c, :], b.ap[:, c * S:(c + 1) * S], PM("gn_w", c, c + 1), PM("gn_b", c, c + 1),
                          ALU.mult, ALU.add, m)
            pool8.give(b, a)
            a = ve.tt(mixT[:, 4:6, :], mixT[:, 4:6, :], bonus, ALU.add, a)
            tok["o_rw"] = ve.tt(mixT[:, 4:6, :], mixT[:, 4:6, :], gate, ALU.mult, a, t_gate)

        def chain(*gens):
            for g in gens:
                yield from g

        chains = []
        for c in range(2):
            r2, st, turner = arena.get(2, 256), arena.get(8), Turner([arena.get(2, P) for _ in range(2)])
            chains.append(chain(memory_attention(c, r2, st, turner),
                                diff_attention((2 * c, 2 * c + 1), arena.get(NT, S), r2, st, turner)))
        run(weave(project_1(), attention_setup(), rwkv(), *chains, diff_attention_end()))
        t_mix = [tok["o_rw"], tok["o_da"], tok["o_mem"], ve.last]
        dump("mixT", mixT)

        def add_product(xT, src, *after):
            for j in range(2):
                h = load(src[j])

                def fin(i, ps, m, j=j):
                    r = resid[:, i, j * 512:(j + 1) * 512]
                    return (ve.tt(r, r, ps, ALU.add, m),)

                run(project_tokens(xT, h, 512, fin, *after))

        add_product(mixT, ins["w_out"], t_mix)
        dump("x_mid", resid[:, :, :])

        def moe(tag, gain, router, router_b, w_gu, w_dn, next_params):
            barrier()
            stack = ExitStack()

            def own(name, shape, dt):
                return stack.enter_context(nc.sbuf_tensor(name + tag, shape, dt))

            marks = [l.last for l in lines]
            t_next = fetch(tail[:, 0:next_params.shape[1]], next_params, *marks)
            size = 8700
            arena = Arena(own("experts", [P, size], F32), size)
            xn, xT = arena.get(NT, D), arena.get(KD, S)
            t = norm_rows(resid, xn, arena.get(4), ve.last)
            t_xn = t
            t_xT = run(to_channels(xn, xT, KD, gain, t))
            lg = arena.get(NT, 20)
            b = run(pool8.take())
            rt = router.rearrange("p (k n) -> p k n", k=KD)
            for i in range(NT):
                for k in range(KD):
                    m = pe.mm(b.ap[:, i * 20:(i + 1) * 20], xT[:, k, i * P:(i + 1) * P], rt[:, k, :], k == 0,
                              k == KD - 1, t_xT, b.free, signal=(k == KD - 1))
            a = ve.tt(lg, b.ap[:, 0:40].rearrange("p (i n) -> p i n", i=NT),
                      router_b.unsqueeze(1).to_broadcast([P, NT, 20]), ALU.add, m)
            pool8.give(b, a)
            dump("logits" + tag, lg)
            gl = lg[:, :, 0:4]
            el = lg[:, :, 4:20].rearrange("p i (g e) -> p i g e", g=4)
            rank4 = C("group_rank").unsqueeze(1).to_broadcast([P, NT, 4])

            def first_best(v, oh, mx, t):
                a = ve.reduce(mx, v, ALU.max, t)
                mb = mx.unsqueeze(2).to_broadcast([P, NT, 4])
                a = ve.tt(oh, v, mb, ALU.is_ge, a)
                a = ve.tt(oh, oh, rank4, ALU.mult, a)
                sc = arena.get(NT)
                a = ve.reduce(sc, oh, ALU.max, a)
                sbc = sc.unsqueeze(2).to_broadcast([P, NT, 4])
                return ve.tt(oh, rank4, sbc, ALU.is_equal, a)

            gmax, goh, gd = arena.get(NT), arena.get(NT, 4), arena.get(NT, 4)
            a = first_best(gl, goh, gmax, a)
            a = ve.tt(gd, gl, gmax.unsqueeze(2).to_broadcast([P, NT, 4]), ALU.subtract, a)
            b_ = ac.act(gd, gd, ACT.Exp, a)
            psel = arena.get(NT)
            a = ve.reduce(psel, gd, ALU.add, b_)
            a = ve.recip(psel, psel, a)
            em, ie = arena.get(NT * 4, 4), arena.get(NT, 4)
            emv = em.rearrange("p (i g) e -> p i g e", i=NT)
            for i in range(NT):
                a = ve.tt(em[:, 4 * i:4 * i + 4, :], el[:, i, :, :], goh[:, i, :].unsqueeze(2).to_broadcast([P, 4, 4]),
                          ALU.mult, a)
            for i in range(NT):
                a = ve.reduce(ie[:, i, :], em[:, 4 * i:4 * i + 4, :].rearrange("p g e -> p e g"), ALU.add, a)
            m1, m2, o1, o2 = arena.get(NT), arena.get(NT), arena.get(NT, 4), arena.get(NT, 4)
            a = first_best(ie, o1, m1, a)
            a = ve.stt(ie, o1, -1e30, ie, ALU.mult, ALU.add, a)
            a = first_best(ie, o2, m2, a)
            a = ve.tt(m2, m2, m1, ALU.subtract, a)
            b_ = ac.act(m2, m2, ACT.Exp, a)
            a = ve.ts(m1, m2, 1.0, None, ALU.add, None, b_)
            a = ve.recip(m1, m1, a)
            a = ve.tt(m1, m1, psel, ALU.mult, a)
            a = ve.tt(m2, m2, m1, ALU.mult, a)
            gates = arena.get(NT, 4)
            a = ve.tt(o1, o1, m1.unsqueeze(2).to_broadcast([P, NT, 4]), ALU.mult, a)
            a = ve.tt(o2, o2, m2.unsqueeze(2).to_broadcast([P, NT, 4]), ALU.mult, a)
            t_gates = ve.tt(gates, o1, o2, ALU.add, a)
            dump("gates" + tag, gates)
            b = run(pool8.take())
            for i in range(NT):
                if i:
                    pe.mm(b.ap[:, 4 * i:4 * i + 4], C("ones"), goh[:, 0, :], True, False, b.free, t_gates)
                m = pe.mm(b.ap[:, 4 * i:4 * i + 4], C("before"), goh[:, i, :], i == 0, True, b.free, t_gates,
                          signal=True)
            for i in range(NT):
                m = pe.mm(b.ap[:, 8:12], C("ones"), goh[:, i, :], i == 0, i == NT - 1, signal=(i == NT - 1))
            place = arena.get(NT, 4)
            counts = arena.get(4)
            top = arena.get(1)
            a = ve.stt(place, b.ap[:, 0:8].rearrange("p (i g) -> p i g", i=NT), 1.0, goh, ALU.add, ALU.mult, m)
            a = ve.ts(place, place, -1.0, None, ALU.add, None, a)
            t_place = a
            a = ve.reduce(top, b.ap[:, 8:12], ALU.max, a)
            pool8.give(b, a)
            top_i = arena.get(1).bitcast(I32)
            t_top = ve.copy(top_i, top, a)

            w_hi = [own(f"w_hi{k}", [P, HALF], F32R)[:, :] for k in range(NSPLIT)]
            w_lo = [own(f"w_lo{k}", [P, HALF], F32R)[:, :] for k in range(NSPLIT)]
            xg = [[own(f"xg_{p}{k}", [P, KD, CAP], F32R) for p in ("hi", "lo")] for k in range(2)]
            hidT = [[own(f"hidT_{p}{k}", [P, 4, CAP], F32R) for p in ("hi", "lo")] for k in range(2)]
            yg = [own(f"yg_{p}", [P, D], F32R) for p in ("hi", "lo")]
            selT = [own(f"selT{k}", [P, NT, P], F32R) for k in range(2)]
            sel = [arena.get(NT, CAP) for _ in range(2)]
            sgate = [arena.get(4) for _ in range(2)]
            th = [arena.get(512) for _ in range(2)]
            hid = [arena.get(512) for _ in range(2)]

            def f32(r):
                return r.bitcast(F32)

            def experts(first):
                gu_banks = Banks([x[:, :] for x in banks_all[0:4]])
                y_banks = [Bank(x[:, :]) for x in banks_all[4:6]]
                misc = Banks([x[:, :] for x in banks_all[6:8]])
                start = [l.last for l in lines]
                free = {}
                yg_free = [None]

                order = []
                for e in range(17):
                    if e < 16:
                        order += [(w_gu[e, 0], 0), (w_gu[e, 0], 1), (w_gu[e, 1], 0), (w_gu[e, 1], 1)]
                    if e:
                        order += [(w_dn[e - 1], 0), (w_dn[e - 1], 1)]
                split_done, used, at_load = [], [], [None]
                aside = []

                def step_aside():
                    for g in list(aside):
                        try:
                            next(g)
                        except StopIteration:
                            aside.remove(g)

                def finish_aside():
                    while aside:
                        step_aside()

                def split_next():
                    n = len(split_done)
                    if n == len(order):
                        return
                    src, half = order[n]
                    if half == 0:
                        at_load[0] = load(src)
                    h, s = at_load[0], n % NSPLIT
                    w = h.slot[:, half * HALF:(half + 1) * HALF]
                    before = used[n - NSPLIT] if n >= NSPLIT else None
                    a = ac.act(w_hi[s], w, ACT.Copy, h.ready, before)
                    v = ve.tt(w_lo[s], w, f32(w_hi[s]), ALU.subtract, a, h.ready, before)
                    if half == 1:
                        h.used = [a, v]
                    split_done.append([a, v])

                def product(outs, x, tiles, n_cols, first_mm, last_mm, *after):
                    n = len(used)
                    s = n % NSPLIT
                    split_next()
                    wh = w_hi[s].rearrange("p (k n) -> p k n", n=n_cols)
                    wl = w_lo[s].rearrange("p (k n) -> p k n", n=n_cols)
                    m = None
                    for k, tile in enumerate(tiles):
                        for j, o in enumerate(outs):
                            cols = slice(j * 512, (j + 1) * 512)
                            st, en = first_mm and k == 0, last_mm and k == len(tiles) - 1
                            pe.mm(o, x[0][:, tile, :], wl[:, k, cols], st, False, *after, split_done[n])
                            pe.mm(o, x[1][:, tile, :], wh[:, k, cols], False, False)
                            m = pe.mm(o, x[0][:, tile, :], wh[:, k, cols], False, en,
                                      signal=(k == len(tiles) - 1 and j == len(outs) - 1))
                    used.append(m)
                    step_aside()
                    return m

                def gather(g):
                    s = g % 2
                    for i in range(NT):
                        a = ve.ts(sel[s][:, i, :], C("iota"), float(first), place[:, i, g:g + 1], ALU.add,
                                  ALU.is_equal, t_place, start, free.get(("sel", s)))
                    t_sel = a
                    for kk_ in range(0, KD, 4):
                        b = yield from misc.take()
                        for k in range(kk_, kk_ + 4):
                            for i in range(NT):
                                m = pe.mm(b.ap[:, (k - kk_) * CAP:(k - kk_ + 1) * CAP], xn[:, i, k * P:(k + 1) * P],
                                          sel[s][:, i, :], i == 0, i == NT - 1, t_sel, t_xn, b.free, start,
                                          signal=(k == kk_ + 3 and i == NT - 1))
                            if k % 2:
                                yield
                        for k in range(kk_, kk_ + 4):
                            ps = b.ap[:, (k - kk_) * CAP:(k - kk_ + 1) * CAP]
                            a = ac.act(xg[s][0][:, k, :], ps, ACT.Copy, m, free.get(("xg", s)), scale=gain[:, k:k + 1])
                        for k in range(kk_, kk_ + 4):
                            ps = b.ap[:, (k - kk_) * CAP:(k - kk_ + 1) * CAP]
                            v = ve.stt(xg[s][1][:, k, :], ps, gain[:, k:k + 1], f32(xg[s][0][:, k, :]), ALU.mult,
                                       ALU.subtract, a)
                        misc.give(b, v)
                    t_xg = v
                    b = yield from misc.take()
                    for i in range(NT):
                        pe.turn(b.ap[:, i * P:(i + 1) * P], sel[s][:, i, :], ident, b.free)
                    for i in range(NT):
                        m = pe.mm(b.ap[:, 256:260], sel[s][:, i, :], gates[:, i, :], i == 0, i == NT - 1, t_gates,
                                  signal=(i == NT - 1))
                    yield
                    a = ve.copy(selT[s][:, :, :], b.ap[:, 0:256].rearrange("p (i q) -> p i q", i=NT), m,
                                free.get(("selT", s)))
                    a = ve.ts(sgate[s], b.ap[:, 256:260], 0.5, None, ALU.mult, None, m, free.get(("sgate", s)))
                    misc.give(b, a)
                    free[("sel", s)] = m
                    ready[g] = (t_xg, a)

                def gate_up(e, t_xg):
                    s = (e // 4) % 2
                    ps = []
                    for which in range(2):
                        b = run(gu_banks.take())
                        for half in range(2):
                            m = product([b.ap], xg[s], range(4 * half, 4 * half + 4), 512, half == 0, half == 1,
                                        t_xg, b.free, start)
                        ps.append((b, m))
                    free[("xg", s)] = m
                    return ps

                def hidden(e, ps, t_gate):
                    (bg_, mg_), (bu, mu_) = ps
                    s, u = (e // 4) % 2, e % 2
                    a = ac.act(th[u], bg_.ap, ACT.Tanh, mg_, start, free.get(("th", u)), scale=0.5)
                    a = ve.stt(th[u], th[u], 1.0, bg_.ap, ALU.add, ALU.mult, a)
                    gu_banks.give(bg_, a)
                    a = ve.stt(hid[u], th[u], sgate[s][:, e % 4:e % 4 + 1], bu.ap, ALU.mult, ALU.mult, a, mu_, t_gate,
                               free.get(("hid", u)))
                    gu_banks.give(bu, a)
                    free[("th", u)] = a
                    free[("sgate", s)] = a
                    return a

                def turn_hidden(e):
                    u = e % 2
                    b = yield from misc.take()
                    for j in range(4):
                        m = pe.turn(b.ap[:, j * CAP:(j + 1) * CAP], hid[u][:, j * P:(j + 1) * P], ident, t_hid[e],
                                    b.free, signal=(j == 3))
                    free[("hid", u)] = m
                    yield
                    ps = b.ap.rearrange("p (j c) -> p j c", j=4)
                    a = ac.act(hidT[u][0][:, :, :], ps, ACT.Copy, m, free.get(("hidT", u)))
                    a = ve.tt(hidT[u][1][:, :, :], ps, f32(hidT[u][0][:, :, :]), ALU.subtract, a)
                    misc.give(b, a)
                    t_hidT[e] = a

                def down(e, half):
                    u = e % 2
                    m = product([y.ap for y in y_banks], hidT[u], (2 * half, 2 * half + 1), D,
                                e % 4 == 0 and half == 0, e % 4 == 3 and half == 1, t_hidT[e],
                                [y.free for y in y_banks], start)
                    free[("hidT", u)] = m
                    return m

                def scatter(g, m):
                    s = g % 2
                    for j in range(2):
                        cols = slice(j * 512, (j + 1) * 512)
                        a = ac.act(yg[0][:, cols], y_banks[j].ap, ACT.Copy, m, yg_free[0])
                        a = ve.tt(yg[1][:, cols], y_banks[j].ap, f32(yg[0][:, cols]), ALU.subtract, a)
                        y_banks[j].free = [a]
                        yield
                        for i in range(NT):
                            b = yield from misc.take()
                            pe.mm(b.ap, selT[s][:, i, :], yg[1][:, cols], True, False, a, b.free)
                            m_ = pe.mm(b.ap, selT[s][:, i, :], yg[0][:, cols], False, True, signal=True)
                            yield
                            r = resid[:, i, cols]
                            v = ve.tt(r, r, b.ap, ALU.add, m_)
                            misc.give(b, v)
                    yg_free[0] = m_
                    free[("selT", s)] = m_

                ready, t_hid, t_hidT = {}, {}, {}
                first_gather = gather(0)
                next(first_gather)
                for _ in range(NSPLIT - 1):
                    split_next()
                run(first_gather)
                for e in range(17):
                    if e:
                        aside.append(turn_hidden(e - 1))
                    if e < 16:
                        if e % 4 == 0:
                            while e // 4 not in ready:
                                step_aside()
                        t_xg, t_gate = ready[e // 4]
                        ps = gate_up(e, t_xg)
                    if e:
                        while e - 1 not in t_hidT:
                            step_aside()
                        m = down(e - 1, 0)
                    if e < 16:
                        t_hid[e] = hidden(e, ps, t_gate)
                    if e:
                        m = down(e - 1, 1)
                        if e % 4 == 0:
                            aside.append(scatter(e // 4 - 1, m))
                        if e < 16 and e % 4 == 1 and e // 4 < 3:
                            aside.append(gather(e // 4 + 1))
                finish_aside()

            counts_read = {}
            for l in lines + (sp,):
                l.wait(t_top)
                counts_read[l.name] = l.read(top_i[0:1, 0:1])
            experts(0)

            marks = [l.last for l in lines]
            outer_loads = list(loads)
            loads.clear()
            outer_sems = sems_now[0]
            sems_now[0] = [sem(f"more_slot{k}{tag}") for k in range(NSLOT)]
            for l in lines + (sp,):
                l.enter(sem("more_" + l.name + tag))
                l.wait(*marks)
            for first in range(CAP, S, CAP):
                experts(first)
                barrier()
            sp.wait(*[l.last for l in lines])
            for l in lines + (sp,):
                l.leave(counts_read[l.name], MORE_ABOVE)
            loads[:] = outer_loads
            sems_now[0] = outer_sems
            barrier()
            stack.close()
            return t_next

        barrier()
        phase_stack.close()
        t_params2 = moe("_1", PM("ffn_norm"), PM("router"), PM("router_b"), ins["w_gu_1"], ins["w_dn_1"],
                        ins["params2"])
        barrier()
        dump("x_1", resid[:, :, :])

        phase_stack = ExitStack()
        arena = open_arena("mixers_2", 31800)
        tok = {}
        hT = arena.get(KD, S)
        u_a, gate_b, q_c = arena.get(4, S), arena.get(4, S), arena.get(4, S)
        rec = arena.get(4, S + 3)
        v_a = arena.get(NT, 512)
        kv_c = arena.get(4, S)
        vg = arena.get(NT, 280)
        PAD = 16
        xd = arena.get(4, S + PAD)
        y_c = arena.get(4, S)
        y_d = arena.get(4, S)
        merged = arena.get(NT, D)
        hn = merged

        def into_channels(dst, off=0):
            def fin(c, n, ps, m):
                return (ac.act(dst[:, c:c + n, off:off + S], ps, ACT.Copy, m),)
            return fin

        t_pad = [ve.memset(rec[:, :, 0:3], 0.0), ve.memset(xd[:, :, 0:PAD], 0.0)]
        nstat = arena.get(4)

        def project_2():
            t = norm_rows(resid, hn, nstat)
            t_hT = yield from to_channels(hn, hT, KD, PP("norm1"), t, t_params2)
            tok["hT"] = t_hT
            h = load(ins["w_vg_2"])

            def fin_vg(i, ps, m):
                return (ac.act(vg[:, i, :], ps, ACT.Copy, m),)

            yield from project_tokens(hT, h, 280, fin_vg, t_hT, stride=280)
            tok["vg"] = ac.last
            h = load(ins["w_kv_2"])
            yield from project_channels(hT, h, 4, into_channels(kv_c), t_hT)
            tok["kv"] = ac.last
            h = load(ins["w_in_2"][4])
            yield from project_channels(hT, h, 4, into_channels(q_c))
            tok["q"] = ac.last
            cmp_w = [load(ins["w_cmp1"][0])]
            for name, k, dst, off in (("rec", 3, rec, 3), ("xd", 5, xd, PAD), ("gate", 2, gate_b, 0)):
                h = load(ins["w_in_2"][k])
                if name == "rec":
                    cmp_w.append(load(ins["w_cmp1"][1]))
                    tok["cmp_w"] = cmp_w
                yield from project_channels(hT, h, 4, into_channels(dst, off))
                tok[name] = ac.last
            h = load(ins["w_in_2"][1])
            yield from project_tokens(hT, h, 512, into(v_a))
            tok["v"] = ac.last
            h = load(ins["w_in_2"][0])
            yield from project_channels(hT, h, 4, into_channels(u_a))
            tok["u"] = ac.last
            tok["projected"] = pe.last

        def gelu(dst, x, tmp, *after):
            a = ac.act(tmp, x, ACT.Square, *after)
            yield
            a = ve.ts(tmp, tmp, 0.044715, 1.0, ALU.mult, ALU.add, a)
            a = ve.tt(tmp, tmp, x, ALU.mult, a)
            yield
            a = ac.act(tmp, tmp, ACT.Tanh, a, scale=0.7978845608028654)
            yield
            a = ve.stt(tmp, tmp, 1.0, x, ALU.add, ALU.mult, a)
            return ve.ts(dst, tmp, 0.5, None, ALU.mult, None, a)

        blocks = [arena.get(32, 15) for _ in range(2)]
        hidc, gtmp = arena.get(2, 15), arena.get(2, 15)
        kc, vc = arena.get(15), arena.get(P)[0:15, :]
        gates3 = arena.get(NT, 24)
        g3 = gates3.rearrange("p i (h b) -> p i h b", b=3)
        pc, pst, pcT = arena.get(8, 15), arena.get(4, 8), [arena.get(8, P) for _ in range(NT)]
        cmask = arena.get(2, P)
        cm = cmask.rearrange("p a b -> p (a b)")

        def compress():
            t_vg = yield from have("vg")
            a = ac.act(gates3, vg[:, :, 256:280], ACT.Tanh, t_vg, scale=0.5)
            tok["g3"] = ve.ts(gates3, gates3, 0.5, 0.5, ALU.mult, ALU.add, a)
            ve.memset(cmask[:, 0, :], 0.0)
            tok["cmask"] = ve.copy(cmask[:, 1, :], C("causal_add"))
            t_kv = yield from have("kv")
            for c in range(2):
                kvv = kv_c[:, c, :].rearrange("p (n b) -> p b n", b=16)
                for half in range(2):
                    pe_ = PP("cmp_pe", c * 32 + half * 16, c * 32 + half * 16 + 16)
                    t_blk = ve.tt(blocks[c][:, half * 16:half * 16 + 16, :], kvv[:, :, half:half + 15],
                                  pe_.unsqueeze(2).to_broadcast([P, 16, 15]), ALU.add, t_kv)
            hs = yield from have("cmp_w")
            b = yield from pool8.take()
            for c, h in enumerate(hs):
                w = h.slot.rearrange("p (l e) -> p l e", l=32)
                for l in range(32):
                    m = pe.mm(b.ap[:, c * 15:c * 15 + 15], w[:, l, :], blocks[c][:, l, :], l == 0, l == 31, h.ready,
                              t_blk, b.free, signal=(l == 31))
                h.used = [m]
                yield
            a = ve.copy(hidc, b.ap[:, 0:30].rearrange("p (c n) -> p c n", c=2), m)
            pool8.give(b, a)
            a = yield from gelu(hidc, hidc, gtmp, a)
            yield
            b = yield from pool8.take()
            pe.mm(b.ap[:, 0:15], PP("cmp_w2", 0, P), hidc[:, 0, :], True, True, a, b.free)
            m = pe.mm(b.ap[0:15, 128:256], hidc[:, 1, :], PP("cmp_w2", P, 2 * P), True, True, signal=True)
            yield
            ve.copy(kc, b.ap[:, 0:15], m)
            t_cmp = ve.copy(vc, b.ap[0:15, 128:256], m)
            pool8.give(b, t_cmp)
            yield
            for i in range(NT):
                bb = []
                for g in range(2):
                    bb.append((yield from pool8.take()))
                    rr = slice(64 * g, 64 * g + 64)
                    for j in range(4):
                        m = pe.mm(bb[g].ap[:, j * 15:j * 15 + 15], q_c[rr, j, i * P:(i + 1) * P], kc[rr, :], True,
                                  True, tok["q"], t_cmp, bb[g].free, signal=(j == 3))
                yield
                ca = C("cmp_add", 15 * i, 15 * i + 15).unsqueeze(1).to_broadcast([P, 4, 15])
                for g in range(2):
                    a = ve.stt(pc[:, 4 * g:4 * g + 4, :], bb[g].ap[:, 0:60].rearrange("p (j n) -> p j n", j=4), 0.125,
                               ca, ALU.mult, ALU.add, m)
                    pool8.give(bb[g], a)
                a = ve.reduce(pst[:, 0, :], pc, ALU.max, a)
                a = ve.tt(pc, pc, pst[:, 0, :].unsqueeze(2).to_broadcast([P, 8, 15]), ALU.subtract, a)
                yield
                a = ac.act(pc, pc, ACT.Exp, a)
                yield
                a = ve.reduce(pst[:, 1, :], pc, ALU.add, a)
                a = ve.recip(pst[:, 2, :], pst[:, 1, :], a)
                a = ve.stt(pst[:, 3, :], pst[:, 2, :], C("cmp_any", i, i + 1), g3[:, i, :, 0], ALU.mult, ALU.mult, a,
                           tok["g3"])
                a = ve.tt(pc, pc, pst[:, 3, :].unsqueeze(2).to_broadcast([P, 8, 15]), ALU.mult, a)
                yield
                bb = []
                for g in range(2):
                    bb.append((yield from pool8.take()))
                    for j in range(4):
                        m = pe.turn(bb[g].ap[0:15, j * P:(j + 1) * P], pc[:, 4 * g + j, :], ident, a, bb[g].free,
                                    signal=(j == 3))
                yield
                for g in range(2):
                    x = ac.act(pcT[i][0:15, 4 * g:4 * g + 4, :],
                               bb[g].ap[0:15, :].rearrange("p (j q) -> p j q", j=4), ACT.Copy, m)
                    pool8.give(bb[g], x)
            tok["pcT"] = x
            tok["cmp"] = t_cmp

        def sparse_attention(tiles, r, st, turner):
            t_q = yield from have("q")
            t_cmask = yield from have("cmask")
            for j in tiles:
                ob = yield from pool8.take()
                for g in range(2):
                    rr = slice(64 * g, 64 * g + 64)
                    hh = 4 * g + j
                    for i in range(NT):
                        n = (i + 1) * P
                        for br in range(2):
                            b = yield from pool8.take()
                            m = pe.mm(b.ap[:, 0:n], q_c[rr, j, i * P:(i + 1) * P], kv_c[rr, 2 + br, 0:n], True, True,
                                      t_q, tok["kv"], b.free, signal=True)
                            yield
                            a = ve.max_of_sum(r[:, br, 0:n], b.ap[:, 0:n], cm[:, S - n:S], 0.125, st[:, br:br + 1],
                                              m, t_cmask)
                            pool8.give(b, a)
                        a = ve.ts(st[:, 2:4], st[:, 0:2], -1.0, None, ALU.mult, None, a)
                        yield
                        for br in range(2):
                            x = ac.act(r[:, br, 0:n], r[:, br, 0:n], ACT.Exp, a, bias=st[:, 2 + br:3 + br],
                                       accum=st[:, 4 + br:5 + br])
                        yield
                        a = ve.recip(st[:, 4:6], st[:, 4:6], x)
                        a = ve.tt(st[:, 6:8], st[:, 4:6], g3[:, i, hh, 1:3], ALU.mult, a, tok["g3"])
                        for br in range(2):
                            x = ve.ts(r[:, br, 0:n], r[:, br, 0:n], st[:, 6 + br:7 + br], None, ALU.mult, None, a)
                        yield
                        got = []
                        for br in range(2):
                            got.append((yield from turner.turn(r[:, br, :], n, x)))
                        yield
                        t_pcT = yield from have("pcT")
                        pe.mm(ob.ap[rr, i * P:(i + 1) * P], vc[:, 64 * g:64 * g + 64], pcT[i][0:15, hh, :], True,
                              False, t_pcT, tok["cmp"], ob.free)
                        for br in range(2):
                            pT, slot_, t_pT = got[br]
                            for k in range(i + 1):
                                m = pe.mm(ob.ap[rr, i * P:(i + 1) * P],
                                          vg[:, k, br * P + 64 * g:br * P + 64 * g + 64],
                                          pT[:, k, :], False, br == 1 and k == i, t_pT, tok["vg"], signal=(k == i))
                            turner.free[slot_] = m
                tok[f"yc{j}"] = ve.copy(y_c[:, j, :], ob.ap[:, 0:S], m)
                pool8.give(ob, tok[f"yc{j}"])

        cl, cz, cy, cs, cq, cp = (arena.get(4) for _ in range(6))
        half_b = arena.get(8)
        xc, la, ti, tmp4 = (arena.get(4, S) for _ in range(4))
        win = [arena.get(4, S + PAD) for _ in range(2)]
        gms = arena.get(2 * NT)

        def pool_mixer():
            t_xd = yield from have("xd")
            Z = S + PAD
            a = ve.tt(win[0][:, :, 1:Z], xd[:, :, 1:Z], xd[:, :, 0:Z - 1], ALU.add, t_xd, t_pad)
            a = ve.tt(win[1][:, 1:4, 3:Z], win[0][:, 1:4, 3:Z], win[0][:, 1:4, 1:Z - 2], ALU.add, a)
            yield
            a = ve.tt(win[0][:, 2:4, 7:Z], win[1][:, 2:4, 7:Z], win[1][:, 2:4, 3:Z - 4], ALU.add, a)
            a = ve.tt(win[1][:, 3, 15:Z], win[0][:, 3, 15:Z], win[0][:, 3, 7:Z - 8], ALU.add, a)
            yield
            for c, wlen in enumerate((2, 4, 8, 16)):
                src = win[c % 2][:, c, :]
                f1 = ve.tt(src[:, PAD:PAD + 16], src[:, PAD:PAD + 16], C("pool_inv", 16 * c, 16 * c + 16), ALU.mult, a)
                f1 = ve.tt(src[:, PAD:PAD + 16], src[:, PAD:PAD + 16], xd[:, c, PAD:PAD + 16], ALU.subtract, f1)
                f2 = ve.stt(src[:, PAD + 16:Z], src[:, PAD + 16:Z], 1.0 / wlen, xd[:, c, PAD + 16:Z], ALU.mult,
                            ALU.subtract, a)
            yield
            for c2 in range(0, 4, 2):
                b = yield from pool8.take()
                for c in (c2, c2 + 1):
                    m = pe.mm(b.ap[:, (c - c2) * S:(c - c2 + 1) * S], PP("pool_w", c * P, (c + 1) * P),
                              win[c % 2][:, c, PAD:Z], True, True, f1, f2, b.free, signal=True)
                yield
                for c in (c2, c2 + 1):
                    a = ve.ts(y_d[:, c, :], b.ap[:, (c - c2) * S:(c - c2 + 1) * S], PP("pool_scale", c, c + 1), None,
                              ALU.mult, None, m)
                pool8.give(b, a)
            tok["y3"] = a

        def recurrence():
            t_rec = yield from have("rec")
            a = ve.ts(cz, PP("lru_lam"), -1.0, None, ALU.mult, None)
            a = ve.tt(cy, PP("lru_lam"), cz, ALU.max, a)
            a = ac.act(cy, cy, ACT.Exp, a, scale=-1.0)
            yield
            a = ve.ts(cs, cy, 2.0, None, ALU.add, None, a)
            a = ve.recip(cs, cs, a)
            a = ve.tt(cs, cs, cy, ALU.mult, a)
            a = ve.tt(cq, cs, cs, ALU.mult, a)
            a = ve.ts(cp, cq, 1.0 / 17, None, ALU.mult, None, a)
            for k in (15, 13, 11, 9, 7, 5, 3):
                a = ve.stt(cp, cp, 1.0 / k, cq, ALU.add, ALU.mult, a)
            a = ve.stt(cp, cp, 1.0, cs, ALU.add, ALU.mult, a)
            a = ve.ts(cp, cp, 2.0, None, ALU.mult, None, a)
            a = ve.stt(cl, cz, 0.0, cp, ALU.max, ALU.add, a)
            t_cl = ve.ts(cl, cl, -4.0, None, ALU.mult, None, a)
            h1 = ve.ts(half_b[:, 0:4], PP("lru_ba"), 0.5, None, ALU.mult, None)
            h2 = ve.ts(half_b[:, 4:8], PP("lru_bx"), 0.5, None, ALU.mult, None)
            yield
            t_xc = []
            for c in range(4):
                a = ve.ts(xc[:, c, :], rec[:, c, 0:S], PP("conv_w", c, c + 1), PP("conv_b", c, c + 1), ALU.mult,
                          ALU.add, t_rec, t_pad)
                for k in range(1, 4):
                    a = ve.stt(xc[:, c, :], rec[:, c, k:k + S], PP("conv_w", 4 * k + c, 4 * k + c + 1), xc[:, c, :],
                               ALU.mult, ALU.add, a)
                t_xc.append(a)
                yield
            for name, dst, hb in (("lru_wa", la, 0), ("lru_wx", ti, 4)):
                for c2 in range(0, 4, 2):
                    b = yield from pool8.take()
                    for c in (c2, c2 + 1):
                        m = pe.mm(b.ap[:, (c - c2) * S:(c - c2 + 1) * S], PP(name, c * P, (c + 1) * P), xc[:, c, :],
                                  True, True, t_xc[c], b.free, signal=True)
                    yield
                    for c in (c2, c2 + 1):
                        a = ac.act(dst[:, c, :], b.ap[:, (c - c2) * S:(c - c2 + 1) * S], ACT.Tanh, m, h1, h2,
                                   bias=half_b[:, hb + c:hb + c + 1], scale=0.5)
                    pool8.give(b, a)
            for c in range(4):
                a = ve.ts(la[:, c, :], la[:, c, :], 1.0, cl[:, c:c + 1], ALU.add, ALU.mult, a, t_cl)
            t_la = ve.last
            yield
            th_ = rec[:, :, 0:S]
            a = ac.act(th_, la, ACT.Tanh, t_la)
            t_a = ac.act(la, la, ACT.Exp, t_la, a)
            yield
            a = ve.ts(tmp4, th_, -1.0, 1.0, ALU.mult, ALU.add, a)
            a = ve.recip(tmp4, tmp4, a)
            yield
            a = ve.tt(tmp4, tmp4, th_, ALU.mult, a)
            a = ve.ts(tmp4, tmp4, -2.0, 1e-30, ALU.mult, ALU.max, a)
            yield
            t_sq = ac.act(tmp4, tmp4, ACT.Sqrt, a)
            a = ve.stt(ti, ti, 1.0, xc, ALU.add, ALU.mult)
            yield
            a = ve.stt(ti, ti, 0.5, tmp4, ALU.mult, ALU.mult, a, t_sq)
            for c in range(4):
                a = ve.scan(th_[:, c, :], la[:, c, :], ti[:, c, :], a, t_a)
                yield
            t_gb = yield from have("gate")
            a = yield from gelu(gate_b, gate_b, tmp4, t_gb, a)
            tok["y1"] = ve.tt(gate_b, gate_b, th_, ALU.mult, a)

        def spatial_gating():
            wsT = PP("gm_wsT").rearrange("p (g t) -> p g t", g=4)
            t_v = yield from have("v")
            yield from have("y1")
            t_ws = ve.tt(wsT, wsT, C("upto").unsqueeze(1).to_broadcast([P, 4, P]), ALU.mult, t_params2)
            v_flat = v_a.rearrange("p i n -> p (i n)")
            g_flat = tmp4.rearrange("p i n -> p (i n)")
            a = yield from gelu(v_flat, v_flat, g_flat, t_v, ve.last)
            ss, rs = gms[:, 0:NT], gms[:, NT:2 * NT]
            for i in range(NT):
                x = ac.act(g_flat[:, i * 512:(i + 1) * 512], v_a[:, i, :], ACT.Square, a, accum=ss[:, i:i + 1])
            r = rstd(rs, ss, 512, EPS, x)
            yield
            for i in range(NT):
                t_vn = ve.ts(v_a[:, i, :], v_a[:, i, :], rs[:, i:i + 1], None, ALU.mult, None, r)
            t_u = yield from have("u")
            t_ug = yield from gelu(u_a, u_a, tmp4, t_u, t_vn)
            mixed = la
            for i in range(NT):
                b = yield from pool8.take()
                for g in range(4):
                    m = pe.mm(b.ap[:, g * P:(g + 1) * P], v_a[:, i, g * P:(g + 1) * P], wsT[:, g, :], True, True,
                              t_vn, t_ws, b.free, signal=(g == 3))
                yield
                for g in range(4):
                    a = ve.stt(mixed[:, g, i * P:(i + 1) * P], b.ap[:, g * P:(g + 1) * P], PP("gm_norm", g, g + 1),
                               PP("gm_b", g * P, (g + 1) * P), ALU.mult, ALU.add, m)
                pool8.give(b, a)
            tok["y0"] = ve.tt(u_a, u_a, mixed, ALU.mult, a, t_ug)

        tg = [arena.get(512) for _ in range(4)]

        def merge():
            yield from have("projected")
            tg_free = [None] * 4
            n_tg = 0
            for first, (n, yT) in enumerate(((3, y_d), (1, gate_b), (0, u_a), (2, y_c))):
                for half in range(2):
                    hm = load(ins["w_mg"][n, half])
                    hb_ = load(ins["w_branch"][n, half])
                    wb = hb_.slot.rearrange("p (k n) -> p k n", k=4)
                    wm = hm.slot.rearrange("p (k n) -> p k n", k=KD)
                    for i in range(NT):
                        bm = yield from pool8.take()
                        for k in range(KD):
                            m1 = pe.mm(bm.ap, hT[:, k, i * P:(i + 1) * P], wm[:, k, :], k == 0, k == KD - 1,
                                       hm.ready, tok["hT"], bm.free, signal=(k == KD - 1))
                            if k % 2:
                                yield
                        if i == NT - 1:
                            hm.used = [m1]
                        u = n_tg % 4
                        n_tg += 1
                        a = ac.act(tg[u], bm.ap, ACT.Tanh, m1, tg_free[u], scale=0.5)
                        pool8.give(bm, a)
                        if n == 2:
                            t_y = []
                            for j in range(4):
                                t_y.append((yield from have(f"yc{j}")))
                        else:
                            t_y = yield from have(f"y{n}")
                        bb_ = yield from pool8.take()
                        for k in range(4):
                            m2 = pe.mm(bb_.ap, yT[:, k, i * P:(i + 1) * P], wb[:, k, :], k == 0, k == 3,
                                       hb_.ready, bb_.free, t_y, signal=(k == 3))
                        yield
                        mv_ = merged[:, i, half * 512:(half + 1) * 512]
                        if first == 0:
                            a = ve.stt(mv_, tg[u], 1.0, bb_.ap, ALU.add, ALU.mult, a, m2)
                            pool8.give(bb_, a)
                        else:
                            a = ve.stt(tg[u], tg[u], 1.0, bb_.ap, ALU.add, ALU.mult, a, m2)
                            pool8.give(bb_, a)
                            a = ve.tt(mv_, mv_, tg[u], ALU.add, a)
                        tg_free[u] = a
                    hb_.used = [m2]
            tok["merged"] = a

        chains = []
        for c in range(2):
            chains.append(sparse_attention((2 * c, 2 * c + 1), arena.get(2, S), arena.get(8),
                                           Turner([arena.get(2, P) for _ in range(3)])))
        run(weave(project_2(), compress(), *chains, pool_mixer(), recurrence(), spatial_gating(), merge()))
        dump("y_c", y_c)
        dump("y_b", gate_b)
        dump("y_d", y_d)
        dump("y_a", u_a)
        mergedT = hT
        t = run(to_channels(merged, mergedT, KD, None, tok["merged"], ve.last, pe.last, scale=0.5))
        add_product(mergedT, ins["w_out_2"], t)
        dump("x_mid2", resid[:, :, :])
        barrier()
        phase_stack.close()
        t_final = moe("_2", PM("norm2"), PM("router_2"), PM("router_b_2"), ins["w_gu_2"], ins["w_dn_2"],
                      ins["final_gain"])
        barrier()
        dump("x_2", resid[:, :, :])

        fin_ = sb("result", [P, NT, D])
        fstat = sb("result_stat", [P, 4])
        t = norm_rows(resid, fin_, fstat[:, :])
        t_end = ve.tt(fin_[:, :, :], fin_[:, :, :], tail[:, 0:D].unsqueeze(1).to_broadcast([P, NT, D]), ALU.mult, t,
                      t_final)

        s_out = sem("stored")

        block = ctx.enter_context(nc.Block())

        @block.sync
        def _(eng):
            for dst, src, sm, behind in small_loads:
                if not behind:
                    eng.dma_start(dst, src).then_inc(sm, 16)
            for step in sp.steps:
                step(eng)
            eng.wait_ge(*t_end)
            eng.dma_start(out.rearrange("a (t p) d -> p (a t) d", p=P), fin_[:, :, :]).then_inc(s_out, 16)
            eng.wait_ge(s_out, 16)

        @block.gpsimd
        def _(eng):
            for step in gp.steps:
                step(eng)

        @block.scalar
        def _(eng):
            for step in ac.steps:
                step(eng)

        @block.tensor
        def _(eng):
            for step in pe.steps:
                step(eng)

        @block.vector
        def _(eng):
            for step in ve.steps:
                step(eng)




def columns(v):
    return np.asarray(v).reshape(-1, P).T


def rows_(v):
    v = np.asarray(v).reshape(1, -1)
    return np.broadcast_to(v, (P, v.shape[1]))


def chunk(w):
    k = w.shape[0] // P
    return w.reshape(k, P, w.shape[1]).transpose(1, 0, 2).reshape(P, -1)


def lay_constants():
    p = np.arange(P)
    j, t = p[:, None], p[None, :]
    f = {}
    f["ident"] = (j == t)
    f["ones"] = np.ones((P, P))
    f["before"] = (j < t)
    f["upto"] = (j <= t)
    f["iota"] = np.broadcast_to(p[None, :], (P, P))
    f["levels"] = np.concatenate([((t // (2 * s) == j // (2 * s)) & (t // s % 2 == 1) & (j // s % 2 == 0))
                                  for s in (1, 2, 4, 8, 16, 32, 64)], axis=1)
    f["pair"] = (j // 64 == t // 64)
    f["causal01"] = (t <= j)
    f["causal_add"] = np.where(t <= j, 0.0, NEG)
    tok = np.arange(S).reshape(NT, P)
    end = np.arange(15) * 16 + 31
    f["cmp_add"] = np.where(end[None, None, :] <= tok[:, :, None], 0.0, NEG).transpose(1, 0, 2).reshape(P, 30)
    f["cmp_any"] = (tok >= 31).T
    f["group_rank"] = np.broadcast_to(np.array([4.0, 3.0, 2.0, 1.0]), (P, 4))
    f["pool_inv"] = np.broadcast_to(
        np.concatenate([1.0 / np.minimum(np.arange(16) + 1, w) for w in (2, 4, 8, 16)]), (P, 64))
    return np.concatenate([f[n].astype(np.float32).reshape(P, -1) for n, _ in CONSTS], axis=1)


def lay(entries, f):
    for n, w in entries:
        assert f[n].shape == (P, w), (n, f[n].shape, w)
    return np.ascontiguousarray(np.concatenate([f[n] for n, _ in entries], axis=1))


def block_diagonal(w):
    z = np.zeros_like(w[..., 0, :, :])
    return np.concatenate([np.concatenate([w[..., 0, :, :], z], -1), np.concatenate([z, w[..., 1, :, :]], -1)], -2)


def arrange(i):
    f = {k: np.asarray(v) for k, v in i.items()}
    o = {"consts": lay_constants(), "x": f["x"][0], "mem": f["mem"][0]}
    pos = f["positions"][0].astype(np.int32)
    o["pos_cols"] = np.ascontiguousarray(pos.reshape(NT, P).T)
    o["pos_rows"] = np.ascontiguousarray(np.broadcast_to(pos[None, :], (P, S)))
    twice = lambda v: np.concatenate([v, v]).reshape(P, 1)

    def router(g, e, bg, be):
        w = np.concatenate([g[0], e[0]], axis=1)
        return chunk(w), rows_(np.concatenate([bg[0], be[0]]))

    r1, rb1 = router(f["w_group_router"], f["w_expert_router"], f["b_group_router"], f["b_expert_router"])
    r2, rb2 = router(f["router_w_group_2"], f["router_w_expert_2"], f["router_b_group_2"], f["router_b_expert_2"])
    p1 = {
        "attn_norm": columns(f["attn_norm"]), "da_q": columns(f["da_q_norm"]), "da_k": columns(f["da_k_norm"]),
        "lam": rows_(np.concatenate([f["da_lambda_q1"][0], f["da_lambda_q2"][0], f["da_lambda_k1"][0],
                                     f["da_lambda_k2"][0]])),
        "subln": columns(f["da_subln"]), "mu": columns(f["rw_mu"]), "w0": columns(f["rw_w0"]),
        "a0": columns(f["rw_a0"]), "w2a2": np.concatenate([f["rw_w2"][0], f["rw_a2"][0]], axis=0),
        "g2": f["rw_g2"][0], "k_k": columns(f["rw_k_k"]), "k_a": columns(f["rw_k_a"]),
        "r_k": columns(f["rw_r_k"]), "gn_w": columns(f["rw_gn_w"]), "gn_b": columns(f["rw_gn_b"]),
        "mem_norm": columns(f["mem_norm"]), "mem_q": twice(f["mem_q_norm"][0]), "mem_k": twice(f["mem_k_norm"][0]),
        "ffn_norm": columns(f["ffn_norm"]), "router": r1, "router_b": rb1, "norm2": columns(f["norm2_g_2"]),
        "router_2": r2, "router_b_2": rb2,
    }
    o["params1"] = lay(PARAMS1, p1)
    w_in = f["w_in"][0]
    o["w_in_a"] = np.stack([chunk(w_in[:, a:a + 512]) for a in range(0, 2560, 512)])
    o["w_in_q"] = chunk(w_in[:, 2560:2816])
    o["w_mem_kv"] = chunk(f["w_mem_kv"][0])
    o["w_out"] = np.stack([chunk(f["w_out"][0][:, a:a + 512]) for a in (0, 512)])
    w2 = f["w_in_2"][0]
    cuts = {"u": 0, "v": 512, "gate": 1024, "rec": 1536, "q": 2048, "kv": 2560, "g": 3328, "xd": 3352, "mg": 3864}
    kinds = [w2[:, 2560 + 128 * c:2688 + 128 * c] for c in range(6)]
    wq = w2[:, 2048:2560].reshape(D, 2, 4, 64).transpose(0, 2, 1, 3).reshape(D, 512)
    o["w_kv_2"] = chunk(np.concatenate([kinds[0], kinds[1], kinds[2], kinds[4]], axis=1))
    o["w_vg_2"] = chunk(np.concatenate([kinds[3], kinds[5], w2[:, 3328:3352]], axis=1))
    o["w_in_2"] = np.stack([chunk(w) for w in (w2[:, 0:512], w2[:, 512:1024], w2[:, 1024:1536], w2[:, 1536:2048], wq,
                                               w2[:, cuts["xd"]:cuts["mg"]])])
    o["w_mg"] = np.stack([np.stack([chunk(w2[:, a:a + 512]) for a in (cuts["mg"] + n * D, cuts["mg"] + n * D + 512)])
                          for n in range(4)])
    wb = f["w_branch_2"][0]
    wb = np.stack([wb[0], wb[1], wb[2].reshape(2, 4, 64, D).transpose(1, 0, 2, 3).reshape(512, D), wb[3]])
    o["w_branch"] = np.stack([np.stack([chunk(w[:, a:a + 512]) for a in (0, 512)]) for w in wb])
    o["w_out_2"] = np.stack([chunk(f["w_out_2"][0][:, a:a + 512]) for a in (0, 512)])
    w1 = f["cmp_w1_2"][0].reshape(2, 2, 32, 64, 64).transpose(0, 2, 1, 3, 4)
    o["w_cmp1"] = block_diagonal(w1).transpose(0, 2, 1, 3).reshape(2, P, SLOT)

    def tiles(w):
        return w.transpose(1, 0, 2).reshape(P, -1)

    pe_ = f["cmp_pe_2"][0].transpose(2, 0, 1).reshape(64, 64)
    p2 = {
        "norm1": columns(f["norm1_g_2"]), "gm_norm": columns(f["gm_norm_g_2"]),
        "gm_wsT": f["gm_ws_2"][0].transpose(2, 0, 1).reshape(P, 512), "gm_b": rows_(f["gm_b_2"][0]),
        "conv_w": np.concatenate([columns(f["conv_w_2"][0][k]) for k in range(4)], axis=1),
        "conv_b": columns(f["conv_b_2"]),
        "lru_wa": tiles(block_diagonal(f["lru_wa_2"][0].reshape(4, 2, 64, 64))),
        "lru_wx": tiles(block_diagonal(f["lru_wx_2"][0].reshape(4, 2, 64, 64))),
        "lru_ba": columns(f["lru_ba_2"]), "lru_bx": columns(f["lru_bx_2"]), "lru_lam": columns(f["lru_lambda_2"]),
        "cmp_pe": np.concatenate([pe_, pe_], axis=0), "cmp_w2": tiles(block_diagonal(f["cmp_w2_2"][0])),
        "pool_w": tiles(f["pool_w_2"][0]), "pool_scale": columns(f["pool_scale_2"]),
    }
    o["params2"] = lay(PARAMS2, p2)
    o["final_gain"] = rows_(f["final_norm_g_2"])
    for tag, (g, u, d) in {"1": ("w_e_gate", "w_e_up", "w_e_down"),
                           "2": ("moe_w_gate_2", "moe_w_up_2", "moe_w_down_2")}.items():
        gu = np.stack([f[g][0], f[u][0]], axis=1)
        o["w_gu_" + tag] = np.ascontiguousarray(
            gu.reshape(16, 2, KD, P, 512).transpose(0, 1, 3, 2, 4)).reshape(16, 2, P, SLOT)
        o["w_dn_" + tag] = np.ascontiguousarray(
            f[d][0].reshape(16, 4, P, D).transpose(0, 2, 1, 3)).reshape(16, P, SLOT)
    return {k: np.ascontiguousarray(v) for k, v in o.items()}


def program(nc, arrays, debug=None):
    ins = {n: nc.dram_tensor("in_" + n, a.shape, mybir.dt.from_np(a.dtype), kind="ExternalInput").ap()
           for n, a in arrays.items()}
    out = nc.dram_tensor("out_0", (1, S, D), F32, kind="ExternalOutput").ap()
    build(nc, ins, out, debug)


def kernel(**inputs):
    import concourse.bacc as _bacc
    from concourse.bass_utils import run_bass_kernel_spmd as _run

    arrays = arrange(inputs)
    nc = _bacc.Bacc("TRN2", target_bir_lowering=False, num_devices=1)
    program(nc, arrays)
    r = _run(nc, [{"in_" + n: a for n, a in arrays.items()}], core_ids=[0])
    return r.results[0]["out_0"]
```
